# Optimizing a Trainium2 kernel written in Bass

```python
import math
import jax
import jax.numpy as jnp
from jax import lax
import numpy as np

D_MODEL = 1024
BATCH = 1
SEQ = 1024
DEPTH = 1
DEC_BATCH = 8
DEC_SEQ = 4
PAST_LEN = 2048
PAGE_SIZE = 128

HEAD_DIM = 64
N_HEADS = 8
N_KV_HEADS = 2
GROUP = N_HEADS // N_KV_HEADS
ATTN_WIDTH = N_HEADS * HEAD_DIM
KV_WIDTH = N_KV_HEADS * HEAD_DIM
CMP_BLOCK = 64
CMP_HIDDEN = 128
SEL_BLOCK = CMP_BLOCK
N_SEL = 16
WINDOW = 512
WIN_QBLOCK = 128
SEL_QBLOCK = 64
ROT_DIM = HEAD_DIM // 4
ROPE_THETA = 500000.0
RNN_WIDTH = D_MODEL - ATTN_WIDTH
RNN_BLOCKS = 8
RNN_BLOCK_W = RNN_WIDTH // RNN_BLOCKS
CONV_W = 4
LRU_C = 8.0
D_FF = ((8 * D_MODEL + 3 * 256 - 1) // (3 * 256)) * 256
IN_COLS = 2 * RNN_WIDTH + ATTN_WIDTH + 6 * KV_WIDTH + 3 * N_HEADS
ATTN_SCALE = HEAD_DIM ** -0.5
EPS = 1e-6
NEG_INF = -1e30
FORCE_SCORE = 1e4

kernel_name = 'hymba_rglru_nsa_adaln_step'

def rmsnorm(x, g):
    xf = x.astype(jnp.float32)
    y = xf * lax.rsqrt(jnp.mean(xf * xf, axis=-1, keepdims=True) + EPS)
    return (y * g.astype(jnp.float32)).astype(x.dtype)

def rope_partial(x, pos):
    half = ROT_DIM // 2
    inv = jnp.exp(jnp.arange(half, dtype=jnp.float32) * (-math.log(ROPE_THETA) / half))
    ang = pos.astype(jnp.float32)[:, None] * inv[None, :]
    cos = jnp.cos(ang)[:, None, :]
    sin = jnp.sin(ang)[:, None, :]
    xf = x.astype(jnp.float32)
    x1, x2 = xf[..., :half], xf[..., half:ROT_DIM]
    out = jnp.concatenate([x1 * cos - x2 * sin, x1 * sin + x2 * cos, xf[..., ROT_DIM:]], axis=-1)
    return out.astype(x.dtype)

def rope_keys(kv, pos):
    return jnp.stack([rope_partial(kv[:, :, 0], pos), kv[:, :, 1]], axis=2)

def to_blocks(kv, n_blocks):
    S = kv.shape[1]
    kv = jnp.pad(kv, ((0, 0), (0, n_blocks * CMP_BLOCK - S), (0, 0), (0, 0), (0, 0)))
    return kv.reshape((kv.shape[0], n_blocks, CMP_BLOCK) + kv.shape[2:])

def split_proj(z):
    B, S, _ = z.shape
    cuts = np.cumsum([RNN_WIDTH, RNN_WIDTH, ATTN_WIDTH, 2 * KV_WIDTH, 2 * KV_WIDTH, 2 * KV_WIDTH]).tolist()
    xr, yr, q, kvc, kvs, kvw, g = jnp.split(z, cuts, axis=-1)
    kv_shape = (B, S, 2, N_KV_HEADS, HEAD_DIM)
    return (xr, yr, q.reshape(B, S, N_HEADS, HEAD_DIM), kvc.reshape(kv_shape), kvs.reshape(kv_shape),
            kvw.reshape(kv_shape), jax.nn.sigmoid(g.reshape(B, S, 3, N_HEADS)))

def lru_combine(left, right):
    a1, b1 = left
    a2, b2 = right
    return a1 * a2, a2 * b1 + b2

def rglru(xr, yr, conv_prev, h0, lp):
    B, S, _ = xr.shape
    xpad = jnp.concatenate([conv_prev.astype(xr.dtype), xr], axis=1)
    xc = lp['conv_b']
    for k in range(CONV_W):
        xc = xc + xpad[:, k:k + S] * lp['conv_w'][k]
    xb = xc.reshape(B, S, RNN_BLOCKS, RNN_BLOCK_W)
    r = jax.nn.sigmoid(jnp.einsum('bsnd,nde->bsne', xb, lp['lru_wa']).reshape(B, S, RNN_WIDTH) + lp['lru_ba'])
    i = jax.nn.sigmoid(jnp.einsum('bsnd,nde->bsne', xb, lp['lru_wx']).reshape(B, S, RNN_WIDTH) + lp['lru_bx'])
    log_a = -LRU_C * r.astype(jnp.float32) * jax.nn.softplus(-lp['lru_lambda'].astype(jnp.float32))
    a = jnp.exp(log_a)
    b = jnp.sqrt(-jnp.expm1(2.0 * log_a)) * (i * xc).astype(jnp.float32)
    b = b.at[:, 0].add(a[:, 0] * h0.astype(jnp.float32))
    _, h = lax.associative_scan(lru_combine, (a, b), axis=1)
    out = h.astype(xr.dtype) * jax.nn.gelu(yr)
    return out, xpad[:, S:], h[:, -1].astype(h0.dtype)

def compress(kv_blocks, lp):
    z = kv_blocks + jnp.transpose(lp['cmp_pe'], (1, 0, 2))[:, :, None, :]
    hid = jax.nn.gelu(jnp.einsum('bnlckd,cldf->bnckf', z, lp['cmp_w1']))
    return jnp.einsum('bnckf,cfd->bnckd', hid, lp['cmp_w2'])

def cmp_attend(q, ckv, q_pos):
    B, Sq = q.shape[:2]
    nb = ckv.shape[1]
    qg = q.reshape(B, Sq, N_KV_HEADS, GROUP, HEAD_DIM)
    s = jnp.einsum('bqkgd,bnkd->bkgqn', qg, ckv[:, :, 0]).astype(jnp.float32) * ATTN_SCALE
    blk_end = (jnp.arange(nb) + 1) * CMP_BLOCK - 1
    m = blk_end[None, :] <= q_pos[:, None]
    p = jnp.where(m, jax.nn.softmax(jnp.where(m, s, NEG_INF), axis=-1), 0.0)
    o = jnp.einsum('bkgqn,bnkd->bqkgd', p.astype(q.dtype), ckv[:, :, 1])
    imp = jnp.transpose(p.sum(axis=2), (0, 2, 1, 3))
    return o.reshape(B, Sq, N_HEADS, HEAD_DIM), imp

def select_blocks(imp, q_pos):
    nb = imp.shape[-1]
    j = jnp.arange(nb)[None, :]
    cur = (q_pos // SEL_BLOCK)[:, None]
    forced = ((j == 0) | (j == cur) | (j == cur - 1))[None, :, None, :]
    future = (j > cur)[None, :, None, :]
    score = jnp.where(future, -FORCE_SCORE, jnp.where(forced, FORCE_SCORE, imp))
    _, idx = lax.top_k(score, min(N_SEL, nb))
    valid = idx <= (q_pos // SEL_BLOCK)[None, :, None, None]
    return idx, valid

def sel_attend(q, q_pos, idx, valid, kg, vg):
    B, Sq = q.shape[:2]
    n_sel = idx.shape[-1]
    qg = q.reshape(B, Sq, N_KV_HEADS, GROUP, HEAD_DIM)
    s = jnp.einsum('bqkgd,bqknld->bqkgnl', qg, kg).astype(jnp.float32) * ATTN_SCALE
    kpos = idx[..., None] * SEL_BLOCK + jnp.arange(SEL_BLOCK)
    m = (valid[..., None] & (kpos <= q_pos[None, :, None, None, None]))[:, :, :, None]
    s = jnp.where(m, s, NEG_INF).reshape(B, Sq, N_KV_HEADS, GROUP, n_sel * SEL_BLOCK)
    p = jax.nn.softmax(s, axis=-1).astype(q.dtype)
    o = jnp.einsum('bqkgm,bqkmd->bqkgd', p, vg.reshape(B, Sq, N_KV_HEADS, n_sel * SEL_BLOCK, HEAD_DIM))
    return o.reshape(B, Sq, N_HEADS, HEAD_DIM)

def sel_prompt(q_rot, pos, idx, valid, kvs):
    B, S = q_rot.shape[:2]
    nq = S // SEL_QBLOCK
    kvb = kvs.reshape((B, S // SEL_BLOCK, SEL_BLOCK) + kvs.shape[2:])
    bi = jnp.arange(B)[:, None, None, None]
    hi = jnp.arange(N_KV_HEADS)[None, None, :, None]

    def blk(a):
        return jnp.moveaxis(a.reshape((B, nq, SEL_QBLOCK) + a.shape[2:]), 1, 0)

    def step(args):
        qb, pb, ib, vb = args
        g = kvb[bi, ib, :, :, hi, :]
        return sel_attend(qb, pb, ib, vb, g[..., 0, :], g[..., 1, :])

    out = lax.map(step, (blk(q_rot), pos.reshape(nq, SEL_QBLOCK), blk(idx), blk(valid)))
    return jnp.moveaxis(out, 0, 1).reshape(B, S, N_HEADS, HEAD_DIM)

def sel_sample(q_rot, pos, idx, valid, sel_pool, kvs_new, page_table):
    B, S = q_rot.shape[:2]
    bpp = PAGE_SIZE // SEL_BLOCK
    nbp = page_table.shape[1] * bpp
    nbn = -(-S // SEL_BLOCK)
    pool_b = sel_pool.reshape((-1, bpp, SEL_BLOCK) + sel_pool.shape[2:])
    new_b = to_blocks(kvs_new, nbn)
    bi = jnp.arange(B)[:, None, None, None]
    hi = jnp.arange(N_KV_HEADS)[None, None, :, None]
    jp = jnp.minimum(idx, nbp - 1)
    page = page_table[bi, jp // bpp]
    g_past = pool_b[page, jp % bpp, :, :, hi, :]
    g_new = new_b[bi, jnp.clip(idx - nbp, 0, nbn - 1), :, :, hi, :]
    g = jnp.where((idx < nbp)[..., None, None, None], g_past, g_new)
    return sel_attend(q_rot, pos, idx, valid, g[..., 0, :], g[..., 1, :])

def window_prompt(q, kv):
    B, S = q.shape[:2]
    nb, nw = S // WIN_QBLOCK, WINDOW // WIN_QBLOCK
    kvp = jnp.pad(kv, ((0, 0), (WINDOW, 0), (0, 0), (0, 0), (0, 0)))
    kvb = kvp.reshape((B, nb + nw, WIN_QBLOCK) + kv.shape[2:])
    band = jnp.stack([kvb[:, i:i + nb] for i in range(nw + 1)], axis=2)
    band = band.reshape((B, nb, (nw + 1) * WIN_QBLOCK) + kv.shape[2:])
    qb = q.reshape(B, nb, WIN_QBLOCK, N_KV_HEADS, GROUP, HEAD_DIM)
    s = jnp.einsum('bnqkgd,bnskd->bnkgqs', qb, band[:, :, :, 0]).astype(jnp.float32) * ATTN_SCALE
    qpos = jnp.arange(S).reshape(nb, WIN_QBLOCK)
    kpos = (jnp.arange(nb)[:, None] - nw) * WIN_QBLOCK + jnp.arange((nw + 1) * WIN_QBLOCK)[None, :]
    diff = qpos[:, :, None] - kpos[:, None, :]
    m = ((diff >= 0) & (diff < WINDOW) & (kpos[:, None, :] >= 0))[None, :, None, None]
    p = jax.nn.softmax(jnp.where(m, s, NEG_INF), axis=-1).astype(q.dtype)
    o = jnp.einsum('bnkgqs,bnskd->bnqkgd', p, band[:, :, :, 1])
    return o.reshape(B, S, N_HEADS, HEAD_DIM)

def window_sample(q, q_pos, buf, kv_new):
    B, Sq = q.shape[:2]
    wb = buf.shape[1]
    kv = jnp.concatenate([buf.astype(kv_new.dtype), kv_new], axis=1)
    kpos = q_pos[0] - wb + jnp.arange(wb + Sq)
    diff = q_pos[:, None] - kpos[None, :]
    m = (diff >= 0) & (diff < WINDOW)
    qg = q.reshape(B, Sq, N_KV_HEADS, GROUP, HEAD_DIM)
    s = jnp.einsum('bqkgd,bskd->bkgqs', qg, kv[:, :, 0]).astype(jnp.float32) * ATTN_SCALE
    p = jax.nn.softmax(jnp.where(m, s, NEG_INF), axis=-1).astype(q.dtype)
    o = jnp.einsum('bkgqs,bskd->bqkgd', p, kv[:, :, 1])
    return o.reshape(B, Sq, N_HEADS, HEAD_DIM), kv[:, Sq:]

def pre_mixer(x, c, lp):
    mods = jnp.split((jax.nn.silu(c) @ lp['w_ada'] + lp['b_ada'])[:, None, :], 6, axis=-1)
    h = rmsnorm(x, lp['ln1']) * (1.0 + mods[1]) + mods[0]
    return mods, split_proj(h @ lp['w_in'])

def post_mixer(x, mods, o_r, o_c, o_s, o_w, gates, lp):
    B, S = x.shape[:2]
    g = gates[..., None]
    attn = g[:, :, 0] * o_c + g[:, :, 1] * o_s + g[:, :, 2] * o_w
    merged = jnp.concatenate([rmsnorm(o_r, lp['gn_rnn']),
                              rmsnorm(attn.reshape(B, S, ATTN_WIDTH), lp['gn_attn'])], axis=-1)
    x = x + mods[2] * (merged @ lp['w_out'])
    h = rmsnorm(x, lp['ln2']) * (1.0 + mods[4]) + mods[3]
    ff = (jax.nn.silu(h @ lp['w_gate']) * (h @ lp['w_up'])) @ lp['w_down']
    return x + mods[5] * ff

def layer_prompt(x, c, lp):
    B, S, _ = x.shape
    mods, (xr, yr, q, kvc, kvs, kvw, gates) = pre_mixer(x, c, lp)
    pos = jnp.arange(S)
    o_r, conv_new, h_new = rglru(xr, yr, jnp.zeros((B, CONV_W - 1, RNN_WIDTH), x.dtype),
                                 jnp.zeros((B, RNN_WIDTH), x.dtype), lp)
    q_rot = rope_partial(q, pos)
    kvs = rope_keys(kvs, pos)
    kvw = rope_keys(kvw, pos)
    ckv = compress(to_blocks(kvc, S // CMP_BLOCK), lp)
    o_c, imp = cmp_attend(q, ckv, pos)
    idx, valid = select_blocks(imp, pos)
    o_s = sel_prompt(q_rot, pos, idx, valid, kvs)
    o_w = window_prompt(q_rot, kvw)
    y = post_mixer(x, mods, o_r, o_c, o_s, o_w, gates, lp)
    new_win = kvw[:, S - min(WINDOW, S):]
    return y, (kvc, kvs, new_win, conv_new, h_new)

def layer_sample(x, c, cmp_pool, sel_pool, win_buf, conv_buf, h0, page_table, lp):
    B, S, _ = x.shape
    past_len = page_table.shape[1] * PAGE_SIZE
    pos = past_len + jnp.arange(S)
    mods, (xr, yr, q, kvc, kvs, kvw, gates) = pre_mixer(x, c, lp)
    o_r, conv_new, h_new = rglru(xr, yr, conv_buf, h0, lp)
    q_rot = rope_partial(q, pos)
    kvs = rope_keys(kvs, pos)
    kvw = rope_keys(kvw, pos)
    past_c = cmp_pool[page_table].reshape((B, past_len // CMP_BLOCK, CMP_BLOCK) + cmp_pool.shape[2:])
    ckv = jnp.concatenate([compress(past_c, lp), compress(to_blocks(kvc, -(-S // CMP_BLOCK)), lp)], axis=1)
    o_c, imp = cmp_attend(q, ckv, pos)
    idx, valid = select_blocks(imp, pos)
    o_s = sel_sample(q_rot, pos, idx, valid, sel_pool, kvs, page_table)
    o_w, new_win = window_sample(q_rot, pos, win_buf, kvw)
    y = post_mixer(x, mods, o_r, o_c, o_s, o_w, gates, lp)
    return y, (kvc, kvs, new_win, conv_new, h_new)

def setup_inputs(seed: int = 0) -> dict:
    key = jax.random.key(seed)
    keys = list(jax.random.split(key, 40))

    def nrm(shape, scale=1.0):
        return jax.random.normal(keys.pop(), shape, jnp.float32) * scale

    n_pages = PAST_LEN // PAGE_SIZE
    n_used = DEC_BATCH * n_pages
    n_pool = (n_used * 5 + 3) // 4
    win_buf = min(WINDOW, PAST_LEN)
    kv_tail = (2, N_KV_HEADS, HEAD_DIM)
    dsc = D_MODEL ** -0.5
    x_prompt = nrm((BATCH, SEQ, D_MODEL))
    x_sample = nrm((DEC_BATCH, DEC_SEQ, D_MODEL))
    cache_cmp_kv = nrm((DEPTH, n_pool, PAGE_SIZE) + kv_tail)
    cache_sel_kv = nrm((DEPTH, n_pool, PAGE_SIZE) + kv_tail)
    state_win_kv = nrm((DEPTH, DEC_BATCH, win_buf) + kv_tail)
    state_conv = nrm((DEPTH, DEC_BATCH, CONV_W - 1, RNN_WIDTH))
    state_lru_h = nrm((DEPTH, DEC_BATCH, RNN_WIDTH), 0.5)
    page_table = jax.random.permutation(keys.pop(), n_pool)[:n_used].reshape(DEC_BATCH, n_pages).astype(jnp.int32)
    u = jax.random.uniform(keys.pop(), (DEPTH, RNN_WIDTH), jnp.float32, 0.9, 0.999)
    s = u ** (1.0 / LRU_C)
    lru_lambda = jnp.log(s) - jnp.log1p(-s)
    return {
        'x_prompt': x_prompt,
        'x_sample': x_sample,
        'cache_cmp_kv': cache_cmp_kv,
        'cache_sel_kv': cache_sel_kv,
        'state_win_kv': state_win_kv,
        'state_conv': state_conv,
        'state_lru_h': state_lru_h,
        'page_table': page_table,
        'c_prompt': nrm((BATCH, D_MODEL)),
        'c_sample': nrm((DEC_BATCH, D_MODEL)),
        'ln1_g': 1.0 + nrm((DEPTH, D_MODEL), 0.02),
        'ln2_g': 1.0 + nrm((DEPTH, D_MODEL), 0.02),
        'w_ada': nrm((DEPTH, D_MODEL, 6 * D_MODEL), 0.5 * dsc),
        'b_ada': nrm((DEPTH, 6 * D_MODEL), 0.02),
        'w_in': nrm((DEPTH, D_MODEL, IN_COLS), dsc),
        'conv_w': nrm((DEPTH, CONV_W, RNN_WIDTH), CONV_W ** -0.5),
        'conv_b': nrm((DEPTH, RNN_WIDTH), 0.02),
        'lru_wa': nrm((DEPTH, RNN_BLOCKS, RNN_BLOCK_W, RNN_BLOCK_W), RNN_BLOCK_W ** -0.5),
        'lru_ba': nrm((DEPTH, RNN_WIDTH), 0.02),
        'lru_wx': nrm((DEPTH, RNN_BLOCKS, RNN_BLOCK_W, RNN_BLOCK_W), RNN_BLOCK_W ** -0.5),
        'lru_bx': nrm((DEPTH, RNN_WIDTH), 0.02),
        'lru_lambda': lru_lambda,
        'cmp_pe': nrm((DEPTH, 2, CMP_BLOCK, HEAD_DIM), 0.1),
        'cmp_w1': nrm((DEPTH, 2, CMP_BLOCK, HEAD_DIM, CMP_HIDDEN), (CMP_BLOCK * HEAD_DIM) ** -0.5),
        'cmp_w2': nrm((DEPTH, 2, CMP_HIDDEN, HEAD_DIM), CMP_HIDDEN ** -0.5),
        'gn_rnn': 1.0 + nrm((DEPTH, RNN_WIDTH), 0.02),
        'gn_attn': 1.0 + nrm((DEPTH, ATTN_WIDTH), 0.02),
        'w_out': nrm((DEPTH, D_MODEL, D_MODEL), dsc),
        'w_gate': nrm((DEPTH, D_MODEL, D_FF), dsc),
        'w_up': nrm((DEPTH, D_MODEL, D_FF), dsc),
        'w_down': nrm((DEPTH, D_FF, D_MODEL), D_FF ** -0.5),
        'final_g': 1.0 + nrm((D_MODEL,), 0.02),
    }

def reference(x_prompt, x_sample, cache_cmp_kv, cache_sel_kv, state_win_kv, state_conv, state_lru_h,
              page_table, c_prompt, c_sample, ln1_g, ln2_g, w_ada, b_ada, w_in, conv_w, conv_b,
              lru_wa, lru_ba, lru_wx, lru_bx, lru_lambda, cmp_pe, cmp_w1, cmp_w2, gn_rnn, gn_attn,
              w_out, w_gate, w_up, w_down, final_g):
    xp, xs = x_prompt, x_sample
    st_p, st_s = [], []
    for l in range(DEPTH):
        lp = {'ln1': ln1_g[l], 'ln2': ln2_g[l], 'w_ada': w_ada[l], 'b_ada': b_ada[l], 'w_in': w_in[l],
              'conv_w': conv_w[l], 'conv_b': conv_b[l], 'lru_wa': lru_wa[l], 'lru_ba': lru_ba[l],
              'lru_wx': lru_wx[l], 'lru_bx': lru_bx[l], 'lru_lambda': lru_lambda[l],
              'cmp_pe': cmp_pe[l], 'cmp_w1': cmp_w1[l], 'cmp_w2': cmp_w2[l],
              'gn_rnn': gn_rnn[l], 'gn_attn': gn_attn[l], 'w_out': w_out[l],
              'w_gate': w_gate[l], 'w_up': w_up[l], 'w_down': w_down[l]}
        xp, new_p = layer_prompt(xp, c_prompt, lp)
        xs, new_s = layer_sample(xs, c_sample, cache_cmp_kv[l], cache_sel_kv[l], state_win_kv[l],
                                 state_conv[l], state_lru_h[l], page_table, lp)
        st_p.append(new_p)
        st_s.append(new_s)
    y_prompt = rmsnorm(xp, final_g)
    y_sample = rmsnorm(xs, final_g)
    new_cmp_kv_prompt = jnp.stack([s[0] for s in st_p], axis=0)
    new_cmp_kv_sample = jnp.stack([s[0] for s in st_s], axis=0)
    new_sel_kv_prompt = jnp.stack([s[1] for s in st_p], axis=0)
    new_sel_kv_sample = jnp.stack([s[1] for s in st_s], axis=0)
    new_win_kv_prompt = jnp.stack([s[2] for s in st_p], axis=0)
    new_win_kv_sample = jnp.stack([s[2] for s in st_s], axis=0)
    new_conv_prompt = jnp.stack([s[3] for s in st_p], axis=0)
    new_conv_sample = jnp.stack([s[3] for s in st_s], axis=0)
    new_lru_h_prompt = jnp.stack([s[4] for s in st_p], axis=0)
    new_lru_h_sample = jnp.stack([s[4] for s in st_s], axis=0)
    return (y_prompt, y_sample, new_cmp_kv_prompt, new_cmp_kv_sample, new_sel_kv_prompt, new_sel_kv_sample,
            new_win_kv_prompt, new_win_kv_sample, new_conv_prompt, new_conv_sample,
            new_lru_h_prompt, new_lru_h_sample)


_drawn_inputs = setup_inputs


def setup_inputs(seed=0):
    import zlib

    import numpy as np

    out = dict(_drawn_inputs(seed))
    spreads = {}
    factors = {'ln1_g': 2.851,
     'ln2_g': 8.0,
     'lru_ba': 8.0,
     'lru_bx': 7.474,
     'gn_rnn': 8.0,
     'gn_attn': 8.0,
     'final_g': 2.987}
    for name, (base, spread) in spreads.items():
        noise = np.random.default_rng([zlib.crc32(name.encode()), seed]).standard_normal(out[name].shape)
        drawn = base * np.exp(spread * noise) if base else spread * noise
        out[name] = jnp.asarray(drawn.astype(out[name].dtype))
    for name, factor in factors.items():
        out[name] = (out[name] * factor).astype(out[name].dtype)
    return out
```

```python
import math
from contextlib import ExitStack

import numpy as np

import concourse.bass as bass
from concourse import mybir

F32 = mybir.dt.float32
I32 = mybir.dt.int32
ALU = mybir.AluOpType
ACT = mybir.ActivationFunctionType
AX = mybir.AxisListType.X
ds = bass.ds

P = 128
D_MODEL = 1024
SEQ = 1024
DEC_BATCH = 8
DEC_SEQ = 4
PAST_LEN = 2048
PAGE_SIZE = 128
N_PAGES = PAST_LEN // PAGE_SIZE
HEAD_DIM = 64
N_HEADS = 8
N_KV = 2
GROUP = N_HEADS // N_KV
ATTN_WIDTH = N_HEADS * HEAD_DIM
KV_WIDTH = N_KV * HEAD_DIM
BLOCK = 64
CMP_HIDDEN = 128
N_SEL = 16
WINDOW = 512
ROT_DIM = HEAD_DIM // 4
HALF = ROT_DIM // 2
ROPE_THETA = 500000.0
RNN_WIDTH = D_MODEL - ATTN_WIDTH
RNN_BLOCK_W = RNN_WIDTH // 8
CONV_W = 4
LRU_C = 8.0
D_FF = ((8 * D_MODEL + 3 * 256 - 1) // (3 * 256)) * 256
SCALE = HEAD_DIM ** -0.5
EPS = 1e-6
NEG = -1e30

KD = D_MODEL // P
RS = DEC_BATCH * DEC_SEQ
ROWS = SEQ + RS
TILES = SEQ // P
NG = 3
GR = ROWS // NG
KR = RNN_WIDTH // P
KA = ATTN_WIDTH // P
KF = D_FF // P
COND = 1 + DEC_BATCH
KV_COLS = 6 * KV_WIDTH
NAT_COLS = KV_COLS + 3 * N_HEADS
Q_COL = 2 * RNN_WIDTH
NAT_COL = Q_COL + ATTN_WIDTH
NBP = SEQ // BLOCK
NBS = PAST_LEN // BLOCK
SG = DEC_BATCH // 4
BT = DEC_BATCH // SG
QR = N_KV * DEC_SEQ * GROUP
TP = PAST_LEN // P
WP = WINDOW // P
L_CHUNK = 8
N_LCH = BLOCK // L_CHUNK
ROWF = L_CHUNK * 2 * KV_WIDTH
NFREE = N_SEL - 3
NCAND = NBS - 2

VEC = {}
_at = 0
for _name, _n in (("b_ada", 6 * KD), ("ln1_g", KD), ("ln2_g", KD), ("final_g", KD), ("gn_rnn", KR),
                  ("gn_attn", KA), ("conv_w", CONV_W * KR), ("conv_b", KR), ("lru_ba", KR), ("lru_bx", KR),
                  ("lru_lambda", KR)):
    VEC[_name] = (_at, _at + _n)
    _at += _n
N_VEC = _at


class Steps:

    def __init__(self, eng, sem):
        self.eng, self.sem, self.base, self.n = eng, sem, 0, 0

    def done(self, ins):
        ins.then_inc(self.sem, 1)
        self.n += 1

    def fence(self):
        self.eng.wait_ge(self.sem, self.base + self.n)

    def then(self, ins):
        self.done(ins)
        self.fence()

    def enter(self, i, per):
        self.start, self.per = self.base + self.n, per
        self.base, self.n = self.start + i * per, 0

    def leave(self, trips):
        assert self.n == self.per, (self.n, self.per)
        self.base, self.n = self.start + trips * self.per, 0


def bcast(ap, axis, n):
    v = ap.unsqueeze(axis)
    shape = list(v.shape)
    shape[axis] = n
    return v.to_broadcast(shape)


def constants():
    f = np.float32
    c = {}
    c["ident"] = np.eye(P, dtype=f)
    inv = np.exp(np.arange(HALF, dtype=f) * f(-math.log(ROPE_THETA) / HALF)).astype(f)
    pos = np.concatenate([np.arange(SEQ), np.tile(PAST_LEN + np.arange(DEC_SEQ), DEC_BATCH)]).astype(f)
    ang = (pos[:, None] * inv[None, :]).astype(f)
    cos, sin = np.cos(ang.astype(np.float64)).astype(f), np.sin(ang.astype(np.float64)).astype(f)
    ct, st = np.ones((P, ROWS), f), np.zeros((P, ROWS), f)
    rot = np.zeros((P, P), f)
    for h in range(2):
        for d in range(ROT_DIM):
            ct[h * HEAD_DIM + d] = cos[:, d % HALF]
            st[h * HEAD_DIM + d] = sin[:, d % HALF]
        for d in range(HALF):
            rot[h * HEAD_DIM + d + HALF, h * HEAD_DIM + d] = -1
            rot[h * HEAD_DIM + d, h * HEAD_DIM + d + HALF] = 1
    c["cos_t"], c["sin_t"], c["rot"] = ct, st, rot
    nat = np.zeros((P, 2, TILES + 1, HALF), f)
    for t in range(TILES + 1):
        n = min(P, ROWS - t * P)
        nat[:n, 0, t], nat[:n, 1, t] = cos[t * P:t * P + n], sin[t * P:t * P + n]
    c["rope_nat"] = nat.reshape(P, -1)
    q, k = np.arange(P)[:, None], np.arange(P)[None, :]
    c["mask_diag"] = np.where(k > q, f(NEG), f(0))
    c["mask_tail"] = np.where(k <= q, f(NEG), f(0))
    qpos = np.arange(TILES)[None, :, None] * P + np.arange(P)[:, None, None]
    end = (np.arange(NBP)[None, None, :] + 1) * BLOCK - 1
    c["mask_cmp"] = np.where(end <= qpos, f(0), f(NEG)).reshape(P, -1)
    r = np.arange(P)
    rb, rs = r // QR, (r % 16) // GROUP
    col = np.arange(RS)
    m = np.zeros((P, SG, RS), f)
    for g in range(SG):
        own = (col[None, :] // DEC_SEQ == (g * BT + rb)[:, None]) & (col[None, :] % DEC_SEQ <= rs[:, None])
        m[:, g] = np.where(own, f(0), f(NEG))
    c["mask_new"] = m.reshape(P, -1)
    tok = np.arange(P)[None, None, :] * WP + np.arange(WP)[None, :, None]
    c["mask_win"] = np.where(tok > rs[:, None, None], f(0), f(NEG)).reshape(P, -1)
    c["same_query"] = (r[:, None] // GROUP == r[None, :] // GROUP).astype(f)
    j, i = np.arange(NCAND)[:, None], np.arange(NCAND)[None, :]
    c["earlier"] = np.broadcast_to((i < j).astype(f).reshape(1, -1), (P, NCAND * NCAND)).copy()
    c["row_in_block"] = (np.arange(P)[:, None] % 2 * N_LCH + np.arange(N_LCH)[None, :]).astype(np.int32)
    c["part_in_page"] = (np.arange(P)[:, None] % 8 + np.zeros((1, DEC_BATCH), int)).astype(np.int32)
    return c


class Ctx:

    def __init__(self, nc, stack, dram):
        self.nc, self.stack, self.dram, self.made = nc, stack, dram, []
        self.psum = stack.enter_context(nc.psum_tensor("banks", [P, 8 * 512], F32))
        self.ps = [self.psum[:, j * 512:(j + 1) * 512] for j in range(8)]

    def sems(self, names):
        made = [self.nc.alloc_semaphore(name=n) for n in names.split()]
        self.made += made
        return made

    def recycle(self):
        self.nc.clear_and_free_semaphores(self.made)
        self.made = []
        self.nc.all_engine_barrier()


def sb(nc, stack, name, shape, dt=F32):
    return stack.enter_context(nc.sbuf_tensor(name, shape, dt))


def load_and_condition(k, xT, mods, vec, state, ident, ones, eps, page_rows, page_parts, win_copied):
    nc, ps, d = k.nc, k.ps, k.dram
    (ident_loaded, vec_loaded, cond_loaded, state_loaded, x_loaded0, x_loaded1, x_loaded2, w_loaded0, w_loaded1,
     cond_ready, small_turned, small_copied, x_turned, x_copied_v, x_copied_a, mods_summed0, mods_summed1,
     mods_taken0, mods_taken1, consts_set, pages_loaded, pages_ready) = k.sems(
        "s1_ident_loaded s1_vec_loaded s1_cond_loaded s1_state_loaded s1_x_loaded0 s1_x_loaded1 s1_x_loaded2 "
        "s1_w_loaded0 s1_w_loaded1 s1_cond_ready s1_small_turned s1_small_copied s1_x_turned s1_x_copied_v "
        "s1_x_copied_a s1_mods_summed0 s1_mods_summed1 s1_mods_taken0 s1_mods_taken1 s1_consts_set s1_pages_loaded s1_pages_ready")
    x_loaded, w_loaded = [x_loaded0, x_loaded1, x_loaded2], [w_loaded0, w_loaded1]
    mods_summed, mods_taken = [mods_summed0, mods_summed1], [mods_taken0, mods_taken1]
    WC = 4
    w_view = d["w_ada"][0].rearrange("(k p) n -> p k n", p=P)
    with ExitStack() as st:
        x_nat = sb(nc, st, "x_nat", [P, TILES + 1, D_MODEL])
        vec_nat = sb(nc, st, "vec_nat", [P, P])
        c_nat = sb(nc, st, "c_nat", [COND, D_MODEL])
        c_act = sb(nc, st, "c_act", [COND, D_MODEL])
        s_nat = sb(nc, st, "s_nat", [4 * DEC_BATCH, RNN_WIDTH])
        cT = sb(nc, st, "cT", [P, KD, COND])
        w = [sb(nc, st, f"w_ada{p}", [P, KD, WC * P]) for p in range(2)]
        table = sb(nc, st, "page_table", [P, SG + DEC_BATCH], I32)
        iota = sb(nc, st, "page_iota", [P, N_LCH + DEC_BATCH], I32)
        block = st.enter_context(nc.Block())

        @block.sync
        def _(sp):
            sp.dma_start(ident[:, :], d["ident"]).then_inc(ident_loaded, 16)
            sp.dma_start(c_nat[0:1, :], d["c_prompt"]).then_inc(cond_loaded, 16)
            sp.dma_start(c_nat[1:COND, :], d["c_sample"]).then_inc(cond_loaded, 16)
            for j in range(2):
                sp.dma_start(x_nat[:, 4 * j:4 * j + 4, :],
                             d["x_prompt"][0, 4 * j * P:(4 * j + 4) * P, :].rearrange("(t p) n -> p t n", p=P)
                             ).then_inc(x_loaded[j], 16)
            sp.dma_start(x_nat[0:RS, TILES, :], d["x_sample"].rearrange("b s n -> (b s) n")).then_inc(x_loaded[2], 16)
            with sp.Fori(0, 6 * KD // WC // 2) as i:
                for p in range(2):
                    sp.wait_ge(mods_summed[p], i + 1)
                    sp.dma_start(w[p][:, :, :], w_view[:, :, ds(i * (2 * WC * P) + p * WC * P, WC * P)]
                                 ).then_inc(w_loaded[p], 16)

        @block.gpsimd
        def _(pool):
            flat = d["page_table"].rearrange("b j -> (b j)")
            for g in range(SG):
                pool.dma_start(table[:, g:g + 1], bcast(flat[g * P // 2:(g + 1) * P // 2], 1, 2).unsqueeze(2),
                               allow_slow_non_contiguous=True).then_inc(pages_loaded, 16)
            for b in range(DEC_BATCH):
                pool.dma_start(table[:, SG + b:SG + b + 1], bcast(d["page_table"][b], 1, 8).unsqueeze(2),
                               allow_slow_non_contiguous=True).then_inc(pages_loaded, 16)
            pool.dma_start(iota[:, 0:N_LCH], d["row_in_block"]).then_inc(pages_loaded, 16)
            pool.dma_start(iota[:, N_LCH:], d["part_in_page"]).then_inc(pages_loaded, 16)
            pool.dma_start(d["new_win_sample"][0].rearrange("b s c h d -> b s (c h d)")[:, 0:WINDOW - DEC_SEQ, :],
                           d["state_win_kv"][0].rearrange("b s c h d -> b s (c h d)")[:, DEC_SEQ:, :]).then_inc(win_copied, 16)
            pool.memset(ones[:, :], 1.0).then_inc(consts_set, 1)
            pool.memset(eps[:, :], EPS).then_inc(consts_set, 1)
            for name, (a, b) in VEC.items():
                src = d[name]
                while len(src.shape) > 1:
                    src = src.rearrange("a b -> (a b)") if len(src.shape) == 2 else src.rearrange("a b c -> (a b c)")
                pool.dma_start(vec_nat[a:b, :], src.rearrange("(r n) -> r n", n=P)).then_inc(vec_loaded, 16)
            pool.dma_start(s_nat[0:3 * DEC_BATCH, :], d["state_conv"][0].rearrange("b w n -> (b w) n")
                           ).then_inc(state_loaded, 16)
            pool.dma_start(s_nat[3 * DEC_BATCH:4 * DEC_BATCH, :], d["state_lru_h"][0]).then_inc(state_loaded, 16)
            pool.wait_ge(consts_set, 2)

        @block.tensor
        def _(pe):
            pe.wait_ge(ident_loaded, 16)
            pe.wait_ge(vec_loaded, 16 * len(VEC))
            pe.transpose(ps[4][:, 0:N_VEC], vec_nat[0:N_VEC, :], ident[0:N_VEC, 0:N_VEC]).then_inc(small_turned, 1)
            pe.wait_ge(cond_ready, 1)
            for c in range(KD):
                t = pe.transpose(ps[5][:, c * COND:(c + 1) * COND], c_act[:, c * P:(c + 1) * P], ident[0:COND, 0:COND])
            t.then_inc(small_turned, 1)
            pe.wait_ge(state_loaded, 32)
            for c in range(KR):
                t = pe.transpose(ps[6][:, c * 32:(c + 1) * 32], s_nat[:, c * P:(c + 1) * P], ident[0:32, 0:32])
            t.then_inc(small_turned, 1)
            for t in range(TILES + 1):
                n = min(P, ROWS - t * P)
                pe.wait_ge(x_loaded[min(t // 4, 2)], 16)
                for h in range(2):
                    step = 2 * t + h
                    if step >= 4:
                        pe.wait_ge(x_copied_a if h else x_copied_v, (step - 4) // 2 + 1)
                    for c in range(4):
                        m = pe.transpose(ps[step % 4][:, c * P:c * P + n], x_nat[0:n, t, (4 * h + c) * P:(4 * h + c + 1) * P],
                                         ident[0:n, 0:n])
                    m.then_inc(x_turned, 1)
            pe.sem_inc(mods_summed[0], 1)
            pe.sem_inc(mods_summed[1], 1)
            pe.wait_ge(small_copied, 3)
            pe.wait_ge(x_copied_v, TILES + 1)
            pe.wait_ge(x_copied_a, TILES + 1)
            with pe.Fori(0, 6 * KD // WC // 2) as i:
                for p in range(2):
                    pe.wait_ge(w_loaded[p], i * 16 + 16)
                    pe.wait_ge(mods_taken[p], i + 1)
                    for m in range(WC):
                        for c in range(KD):
                            mm = pe.matmul(ps[p][:, m * COND:(m + 1) * COND], lhsT=w[p][:, c, m * P:(m + 1) * P],
                                           rhs=cT[:, c, :], start=(c == 0), stop=(c == KD - 1))
                    mm.then_inc(mods_summed[p], 1)

        @block.scalar
        def _(act):
            act.wait_ge(cond_loaded, 32)
            act.activation(c_act[:, :], c_nat[:, :], ACT.Silu).then_inc(cond_ready, 1)
            for t in range(TILES + 1):
                n = min(P, ROWS - t * P)
                act.wait_ge(x_turned, 2 * t + 2)
                act.activation(xT[:, 4:8, t * P:t * P + n],
                               ps[(2 * t + 1) % 4][:, :].rearrange("p (c n) -> p c n", c=4)[:, :, 0:n],
                               ACT.Copy).then_inc(x_copied_a, 1)

        @block.vector
        def _(dve):
            dve.sem_inc(mods_taken[0], 1)
            dve.sem_inc(mods_taken[1], 1)
            dve.wait_ge(small_turned, 1)
            dve.tensor_copy(vec[:, :], ps[4][:, 0:N_VEC]).then_inc(small_copied, 1)
            dve.wait_ge(small_turned, 2)
            dve.tensor_copy(cT[:, :, :], ps[5][:, 0:KD * COND].rearrange("p (c n) -> p c n", c=KD)).then_inc(small_copied, 1)
            dve.wait_ge(small_turned, 3)
            dve.tensor_copy(state[:, :, :], ps[6][:, 0:KR * 32].rearrange("p (c n) -> p c n", c=KR)).then_inc(small_copied, 1)
            for t in range(TILES + 1):
                n = min(P, ROWS - t * P)
                dve.wait_ge(x_turned, 2 * t + 1)
                dve.tensor_copy(xT[:, 0:4, t * P:t * P + n],
                                ps[(2 * t) % 4][:, :].rearrange("p (c n) -> p c n", c=4)[:, :, 0:n]
                                ).then_inc(x_copied_v, 1)
            dve.wait_ge(small_copied, 1)
            dve.wait_ge(pages_loaded, 16 * (SG + DEC_BATCH + 2))
            for g in range(SG):
                dve.scalar_tensor_tensor(page_rows[:, g, :], table[:, g:g + 1].to_broadcast([P, N_LCH]), 2 * N_LCH,
                                         iota[:, 0:N_LCH], ALU.mult, ALU.add).then_inc(pages_ready, 1)
            dve.scalar_tensor_tensor(page_parts[:, :], table[:, SG:], 8, iota[:, N_LCH:], ALU.mult, ALU.add
                                     ).then_inc(pages_ready, 1)
            dve.wait_ge(pages_ready, SG + 1)
            with dve.Fori(0, 6 * KD // WC // 2) as i:
                for p in range(2):
                    dve.wait_ge(mods_summed[p], i + 2)
                    dve.tensor_tensor(mods[:, ds(i * (2 * WC) + p * WC, WC), :],
                                      ps[p][:, 0:WC * COND].rearrange("p (m c) -> p m c", m=WC),
                                      bcast(vec[:, ds(i * (2 * WC) + p * WC, WC)], 2, COND), ALU.add
                                      ).then_inc(mods_taken[p], 1)


def norm_rows(k, tag, parts, sources, outs, adaln=None):
    nc, ps = k.nc, k.ps
    g_of, factors, shifts, ones, eps = adaln
    sq_ready, sq_used0, sq_used1, summed, root_ready, stepped, scaled, done_a = k.sems(
        " ".join(f"{tag}_{n}" for n in "sq_ready sq_used0 sq_used1 summed root_ready stepped scaled done_a".split()))
    sq_used = [sq_used0, sq_used1]
    NPART = len(parts)
    with ExitStack() as st:
        sq = [sb(nc, st, f"{tag}_sq{p}", [P, ROWS]) for p in range(2)]
        rstd = [sb(nc, st, f"{tag}_rstd{n}", [P, ROWS]) for n in range(NPART)]
        gain = sb(nc, st, f"{tag}_gain", [P, KD, COND])
        block = st.enter_context(nc.Block())

        @block.scalar
        def _(act):
            n = 0
            for chunks in parts:
                for c in chunks:
                    if n >= 2:
                        act.wait_ge(sq_used[n % 2], n // 2)
                    act.activation(sq[n % 2][:, :], sources(c), ACT.Square).then_inc(sq_ready, 1)
                    n += 1
            for j, chunks in enumerate(parts):
                act.wait_ge(summed, j + 1)
                for g in range(NG):
                    r = act.activation(rstd[j][:, g * GR:(g + 1) * GR], ps[NG * j + g][:, 0:GR], ACT.Sqrt,
                                       bias=eps[:, 0:1], scale=1.0 / (P * len(chunks)))
                r.then_inc(root_ready, 1)
            if shifts is not None:
                for n, c in enumerate(c for chunks in parts for c in chunks):
                    act.wait_ge(scaled, n + 1)
                    act.activation(outs(c)[:, 0:SEQ], outs(c)[:, 0:SEQ], ACT.Identity, bias=shifts(c)[:, 0:1],
                                   scale=gain[:, c, 0:1]).then_inc(done_a, 1)
                act.wait_ge(done_a, KD)

        @block.tensor
        def _(pe):
            n = 0
            for j, chunks in enumerate(parts):
                for i, c in enumerate(chunks):
                    pe.wait_ge(sq_ready, n + 1)
                    for g in range(NG):
                        m = pe.matmul(ps[NG * j + g][:, 0:GR], lhsT=ones[:, :], rhs=sq[n % 2][:, g * GR:(g + 1) * GR],
                                      start=(i == 0), stop=(i == len(chunks) - 1))
                    m.then_inc(sq_used[n % 2], 1)
                    n += 1
                pe.wait_ge(sq_used[(n - 1) % 2], (n - 1) // 2 + 1)
                pe.sem_inc(summed, 1)

        @block.vector
        def _(dve):
            s = Steps(dve, stepped)
            if shifts is not None:
                s.done(dve.scalar_tensor_tensor(gain[:, :, :], factors, 1.0, bcast(g_of, 2, COND), ALU.add, ALU.mult))
            n = 0
            for j, chunks in enumerate(parts):
                dve.wait_ge(root_ready, j + 1)
                s.then(dve.reciprocal(rstd[j][:, :], rstd[j][:, :]))
                for c in chunks:
                    if shifts is None:
                        dve.scalar_tensor_tensor(outs(c), sources(c), g_of[:, n:n + 1], rstd[j][:, :], ALU.mult,
                                                 ALU.mult).then_inc(scaled, 1)
                    else:
                        dve.tensor_tensor(outs(c), sources(c), rstd[j][:, :], ALU.mult).then_inc(scaled, 1)
                    n += 1
            if shifts is not None:
                for n, c in enumerate(c for chunks in parts for c in chunks):
                    rows = outs(c)[:, SEQ:ROWS].rearrange("p (b s) -> p b s", b=DEC_BATCH)
                    dve.wait_ge(scaled, n + 1)
                    s.then(dve.tensor_tensor(rows, rows, bcast(gain[:, c, 1:COND], 2, DEC_SEQ), ALU.mult))
                    s.then(dve.tensor_tensor(rows, rows, bcast(shifts(c)[:, 1:COND], 2, DEC_SEQ), ALU.add))
            dve.wait_ge(scaled, sum(map(len, parts)))


def project(k, tag, trips, KC, loads, moving, take, space=None):
    nc, ps = k.nc, k.ps
    names = "loaded0 loaded1 summed0 summed1 taken0 taken1 stepped"
    loaded0, loaded1, summed0, summed1, taken0, taken1, stepped = k.sems(" ".join(f"{tag}_{n}" for n in names.split()))
    loaded, summed, taken = [loaded0, loaded1], [summed0, summed1], [taken0, taken1]
    n_loads, per = take.n_loads, take.per
    with ExitStack() as st:
        if space is None:
            space = sb(nc, st, f"{tag}_w", [P, 2 * KC * P])
        w = [space[:, p * KC * P:(p + 1) * KC * P].rearrange("p (k n) -> p k n", k=KC) for p in range(2)]
        tmp = sb(nc, st, f"{tag}_tmp", [P, 2, RS])
        block = st.enter_context(nc.Block())

        @block.sync
        def _(sp):
            with sp.Fori(0, trips) as i:
                for p in range(2):
                    sp.wait_ge(summed[p], i + 1)
                    for x in loads(sp, i, p, w[p]):
                        x.then_inc(loaded[p], 16)

        @block.tensor
        def _(pe):
            pe.sem_inc(summed[0], 1)
            pe.sem_inc(summed[1], 1)
            with pe.Fori(0, trips) as i:
                for p in range(2):
                    pe.wait_ge(loaded[p], i * (16 * n_loads) + 16 * n_loads)
                    pe.wait_ge(taken[p], i + 1)
                    for g in range(NG):
                        for c in range(KC):
                            m = pe.matmul(ps[NG * p + g][:, 0:GR], lhsT=w[p][:, c, :],
                                          rhs=moving(c)[:, g * GR:(g + 1) * GR], start=(c == 0), stop=(c == KC - 1))
                    m.then_inc(summed[p], 1)

        @block.vector
        def _(dve):
            s = Steps(dve, stepped)
            dve.sem_inc(taken[0], 1)
            dve.sem_inc(taken[1], 1)
            with dve.Fori(0, trips) as i:
                s.enter(i, per)
                for p in range(2):
                    dve.wait_ge(summed[p], i + 2)
                    take(dve, s, i, p, [ps[NG * p + g][:, 0:GR] for g in range(NG)], tmp[:, p, :]).then_inc(taken[p], 1)
                s.leave(trips)
            for p in range(2):
                dve.wait_ge(taken[p], trips + 1)


def prompt_split(g):
    a, b = g * GR, (g + 1) * GR
    return (a, min(b, SEQ)), ((SEQ, b) if b > SEQ else None)


def copy_chunk(dst):
    def take(dve, s, i, p, banks, tmp):
        for g in range(NG):
            r = dve.tensor_copy(dst[:, ds(i * 2 + p, 1), g * GR:(g + 1) * GR], banks[g].unsqueeze(1))
            if g < NG - 1:
                s.done(r)
        return r
    take.n_loads, take.per = 1, 2 * (NG - 1)
    return take


def rg_lru(k, z, oR, vec, state, ident):
    nc, ps, d = k.nc, k.ps, k.dram
    (cleared, loaded, conv_done, stepped, summed, act_done, rates_ready, last_ready, last_turned, last_copied, stored,
     abs_ready, decay_ready) = k.sems(
        "s3_cleared s3_loaded s3_conv_done s3_stepped s3_summed s3_act_done s3_rates_ready s3_last_ready s3_last_turned "
        "s3_last_copied s3_stored s3_abs_ready s3_decay_ready")
    V = {n: vec[:, a:b] for n, (a, b) in VEC.items()}
    LAST = 3 + 3 * DEC_BATCH + 1 + DEC_BATCH
    with ExitStack() as st:
        wa = sb(nc, st, "wa", [P, 2, KR, P])
        r4 = sb(nc, st, "r4", [P, KR, ROWS])
        i4 = sb(nc, st, "i4", [P, KR, ROWS])
        a4 = z[:, 0:KR, :]
        xs = sb(nc, st, "xs", [P, KR, DEC_BATCH, CONV_W - 1 + DEC_SEQ])
        t = sb(nc, st, "lru_small", [P, 8, KR])
        last = sb(nc, st, "last", [P, KR, LAST])
        last_nat = i4[0:LAST, 0, 0:RNN_WIDTH]
        block = st.enter_context(nc.Block())

        @block.sync
        def _(sp):
            sp.wait_ge(cleared, 1)
            for j, w in enumerate(("lru_wa", "lru_wx")):
                for h in range(2):
                    b = h * RNN_BLOCK_W
                    sp.dma_start(wa[b:b + RNN_BLOCK_W, j, :, b:b + RNN_BLOCK_W],
                                 d[w][0].rearrange("(c h) a e -> h a c e", h=2)[h]).then_inc(loaded, 16)
            sp.wait_ge(last_copied, 1)
            n = 3 * DEC_BATCH
            sp.dma_start(d["new_conv_prompt"][0, 0], last_nat[0:3, :]).then_inc(stored, 16)
            sp.dma_start(d["new_conv_sample"][0].rearrange("b w n -> (b w) n"), last_nat[3:3 + n, :]).then_inc(stored, 16)
            sp.dma_start(d["new_lru_h_prompt"][0], last_nat[3 + n:4 + n, :]).then_inc(stored, 16)
            sp.dma_start(d["new_lru_h_sample"][0], last_nat[4 + n:LAST, :]).then_inc(stored, 16)
            sp.wait_ge(stored, 64)

        @block.gpsimd
        def _(pool):
            pool.memset(wa[:, :, :, :], 0.0).then_inc(cleared, 1)

        @block.tensor
        def _(pe):
            pe.wait_ge(loaded, 64)
            for c in range(KR):
                pe.wait_ge(conv_done, c + 1)
                if c:
                    pe.wait_ge(act_done, 2 * c)
                for j in range(2):
                    for g in range(NG):
                        m = pe.matmul(ps[NG * j + g][:, 0:GR], lhsT=wa[:, j, c, :], rhs=oR[:, c, g * GR:(g + 1) * GR],
                                      start=True, stop=True)
                    m.then_inc(summed, 1)
            pe.wait_ge(last_ready, 1)
            for c in range(KR):
                m = pe.transpose(ps[6][0:LAST, c * P:(c + 1) * P], last[:, c, :], ident[:, :])
            m.then_inc(last_turned, 1)

        @block.scalar
        def _(act):
            s = Steps(act, act_done)
            for c in range(KR):
                for j, (dst, b) in enumerate(((r4, "lru_ba"), (i4, "lru_bx"))):
                    act.wait_ge(summed, 2 * c + j + 1)
                    for g in range(NG):
                        r = act.activation(dst[:, c, g * GR:(g + 1) * GR], ps[NG * j + g][:, 0:GR], ACT.Sigmoid,
                                           bias=V[b][:, c:c + 1])
                    s.done(r)
            act.wait_ge(abs_ready, 1)
            act.activation(t[:, 1, :], t[:, 0, :], ACT.Exp).then_inc(rates_ready, 1)
            s.fence()
            act.wait_ge(decay_ready, 1)
            for c in range(KR):
                s.done(act.activation(a4[:, c, :], r4[:, c, :], ACT.Exp, scale=t[:, 6, c:c + 1]))
                s.fence()
                s.done(act.activation(r4[:, c, :], r4[:, c, :], ACT.Tanh, scale=t[:, 7, c:c + 1]))
            for c in range(KR):
                act.wait_ge(rates_ready, 2 + c)
                s.done(act.activation(r4[:, c, :], r4[:, c, :], ACT.Sqrt, scale=2.0))
            for c in range(KR):
                s.done(act.activation(z[:, KR + c, :], z[:, KR + c, :], ACT.Gelu_apprx_tanh))

        @block.vector
        def _(dve):
            s = Steps(dve, stepped)
            lam = V["lru_lambda"]
            s.then(dve.tensor_scalar(t[:, 2, :], lam, -1.0, None, ALU.mult))
            dve.tensor_tensor(t[:, 0, :], lam, t[:, 2, :], ALU.min).then_inc(abs_ready, 1)
            s.done(dve.tensor_copy(xs[:, :, :, 0:3], state[:, :, 0:3 * DEC_BATCH].rearrange("p c (b w) -> p c b w", w=3)))
            s.then(dve.tensor_copy(xs[:, :, :, 3:], z[:, 0:KR, SEQ:ROWS].rearrange("p c (b s) -> p c b s", s=DEC_SEQ)))
            s.done(dve.tensor_copy(last[:, :, 0:3], z[:, 0:KR, SEQ - 3:SEQ]))
            s.done(dve.tensor_copy(last[:, :, 3:3 + 3 * DEC_BATCH].rearrange("p c (b w) -> p c b w", w=3), xs[:, :, :, DEC_SEQ:]))
            for c in range(KR):
                x, o = z[:, c, :], oR[:, c, :]
                so = o[:, SEQ:ROWS].rearrange("p (b s) -> p b s", s=DEC_SEQ)
                w = [V["conv_w"][:, j * KR + c:j * KR + c + 1] for j in range(CONV_W)]
                b = V["conv_b"][:, c:c + 1]
                s.done(dve.tensor_scalar(o[:, 0:SEQ], x[:, 0:SEQ], w[3], b, ALU.mult, ALU.add))
                s.then(dve.tensor_scalar(so, xs[:, c, :, 3:3 + DEC_SEQ], w[3], b, ALU.mult, ALU.add))
                for j in (2, 1, 0):
                    lag = 3 - j
                    s.done(dve.scalar_tensor_tensor(o[:, lag:SEQ], x[:, 0:SEQ - lag], w[j], o[:, lag:SEQ], ALU.mult, ALU.add))
                    r = dve.scalar_tensor_tensor(so, xs[:, c, :, j:j + DEC_SEQ], w[j], so, ALU.mult, ALU.add)
                    if j:
                        s.then(r)
                    else:
                        s.fence()
                        r.then_inc(conv_done, 1)
            dve.wait_ge(rates_ready, 1)
            s.then(dve.tensor_scalar(t[:, 3, :], t[:, 1, :], 2.0, None, ALU.add))
            s.then(dve.reciprocal(t[:, 3, :], t[:, 3, :]))
            s.then(dve.tensor_tensor(t[:, 1, :], t[:, 1, :], t[:, 3, :], ALU.mult))
            s.then(dve.tensor_tensor(t[:, 3, :], t[:, 1, :], t[:, 1, :], ALU.mult))
            s.then(dve.tensor_scalar(t[:, 4, :], t[:, 3, :], 1.0 / 17, 1.0 / 15, ALU.mult, ALU.add))
            for n in (13, 11, 9, 7, 5, 3, 1):
                s.then(dve.tensor_tensor(t[:, 4, :], t[:, 4, :], t[:, 3, :], ALU.mult))
                s.then(dve.tensor_scalar(t[:, 4, :], t[:, 4, :], 1.0 / n, None, ALU.add))
            s.then(dve.scalar_tensor_tensor(t[:, 4, :], t[:, 4, :], 2.0, t[:, 1, :], ALU.mult, ALU.mult))
            s.then(dve.scalar_tensor_tensor(t[:, 5, :], t[:, 2, :], 0.0, t[:, 4, :], ALU.max, ALU.add))
            s.then(dve.tensor_scalar(t[:, 6, :], t[:, 5, :], -LRU_C, None, ALU.mult))
            dve.tensor_scalar(t[:, 7, :], t[:, 5, :], LRU_C, None, ALU.mult).then_inc(decay_ready, 1)
            for c in range(KR):
                dve.wait_ge(act_done, 2 * KR + 2 * c + 2)
                s.then(dve.tensor_tensor(oR[:, c, :], oR[:, c, :], i4[:, c, :], ALU.mult))
                s.then(dve.tensor_scalar(i4[:, c, :], r4[:, c, :], 1.0, None, ALU.add))
                s.then(dve.reciprocal(i4[:, c, :], i4[:, c, :]))
                dve.tensor_tensor(r4[:, c, :], r4[:, c, :], i4[:, c, :], ALU.mult).then_inc(rates_ready, 1)
            for c in range(KR):
                dve.wait_ge(act_done, 4 * KR + c + 1)
                s.then(dve.tensor_tensor(r4[:, c, :], r4[:, c, :], oR[:, c, :], ALU.mult))
                first_b = r4[:, c, SEQ:ROWS:DEC_SEQ]
                first_a = a4[:, c, SEQ:ROWS:DEC_SEQ]
                s.then(dve.tensor_tensor(t[:, 0:2, :].rearrange("p a b -> p (a b)"), first_a, state[:, c, 3 * DEC_BATCH:], ALU.mult))
                s.then(dve.tensor_tensor(first_b, first_b, t[:, 0:2, :].rearrange("p a b -> p (a b)"), ALU.add))
                s.then(dve.memset(first_a, 0.0))
                s.then(dve.tensor_tensor_scan(oR[:, c, :], a4[:, c, :], r4[:, c, :], 0.0, ALU.mult, ALU.add))
                s.done(dve.tensor_copy(last[:, c, 27:28], oR[:, c, SEQ - 1:SEQ]))
                s.done(dve.tensor_copy(last[:, c, 28:36], oR[:, c, SEQ + DEC_SEQ - 1:ROWS:DEC_SEQ]))
            s.fence()
            dve.sem_inc(last_ready, 1)
            for c in range(KR):
                dve.wait_ge(act_done, 5 * KR + c + 1)
                s.done(dve.tensor_tensor(oR[:, c, :], oR[:, c, :], z[:, KR + c, :], ALU.mult))
            dve.wait_ge(last_turned, 1)
            dve.tensor_copy(last_nat, ps[6][0:LAST, :]).then_inc(last_copied, 1)


def keys_and_values(k, hT, qT, qR, kvn, kT, gates, q_plain, q_rot, k_new, v_new, gate_rows, ident, kv_stored):
    nc, ps, d = k.nc, k.ps, k.dram
    (w_loaded, tabs_loaded, rot_summed, turned_taken, nat_summed, nat_v, nat_a, stepped, keys_ready, gates_ready,
     scratch_stored, gates_loaded, staged_clear, queries_rotated) = k.sems(
        "s4_w_loaded s4_tabs_loaded s4_rot_summed s4_turned_taken s4_nat_summed s4_nat_v s4_nat_a s4_stepped "
        "s4_keys_ready s4_gates_ready s4_scratch_stored s4_gates_loaded s4_staged_clear s4_queries_rotated")
    HN = NAT_COLS // 2
    T9 = TILES + 1
    with ExitStack() as st:
        w = sb(nc, st, "w_nat", [P, KD, NAT_COLS])
        tables = kvn[:, 0:3, :].rearrange("p t n -> p (t n)")
        cos_t, sin_t = tables[:, 0:ROWS], tables[:, ROWS:2 * ROWS]
        rot = sb(nc, st, "rot_m", [P, P])
        rope = sb(nc, st, "rope_nat", [P, 2, T9, HALF])
        tmp = sb(nc, st, "rope_tmp", [P, 4, T9 * N_KV * HALF])
        qtmp = sb(nc, st, "q_tmp", [P, 2, GR])
        block = st.enter_context(nc.Block())

        def rows_of(t):
            return min(P, ROWS - t * P)

        @block.sync
        def _(sp):
            sp.dma_start(rot[:, :], d["rot"]).then_inc(tabs_loaded, 16)
            sp.dma_start(cos_t, d["cos_t"]).then_inc(tabs_loaded, 16)
            sp.dma_start(sin_t, d["sin_t"]).then_inc(tabs_loaded, 16)
            sp.dma_start(rope[:, :, :, :].rearrange("p a t n -> p (a t n)"), d["rope_nat"]).then_inc(tabs_loaded, 16)
            sp.dma_start(w[:, :, :], d["w_in"][0, :, NAT_COL:NAT_COL + NAT_COLS].rearrange("(k p) n -> p k n", p=P)
                         ).then_inc(w_loaded, 16)
            sp.wait_ge(nat_v, T9)
            sp.wait_ge(nat_a, T9)
            flat = {n: d[n].rearrange("x b s c h d -> (x b s) (c h d)") for n in
                    ("new_cmp_prompt", "new_cmp_sample", "new_sel_prompt", "new_sel_sample", "new_win_prompt")}
            W2 = 2 * KV_WIDTH
            sp.dma_start(flat["new_cmp_prompt"].rearrange("(t p) n -> p t n", p=P), kvn[:, 0:TILES, 0:W2]).then_inc(kv_stored, 16)
            sp.dma_start(flat["new_cmp_sample"], kvn[0:RS, TILES, 0:W2]).then_inc(kv_stored, 16)
            sp.wait_ge(keys_ready, 1)
            sp.dma_start(flat["new_sel_prompt"].rearrange("(t p) n -> p t n", p=P), kvn[:, 0:TILES, W2:2 * W2]).then_inc(kv_stored, 16)
            sp.dma_start(flat["new_sel_sample"], kvn[0:RS, TILES, W2:2 * W2]).then_inc(kv_stored, 16)
            sp.dma_start(flat["new_win_prompt"].rearrange("(t p) n -> p t n", p=P),
                         kvn[:, TILES - WINDOW // P:TILES, 2 * W2:3 * W2]).then_inc(kv_stored, 16)
            for b in range(DEC_BATCH):
                sp.dma_start(d["new_win_sample"][0, b].rearrange("s c h d -> s (c h d)")[WINDOW - DEC_SEQ:WINDOW, :],
                             kvn[b * DEC_SEQ:(b + 1) * DEC_SEQ, TILES, 2 * W2:3 * W2]).then_inc(kv_stored, 16)
            sp.wait_ge(kv_stored, 16 * (5 + DEC_BATCH))

        @block.gpsimd
        def _(pool):
            pool.wait_ge(gates_ready, T9)
            scratch = d["gate_scratch"]
            pool.dma_start(scratch, gates[0:RS, TILES, :]).then_inc(scratch_stored, 16)
            pool.wait_ge(scratch_stored, 16)
            for g in range(SG):
                for b in range(BT):
                    for h in range(N_KV):
                        r0 = b * QR + h * DEC_SEQ * GROUP
                        row = (g * BT + b) * DEC_SEQ
                        src = scratch[row:row + DEC_SEQ, :].rearrange("s (br k g) -> k s g br", br=3, k=N_KV)[h]
                        for s in range(DEC_SEQ):
                            pool.dma_start(gate_rows[r0 + s * GROUP:r0 + (s + 1) * GROUP, g, :], src[s],
                                           allow_slow_non_contiguous=True).then_inc(gates_loaded, 16)
            pool.wait_ge(gates_loaded, 16 * SG * BT * N_KV * DEC_SEQ)

        @block.tensor
        def _(pe):
            pe.wait_ge(tabs_loaded, 64)
            step = 0
            for c in range(KA):
                for g in range(NG):
                    if step >= 4:
                        pe.wait_ge(turned_taken, step - 3)
                    pe.matmul(ps[4 + step % 4][:, 0:GR], lhsT=rot[:, :], rhs=qT[:, c, g * GR:(g + 1) * GR], start=True,
                              stop=True).then_inc(rot_summed, 1)
                    step += 1
            pe.wait_ge(w_loaded, 16)
            for t in range(T9):
                n = rows_of(t)
                if t >= 2:
                    pe.wait_ge(nat_v, t - 1)
                    pe.wait_ge(nat_a, t - 1)
                for h in range(2):
                    for c in range(KD):
                        m = pe.matmul(ps[2 * (t % 2) + h][0:n, 0:HN], lhsT=hT[:, c, t * P:t * P + n],
                                      rhs=w[:, c, h * HN:(h + 1) * HN], start=(c == 0), stop=(c == KD - 1))
                m.then_inc(nat_summed, 1)
            pe.wait_ge(keys_ready, 1)
            for kind in range(2):
                col = 2 * KV_WIDTH * (1 + kind)
                for half in range(3):
                    pe.wait_ge(turned_taken, step - 3)
                    tiles = range(4 * half, min(4 * half + 4, T9))
                    for j, t in enumerate(tiles):
                        n = rows_of(t)
                        m = pe.transpose(ps[4 + step % 4][:, j * P:j * P + n], kvn[0:n, t, col:col + KV_WIDTH], ident[0:n, 0:n])
                    m.then_inc(rot_summed, 1)
                    step += 1

        @block.scalar
        def _(act):
            for t in range(T9):
                n = rows_of(t)
                act.wait_ge(nat_summed, t + 1)
                bank = ps[2 * (t % 2) + 1]
                if t == 0:
                    act.wait_ge(queries_rotated, 1)
                if t == TILES:
                    act.wait_ge(staged_clear, 2)
                act.activation(gates[0:n, t, :], bank[0:n, KV_COLS - HN:HN], ACT.Sigmoid).then_inc(gates_ready, 1)
                act.activation(kvn[0:n, t, HN:KV_COLS], bank[0:n, 0:KV_COLS - HN], ACT.Copy).then_inc(nat_a, 1)
            act.wait_ge(gates_ready, T9)

        @block.vector
        def _(dve):
            s = Steps(dve, stepped)
            dve.memset(kvn[:, TILES, :], 0.0).then_inc(staged_clear, 1)
            dve.memset(gates[:, TILES, :], 0.0).then_inc(staged_clear, 1)
            s.done(dve.memset(q_plain[:, :, :], 0.0))
            s.done(dve.memset(q_rot[:, :, :], 0.0))
            dve.wait_ge(tabs_loaded, 64)
            step = 0
            for c in range(KA):
                for g in range(NG):
                    cols = slice(g * GR, (g + 1) * GR)
                    s.done(dve.tensor_tensor(qR[:, c, cols], qT[:, c, cols], cos_t[:, cols], ALU.mult))
                    dve.wait_ge(rot_summed, step + 1)
                    dve.tensor_tensor(qtmp[:, step % 2, :], ps[4 + step % 4][:, 0:GR], sin_t[:, cols], ALU.mult
                                      ).then_inc(turned_taken, 1)
                    dve.wait_ge(turned_taken, step + 1)
                    s.fence()
                    s.done(dve.tensor_tensor(qR[:, c, cols], qR[:, c, cols], qtmp[:, step % 2, :], ALU.add))
                    step += 1
            s.fence()
            dve.sem_inc(queries_rotated, 1)
            for b in range(BT):
                for h in range(N_KV):
                    part = slice(h * HEAD_DIM, (h + 1) * HEAD_DIM)
                    c0 = b * QR + h * DEC_SEQ * GROUP
                    for dst, src in ((q_plain, qT), (q_rot, qR)):
                        for g in range(SG):
                            row = SEQ + (g * BT + b) * DEC_SEQ
                            s.done(dve.tensor_copy(
                                dst[part, g * BT + b, c0:c0 + DEC_SEQ * GROUP].rearrange("p (s g) -> p s g", g=GROUP),
                                src[part, :, row:row + DEC_SEQ].rearrange("p g s -> p s g")))
            dve.wait_ge(staged_clear, 2)
            for t in range(T9):
                n = rows_of(t)
                dve.wait_ge(nat_summed, t + 1)
                dve.tensor_copy(kvn[0:n, t, 0:HN], ps[2 * (t % 2)][0:n, 0:HN]).then_inc(nat_v, 1)
            dve.wait_ge(nat_v, T9)
            dve.wait_ge(nat_a, T9)
            cos, sin = bcast(rope[:, 0, :, :], 2, N_KV), bcast(rope[:, 1, :, :], 2, N_KV)
            T = [tmp[:, j, :].rearrange("p (t h n) -> p t h n", h=N_KV, n=HALF) for j in range(4)]
            for kind in range(2):
                col = 2 * KV_WIDTH * (1 + kind)
                heads = kvn[:, :, col:col + KV_WIDTH].rearrange("p t (h n) -> p t h n", h=N_KV)
                x1, x2 = heads[:, :, :, 0:HALF], heads[:, :, :, HALF:ROT_DIM]
                s.done(dve.tensor_tensor(T[0], x1, cos, ALU.mult))
                s.done(dve.tensor_tensor(T[1], x2, sin, ALU.mult))
                s.done(dve.tensor_tensor(T[2], x1, sin, ALU.mult))
                s.then(dve.tensor_tensor(T[3], x2, cos, ALU.mult))
                s.done(dve.tensor_tensor(x1, T[0], T[1], ALU.subtract))
                s.then(dve.tensor_tensor(x2, T[2], T[3], ALU.add))
            dve.sem_inc(keys_ready, 1)
            for kind in range(2):
                for half in range(3):
                    dve.wait_ge(rot_summed, step + 1)
                    n = min(4 * P, ROWS - half * 4 * P)
                    dve.tensor_copy(kT[:, kind, half * 4 * P:half * 4 * P + n], ps[4 + step % 4][:, 0:n]).then_inc(turned_taken, 1)
                    step += 1
                col = 2 * KV_WIDTH * (1 + kind)
                s.done(dve.tensor_copy(v_new[:, kind, :], kvn[0:RS, TILES, col + KV_WIDTH:col + 2 * KV_WIDTH]))
                dve.wait_ge(turned_taken, step)
                s.done(dve.tensor_copy(k_new[:, kind, :], kT[:, kind, SEQ:ROWS]))
            s.fence()


def compress(k, ck_s, cv_s, ck_p, cv_p, ident, page_rows, space):
    nc, ps, d = k.nc, k.ps, k.dram
    (w1_loaded0, w1_loaded1, rows_loaded00, rows_loaded01, rows_loaded10, rows_loaded11, p_loaded0, p_loaded1, multiplied,
     turned, copied_v, copied_a, zero_set, all_summed, bias_ready, hid_ready, w2_loaded, w2_clear, out_summed,
     out_taken) = k.sems(
        " ".join("s5_" + n for n in ("w1_loaded0 w1_loaded1 rows_loaded00 rows_loaded01 rows_loaded10 rows_loaded11 p_loaded0 "
                                     "p_loaded1 multiplied turned copied_v copied_a zero_set all_summed bias_ready hid_ready "
                                     "w2_loaded w2_clear out_summed out_taken").split()))
    w1_loaded, p_loaded = [w1_loaded0, w1_loaded1], [p_loaded0, p_loaded1]
    rows_loaded = [[rows_loaded00, rows_loaded01], [rows_loaded10, rows_loaded11]]
    NPB = NBP + 1
    counts = [P, P, NPB]
    LP = L_CHUNK // 2
    STEPS = (SG + 1) * LP
    TRIPS = N_LCH // 2
    AHEAD = STEPS + 1
    cmp_rows = d["cache_cmp_kv"][0].rearrange("a (r l) c h d -> (a r) (l c h d)", l=L_CHUNK)
    prompt_rows = d["new_cmp_prompt"][0, 0].rearrange("(n l) c h d -> n (l c h d)", l=BLOCK)
    w1_view = d["cmp_w1"][0].rearrange("c (l m) d f -> (m d) c l f", m=2)
    with ExitStack() as st:
        w1 = [sb(nc, st, f"w1_{p}", [P, 2, LP, CMP_HIDDEN]) for p in range(2)]
        rows = [[space[:, (2 * g + p) * ROWF:(2 * g + p + 1) * ROWF] for p in range(2)] for g in range(SG)]
        prows = [sb(nc, st, f"prompt_rows{p}", [NPB, ROWF]) for p in range(2)]
        zt = [sb(nc, st, f"zt{p}", [P, 2, 2 * P]) for p in range(2)]
        zero = sb(nc, st, "zero", [P, 512])
        bias = sb(nc, st, "cmp_bias", [P, 2])
        hid = sb(nc, st, "hid", [P, 2, SG, 2 * P])
        hid_p = sb(nc, st, "hid_p", [P, 2, 2 * NPB])
        w2k = sb(nc, st, "w2k", [P, N_KV, P])
        w2v = sb(nc, st, "w2v", [P, HEAD_DIM])
        block = st.enter_context(nc.Block())

        def turn_of(v):
            return v // LP, v % LP

        def source(v, p):
            g, l = turn_of(v)
            n = counts[g]
            buf = (rows[g][p] if g < SG else prows[p][:, :])[0:n, :].rearrange("p (l c n) -> p l c n", c=2, n=KV_WIDTH)
            return buf[:, 2 * l:2 * l + 2], n

        def sums(g, c):
            n = 2 * counts[g]
            return ps[c][:, g * n:(g + 1) * n] if g < SG else ps[2][:, c * n:(c + 1) * n]

        @block.sync
        def _(sp):
            for j in range(N_KV):
                sp.dma_start(w2v[:, :], d["cmp_w2"][0, 1]).then_inc(w2_loaded, 16) if j == 0 else None
                if j == 0:
                    sp.wait_ge(w2_clear, 1)
                sp.dma_start(w2k[:, j, j * HEAD_DIM:(j + 1) * HEAD_DIM], d["cmp_w2"][0, 0]).then_inc(w2_loaded, 16)
            pe_enc = d["cmp_pe"][0].rearrange("c l d -> l c d")
            with sp.Fori(0, TRIPS) as i:
                for p in range(2):
                    sp.wait_ge(multiplied, i * (2 * STEPS) + (p - 1) * STEPS + AHEAD)
                    for c in range(2):
                        sp.dma_start(w1[p][:, c, :, :], w1_view[:, c, ds(i * (2 * LP) + p * LP, LP), :]).then_inc(w1_loaded[p], 16)
                    sp.dma_start(prows[p][0:NBP, :], prompt_rows[:, ds(i * (2 * ROWF) + p * ROWF, ROWF)]).then_inc(p_loaded[p], 16)
                    for h in range(N_KV):
                        sp.dma_start(prows[p][NBP:NPB, :].rearrange("p (l c h d) -> p l c h d", c=2, h=N_KV, d=HEAD_DIM)[:, :, :, h],
                                     pe_enc[ds(i * (2 * L_CHUNK) + p * L_CHUNK, L_CHUNK)].unsqueeze(0)).then_inc(p_loaded[p], 16)

        @block.gpsimd
        def _(pool):
            pool.memset(zero[:, :], 0.0).then_inc(zero_set, 1)
            pool.memset(w2k[:, :, :], 0.0).then_inc(w2_clear, 1)
            for n in range(N_LCH):
                p = n % 2
                if n >= 2:
                    pool.wait_ge(multiplied, (n - 1) * STEPS + AHEAD)
                for g in range(SG):
                    pool.indirect_dma_start(rows[g][p], None, cmp_rows,
                                            bass.IndirectOffsetOnAxis(ap=page_rows[:, g, n:n + 1], axis=0)
                                            ).then_inc(rows_loaded[g][p], 16)

        @block.tensor
        def _(pe):
            pe.wait_ge(zero_set, 1)
            for b in range(3):
                pe.matmul(ps[b][:, :], lhsT=zero[:, 0:P], rhs=zero[:, :], start=True, stop=False, skip_group_check=True)
            pe.sem_inc(multiplied, AHEAD)
            with pe.Fori(0, TRIPS) as i:
                for p in range(2):
                    def turn(v):
                        at = p * STEPS + v
                        src, n = source(v, p)
                        if v == 0:
                            pe.wait_ge(w1_loaded[p], i * 32 + 32)
                            pe.wait_ge(rows_loaded[0][p], i * 16 + 16)
                        if v == LP:
                            pe.wait_ge(rows_loaded[1][p], i * 16 + 16)
                        for e in range(2):
                            for c in range(2):
                                m = pe.transpose(ps[4 + 2 * (at % 2) + e][:, c * n:(c + 1) * n], src[:, e, c, :], ident[0:n, 0:n])
                        m.then_inc(turned, 1)

                    def multiply(v):
                        at = p * STEPS + v
                        g, l = turn_of(v)
                        n = 2 * counts[g]
                        if v == 2 * LP - 2:
                            pe.wait_ge(p_loaded[p], i * 48 + 48)
                        pe.wait_ge(copied_v, i * (4 * STEPS) + 2 * at + 2)
                        pe.wait_ge(copied_a, i * (4 * STEPS) + 2 * at + 2)
                        for c in range(2):
                            m = pe.matmul(sums(g, c), lhsT=w1[p][:, c, l, :], rhs=zt[at % 2][:, c, 0:n],
                                          start=False, stop=False, skip_group_check=True)
                        return m
                    turn(0)
                    for v in range(STEPS):
                        if v + 1 < STEPS:
                            turn(v + 1)
                        multiply(v).then_inc(multiplied, 1)
            for b in range(3):
                m = pe.matmul(ps[b][:, :], lhsT=zero[:, 0:P], rhs=zero[:, :], start=False, stop=True, skip_group_check=True)
            m.then_inc(all_summed, 1)
            pe.wait_ge(w2_loaded, 48)
            pe.wait_ge(hid_ready, 6)
            for g in range(SG):
                for h in range(N_KV):
                    pe.matmul(ps[6][:, g * P:(g + 1) * P], lhsT=w2k[:, h, :], rhs=hid[:, 0, g, h * P:(h + 1) * P],
                              start=(h == 0), stop=(h == 1))
            for h in range(N_KV):
                pe.matmul(ps[6][:, 2 * P:2 * P + NBP], lhsT=w2k[:, h, :], rhs=hid_p[:, 0, h * NPB:h * NPB + NBP],
                          start=(h == 0), stop=(h == 1))
            for h in range(N_KV):
                m = pe.matmul(ps[7][0:NBP, h * HEAD_DIM:(h + 1) * HEAD_DIM], lhsT=hid_p[:, 1, h * NPB:h * NPB + NBP], rhs=w2v[:, :],
                              start=True, stop=True)
            m.then_inc(out_summed, 1)
            for b in range(DEC_BATCH):
                g, r = b // BT, (b % BT) * NBS
                for h in range(N_KV):
                    m = pe.matmul(ps[g][0:NBS, (b % BT) * KV_WIDTH + h * HEAD_DIM:(b % BT) * KV_WIDTH + (h + 1) * HEAD_DIM],
                                  lhsT=hid[:, 1, g, h * P + r:h * P + r + NBS], rhs=w2v[:, :], start=True, stop=True)
                if b % BT == BT - 1:
                    m.then_inc(out_summed, 1)

        def copy_turn(eng, copy, copied, e, i, p, v):
            at = p * STEPS + v
            n = counts[turn_of(v)[0]]
            eng.wait_ge(turned, i * (2 * STEPS) + at + 1)
            eng.wait_ge(multiplied, i * (2 * STEPS) + at - 1 + AHEAD)
            for h in range(N_KV):
                copy(zt[at % 2][e * HEAD_DIM:(e + 1) * HEAD_DIM, :, h * n:(h + 1) * n],
                     ps[4 + 2 * (at % 2) + e][h * HEAD_DIM:(h + 1) * HEAD_DIM, 0:2 * n].rearrange("p (c n) -> p c n", c=2)
                     ).then_inc(copied, 1)

        @block.scalar
        def _(act):
            with act.Fori(0, TRIPS) as i:
                for p in range(2):
                    for v in range(STEPS):
                        copy_turn(act, lambda o, x: act.activation(o, x, ACT.Copy), copied_a, 1, i, p, v)
            act.wait_ge(bias_ready, 1)
            for c in range(2):
                for g in range(SG + 1):
                    dst = hid[:, c, g, :] if g < SG else hid_p[:, c, :]
                    act.activation(dst, sums(g, c), ACT.Gelu_apprx_tanh, bias=bias[:, c:c + 1]
                                   ).then_inc(hid_ready, 1)

        @block.vector
        def _(dve):
            with dve.Fori(0, TRIPS) as i:
                for p in range(2):
                    for v in range(STEPS):
                        copy_turn(dve, dve.tensor_copy, copied_v, 0, i, p, v)
            dve.wait_ge(all_summed, 1)
            for c in range(2):
                m = dve.tensor_copy(bias[:, c:c + 1], sums(SG, c)[:, NBP:NPB])
            m.then_inc(bias_ready, 1)
            dve.wait_ge(out_summed, 1)
            dve.tensor_copy(ck_s[:, :], ps[6][:, 0:SG * P]).then_inc(out_taken, 1)
            dve.tensor_copy(ck_p[:, :], ps[6][:, SG * P:SG * P + NBP]).then_inc(out_taken, 1)
            dve.tensor_copy(cv_p[:, :], ps[7][0:NBP, 0:KV_WIDTH]).then_inc(out_taken, 1)
            for g in range(SG):
                dve.wait_ge(out_summed, g + 2)
                dve.tensor_copy(cv_s[:, g * BT:(g + 1) * BT, :], ps[g][0:NBS, :].rearrange("p (b n) -> p b n", b=BT)
                                ).then_inc(out_taken, 1)
            dve.wait_ge(out_taken, 5)


def prompt_attention(k, qT, qR, kvn, kT, gates, ck_p, cv_p, attn, ident):
    nc, ps, psum, d = k.nc, k.ps, k.psum, k.dram
    (masks_loaded, v_clear, v_spread, staged, scored, max_ready, probs_ready, turned0, turned1, copied0, copied1,
     out_summed, merged, stepped, cmp_scored, cmp_shifted, cmp_exp, cmp_probs, cmp_turned, cmp_copied, cmp_summed,
     cmp_merged, merged_half) = k.sems(" ".join("s6_" + n for n in (
         "masks_loaded v_clear v_spread staged scored max_ready probs_ready turned0 turned1 copied0 copied1 out_summed "
         "merged stepped cmp_scored cmp_shifted cmp_exp cmp_probs cmp_turned cmp_copied cmp_summed cmp_merged merged_half").split()))
    WT = WINDOW // P
    units = [(t, h, br) for t in range(TILES) for h in range(N_KV) for br in (1, 2)]
    tiles_of = [list(range(t + 1)) if br == 1 else list(range(max(0, t - WT), t + 1)) for t, h, br in units]
    U = len(units)
    second = [len(x) > 4 for x in tiles_of]
    upto = [sum(second[:u + 1]) for u in range(U)]
    C1 = upto[-1]
    HT = TILES // 2
    with ExitStack() as st:
        diag = sb(nc, st, "mask_diag", [P, P])
        tail = sb(nc, st, "mask_tail", [P, P])
        cmask = sb(nc, st, "mask_cmp", [P, TILES, NBP])
        vx = sb(nc, st, "v_spread", [P, HT * N_KV, HEAD_DIM])
        Q = [sb(nc, st, f"q_rot{h}", [P, SEQ]) for h in range(N_KV)]
        QC = [sb(nc, st, f"q_plain{h}", [P, SEQ]) for h in range(N_KV)]
        probs = [sb(nc, st, f"probs{p}", [P, SEQ]) for p in range(2)]
        pT = [sb(nc, st, f"probsT{p}", [P, SEQ]) for p in range(2)]
        nmax = sb(nc, st, "neg_max", [P, 4])
        den = sb(nc, st, "den", [P, 4])
        coef = sb(nc, st, "coef", [P, 4])
        gsel = sb(nc, st, "gate_pair", [P, TILES, 3, N_KV])
        cs = sb(nc, st, "cmp_probs", [P, TILES, N_KV, NBP])
        cst = sb(nc, st, "cmp_stat", [P, 2, TILES, N_KV])
        cT = pT[1][:, SEQ - 2 * P:SEQ].rearrange("p (a n) -> p a n", a=2)
        block = st.enter_context(nc.Block())

        @block.sync
        def _(sp):
            sp.dma_start(diag[:, :], d["mask_diag"]).then_inc(masks_loaded, 16)
            sp.dma_start(tail[:, :], d["mask_tail"]).then_inc(masks_loaded, 16)
            sp.dma_start(cmask[:, :, :].rearrange("p t n -> p (t n)"), d["mask_cmp"]).then_inc(masks_loaded, 16)
            sp.wait_ge(v_clear, 1)
            for j in range(HT * N_KV):
                sp.dma_start(vx[j * NBP:(j + 1) * NBP, j, :], cv_p[:, (j % N_KV) * HEAD_DIM:(j % N_KV + 1) * HEAD_DIM]
                             ).then_inc(v_spread, 16)

        @block.gpsimd
        def _(pool):
            pool.memset(vx[:, :, :], 0.0).then_inc(v_clear, 1)

        @block.tensor
        def _(pe):
            pe.wait_ge(masks_loaded, 48)
            pe.wait_ge(v_spread, 16 * HT * N_KV)
            with pe.Fori(0, KA) as i:
                def qk(u):
                    t, h, br = units[u]
                    if u == 0:
                        pe.wait_ge(staged, i * 4 + 4)
                    if u >= 2:
                        pe.wait_ge(probs_ready, i * U + u - 1)
                    base, k0, n = (u % 2) * 1024, tiles_of[u][0] * P, len(tiles_of[u]) * P
                    q = Q[h][:, t * P:(t + 1) * P]
                    masks = {n - P: diag}
                    if br == 2 and t >= WT:
                        masks[0] = tail
                    for a in range(0, n, 512):
                        b = min(a + 512, n)
                        own = [(x, m) for x, m in masks.items() if a <= x < b]
                        m = pe.matmul(psum[:, base + a:base + b], lhsT=q, rhs=kT[:, br - 1, k0 + a:k0 + b],
                                      start=True, stop=not own, skip_group_check=True)
                        for x, mask in own:
                            m = pe.matmul(psum[:, base + x:base + x + P], lhsT=ident[:, :], rhs=mask[:, :],
                                          start=False, stop=(x, mask) == own[-1], skip_group_check=True)
                    m.then_inc(scored, 1)

                def turn(u):
                    pe.wait_ge(probs_ready, i * U + u + 1)
                    n = len(tiles_of[u])
                    if u >= 1:
                        pe.wait_ge(copied0, i * U + u)
                    for j in range(min(n, 4)):
                        m = pe.transpose(ps[4][:, j * P:(j + 1) * P], probs[u % 2][:, j * P:(j + 1) * P], ident[:, :])
                    m.then_inc(turned0, 1)
                    if second[u]:
                        if upto[u] >= 2:
                            pe.wait_ge(copied1, i * C1 + upto[u] - 1)
                        for j in range(4, n):
                            m = pe.transpose(ps[5][:, (j - 4) * P:(j - 3) * P], probs[u % 2][:, j * P:(j + 1) * P], ident[:, :])
                        m.then_inc(turned1, 1)

                def pv(u):
                    t, h, br = units[u]
                    pe.wait_ge(copied0, i * U + u + 1)
                    if second[u]:
                        pe.wait_ge(copied1, i * C1 + upto[u])
                    if u >= 2:
                        pe.wait_ge(merged, i * U + u - 1)
                    elif u == 0:
                        pe.wait_ge(cmp_merged, i * 2 + 2)
                    col = 2 * KV_WIDTH * br + KV_WIDTH + h * HEAD_DIM
                    for j, kt in enumerate(tiles_of[u]):
                        m = pe.matmul(ps[6 + u % 2][:, 0:HEAD_DIM], lhsT=pT[u % 2][:, j * P:(j + 1) * P],
                                      rhs=kvn[:, kt, col:col + HEAD_DIM], start=(j == 0), stop=(j == len(tiles_of[u]) - 1))
                    m.then_inc(out_summed, 1)

                pe.wait_ge(staged, i * 4 + 4)
                for t in range(TILES):
                    for h in range(N_KV):
                        m = pe.matmul(ps[6][:, (t * N_KV + h) * NBP:(t * N_KV + h + 1) * NBP], lhsT=QC[h][:, t * P:(t + 1) * P],
                                      rhs=ck_p[:, :], start=True, stop=True)
                m.then_inc(cmp_scored, 1)
                qk(0)
                qk(1)
                pe.wait_ge(cmp_probs, i + 1)
                flat = cs[:, :, :, :].rearrange("p t h n -> p (t h n)")
                for j in range(2):
                    m = pe.transpose(ps[7][:, j * P:(j + 1) * P], flat[:, j * P:(j + 1) * P], ident[:, :])
                m.then_inc(cmp_turned, 1)
                pe.wait_ge(cmp_copied, i + 1)
                for j in range(2):
                    pe.matmul(ps[6 + j][:, :], lhsT=cT[:, j, :], rhs=vx[:, :, :].rearrange("p j n -> p (j n)"), start=True,
                              stop=True).then_inc(cmp_summed, 1)
                for u in range(U + 2):
                    if 2 <= u < U:
                        qk(u)
                    if 1 <= u <= U:
                        turn(u - 1)
                    if u >= 2:
                        pv(u - 2)

        @block.scalar
        def _(act):
            with act.Fori(0, KA) as i:
                def exp(u):
                    act.wait_ge(max_ready, i * U + u + 1)
                    if u >= 2:
                        act.wait_ge(turned0, i * U + u - 1)
                        if second[u - 2]:
                            act.wait_ge(turned1, i * C1 + upto[u - 2])
                    n = len(tiles_of[u]) * P
                    if u >= 4:
                        act.wait_ge(merged, i * U + u - 3)
                    act.activation(probs[u % 2][:, 0:n], psum[:, (u % 2) * 1024:(u % 2) * 1024 + n], ACT.Exp,
                                   bias=nmax[:, u % 4:u % 4 + 1], accum_out=den[:, u % 4:u % 4 + 1]).then_inc(probs_ready, 1)

                def copy(u):
                    act.wait_ge(turned0, i * U + u + 1)
                    if u >= 2:
                        act.wait_ge(out_summed, i * U + u - 1)
                    n = min(len(tiles_of[u]), 4) * P
                    act.activation(pT[u % 2][:, 0:n], ps[4][:, 0:n], ACT.Copy).then_inc(copied0, 1)

                act.wait_ge(cmp_shifted, i + 1)
                act.activation(cs[:, :, :, :], cs[:, :, :, :], ACT.Exp).then_inc(cmp_exp, 1)
                for u in range(U + 1):
                    if u < U:
                        exp(u)
                    if u >= 1:
                        copy(u - 1)

        @block.vector
        def _(dve):
            s = Steps(dve, stepped)
            for h in range(N_KV):
                other = slice((1 - h) * HEAD_DIM, (2 - h) * HEAD_DIM)
                s.done(dve.memset(Q[h][other, :], 0.0))
                s.done(dve.memset(QC[h][other, :], 0.0))
            s.fence()
            dve.wait_ge(masks_loaded, 48)
            per = 2 + 7 + 2 * U
            with dve.Fori(0, KA) as i:
                s.enter(i, per)

                def top(u):
                    dve.wait_ge(scored, i * U + u + 1)
                    if u >= 4:
                        dve.wait_ge(probs_ready, i * U + u - 3)
                    n = len(tiles_of[u]) * P
                    dve.tensor_reduce(nmax[:, u % 4:u % 4 + 1], psum[:, (u % 2) * 1024:(u % 2) * 1024 + n], AX, ALU.max,
                                      negate=True).then_inc(max_ready, 1)

                def copy(u):
                    if second[u]:
                        dve.wait_ge(turned1, i * C1 + upto[u])
                        if u >= 2:
                            dve.wait_ge(out_summed, i * U + u - 1)
                        n = len(tiles_of[u]) * P
                        dve.tensor_copy(pT[u % 2][:, 512:n], ps[5][:, 0:n - 512]).then_inc(copied1, 1)

                def merge(u):
                    t, h, br = units[u]
                    j = slice(u % 4, u % 4 + 1)
                    dve.wait_ge(probs_ready, i * U + u + 1)
                    s.then(dve.reciprocal(coef[:, j], den[:, j]))
                    s.then(dve.tensor_tensor(coef[:, j], coef[:, j], gsel[:, t, br, h:h + 1], ALU.mult))
                    dve.wait_ge(out_summed, i * U + u + 1)
                    out = attn[:, t, ds(i * HEAD_DIM + h * GROUP * HEAD_DIM, HEAD_DIM)]
                    if u:
                        dve.wait_ge(merged, i * U + u)
                    dve.scalar_tensor_tensor(out, ps[6 + u % 2][:, 0:HEAD_DIM], coef[:, j], out, ALU.mult, ALU.add
                                             ).then_inc(merged, 1)

                for h in range(N_KV):
                    part = slice(h * HEAD_DIM, (h + 1) * HEAD_DIM)
                    for dst, src in ((Q, qR), (QC, qT)):
                        dve.tensor_scalar(dst[h][part, :], src[part, ds(i, 1), 0:SEQ].rearrange("p a n -> p (a n)"), SCALE,
                                          None, ALU.mult).then_inc(staged, 1)
                for h in range(N_KV):
                    s.done(dve.tensor_copy(gsel[:, :, :, h], gates[:, 0:TILES, :].rearrange("p t (b h) -> p t b h", b=3)[
                        :, :, :, ds(i + h * GROUP, 1)].rearrange("p t b h -> p t (b h)")))
                dve.wait_ge(cmp_scored, i + 1)
                scores = ps[6][:, 0:TILES * N_KV * NBP].rearrange("p (t h n) -> p t h n", h=N_KV, n=NBP)
                s.then(dve.tensor_tensor(cs[:, :, :, :], scores, bcast(cmask[:, :, :], 2, N_KV), ALU.add))
                s.then(dve.tensor_reduce(cst[:, 0, :, :], cs[:, :, :, :], AX, ALU.max))
                s.then(dve.tensor_scalar(cst[:, 0, :, :], cst[:, 0, :, :], -1e29, None, ALU.max))
                dve.tensor_tensor(cs[:, :, :, :], cs[:, :, :, :], bcast(cst[:, 0, :, :], 3, NBP), ALU.subtract
                                  ).then_inc(cmp_shifted, 1)
                dve.wait_ge(cmp_exp, i + 1)
                s.then(dve.tensor_reduce(cst[:, 1, :, :], cs[:, :, :, :], AX, ALU.add))
                s.then(dve.tensor_scalar(cst[:, 1, :, :], cst[:, 1, :, :], 1e-30, None, ALU.max))
                s.then(dve.reciprocal(cst[:, 1, :, :], cst[:, 1, :, :]))
                s.then(dve.tensor_tensor(cst[:, 1, :, :], cst[:, 1, :, :], gsel[:, :, 0, :], ALU.mult))
                dve.tensor_tensor(cs[:, :, :, :], cs[:, :, :, :], bcast(cst[:, 1, :, :], 3, NBP), ALU.mult
                                  ).then_inc(cmp_probs, 1)
                top(0)
                top(1)
                dve.wait_ge(cmp_turned, i + 1)
                dve.tensor_copy(cT[:, :, :], ps[7][:, 0:2 * P].rearrange("p (a n) -> p a n", a=2)).then_inc(cmp_copied, 1)
                for j in range(2):
                    dve.wait_ge(cmp_summed, i * 2 + j + 1)
                    for h in range(N_KV):
                        r = dve.tensor_copy(attn[:, j * HT:(j + 1) * HT, ds(i * HEAD_DIM + h * GROUP * HEAD_DIM, HEAD_DIM)],
                                            ps[6 + j][:, :].rearrange("p (t h n) -> p t h n", h=N_KV, n=HEAD_DIM)[:, :, h, :])
                        r.then_inc(cmp_merged if h else merged_half, 1)
                dve.wait_ge(cmp_merged, i * 2 + 2)
                dve.wait_ge(merged_half, i * 2 + 2)
                for u in range(U + 2):
                    if 2 <= u < U:
                        top(u)
                    if 1 <= u <= U:
                        copy(u - 1)
                    if u >= 2:
                        merge(u - 2)
                s.leave(KA)
            dve.wait_ge(merged, KA * U)


def sample_attention(k, q_plain, q_rot, k_new, v_new, gate_rows, ck_s, cv_s, page_parts, attn, ident, space):
    nc, ps, d = k.nc, k.ps, k.dram
    (masks_loaded, kv_loaded, win_loaded, consts_set, misc_summed, misc_taken, k_turned, k_copied_v, k_copied_a, k_used,
     chunk_taken, exp_ready, exp_done, cmp_norm, probs_scaled, p_turned, p_copied_v, p_copied_a, p_used, opened, out_done,
     out_taken, out_stored, out_back, stepped) = k.sems(" ".join("s7_" + n for n in (
         "masks_loaded kv_loaded win_loaded consts_set misc_summed misc_taken k_turned k_copied_v k_copied_a k_used "
         "chunk_taken exp_ready exp_done cmp_norm probs_scaled p_turned p_copied_v p_copied_a p_used opened out_done "
         "out_taken out_stored out_back stepped").split()))
    NS, NW = PAST_LEN + RS, WINDOW + RS
    CH = 5
    UN = CH * BT
    TURNS = [("cmp", 0, 0, False), ("win", 0, 4, False), ("win", 4, 1, True)] + [
        ("sel", 4 * j, 4, False) for j in range(4)] + [("sel", 16, 1, True)]
    NT = len(TURNS)
    MISC = 4
    runs = d["cache_sel_kv"][0].rearrange("a (r t) c h d -> (a r) (t c h d)", t=TP)
    with ExitStack() as st:
        kv = sb(nc, st, "past_kv", [P, BT, TP, 2 * KV_WIDTH])
        wkv = sb(nc, st, "win_kv", [P, BT, WP, 2 * KV_WIDTH])
        kTs = [sb(nc, st, f"kTs{j}", [P, 512]) for j in range(4)]
        sel = sb(nc, st, "sel_scores", [P, NS])
        win = sb(nc, st, "win_scores", [P, NW])
        cmp_ = sb(nc, st, "cmp_scores", [P, NBS])
        cmp_g = sb(nc, st, "cmp_gated", [P, NBS])
        pT = [sb(nc, st, f"s_probsT{j}", [P, 4, P]) for j in range(2)]
        zero = sb(nc, st, "s_zero", [P, QR])
        mask_new = sb(nc, st, "mask_new", [P, SG, RS])
        mask_win = sb(nc, st, "mask_win", [P, WP * P])
        square = NCAND * NCAND
        earlier = space[:, 0:square].rearrange("p (a b) -> p a b", a=NCAND)
        ranks = space[:, square:3 * square].rearrange("p (x a b) -> p x a b", x=2, a=NCAND)
        same = space[:, 3 * square:3 * square + P]
        out = space[0:QR, 3 * square + P:3 * square + P + 512]
        imp = sb(nc, st, "importance", [P, NBS])
        rank = sb(nc, st, "rank", [P, NCAND])
        unselected = sb(nc, st, "unselected", [P, NBS])
        stat = sb(nc, st, "s_stat", [P, 3, 3])
        block = st.enter_context(nc.Block())
        rows_of = {"cmp": cmp_g, "win": win, "sel": sel}

        def unit(w):
            return w // BT, w % BT

        def copied(eng, count_v, count_a, n, base):
            eng.wait_ge(count_a if n % 2 else count_v, base + n // 2 + 1)

        @block.sync
        def _(sp):
            for dst, name in ((mask_new[:, :, :].rearrange("p g n -> p (g n)"), "mask_new"), (mask_win[:, :], "mask_win"),
                              (same, "same_query"), (space[:, 0:square], "earlier")):
                sp.dma_start(dst, d[name]).then_inc(masks_loaded, 16)
            for g in range(SG):
                if g:
                    sp.wait_ge(p_used, NT * g)
                for b in range(BT):
                    sp.dma_start(wkv[:, b, :, :], d["state_win_kv"][0, g * BT + b].rearrange("(p t) c h d -> p t (c h d)", p=P)
                                 ).then_inc(win_loaded, 16)
                sp.wait_ge(out_taken, g + 1)
                sp.dma_start(d["attn_scratch"][g].rearrange("r b n -> r (b n)"), out).then_inc(out_stored, 16)
                sp.wait_ge(out_stored, 16 * (g + 1))
                for b in range(BT):
                    for h in range(N_KV):
                        src = d["attn_scratch"][g, h * DEC_SEQ * GROUP:(h + 1) * DEC_SEQ * GROUP, b,
                                                h * HEAD_DIM:(h + 1) * HEAD_DIM].rearrange("(s q) n -> s q n", q=GROUP)
                        row = (g * BT + b) * DEC_SEQ
                        sp.dma_start(attn[row:row + DEC_SEQ, TILES, h * GROUP * HEAD_DIM:(h + 1) * GROUP * HEAD_DIM].rearrange(
                            "s (q n) -> s q n", q=GROUP), src).then_inc(out_back, 16)
            sp.wait_ge(out_back, 16 * SG * BT * N_KV)

        @block.gpsimd
        def _(pool):
            pool.memset(zero[:, :], 0.0).then_inc(consts_set, 1)
            for g in range(SG):
                if g:
                    pool.wait_ge(p_used, NT * g)
                for b in range(BT):
                    n = g * BT + b
                    pool.indirect_dma_start(kv[:, b, :, :].rearrange("p t n -> p (t n)"), None, runs,
                                            bass.IndirectOffsetOnAxis(ap=page_parts[:, n:n + 1], axis=0)).then_inc(kv_loaded, 16)
            pool.wait_ge(kv_loaded, 16 * DEC_BATCH)

        @block.tensor
        def _(pe):
            pe.wait_ge(consts_set, 1)
            pe.wait_ge(masks_loaded, 64)
            for g in range(SG):
                def misc(m, product):
                    if g * MISC + m:
                        pe.wait_ge(misc_taken, g * MISC + m)
                    product().then_inc(misc_summed, 1)

                def over_samples(rhs_of, lhs, cols):
                    def product():
                        for b in range(BT):
                            r = pe.matmul(ps[7][:, 0:cols], lhsT=lhs[:, g * BT + b, :], rhs=rhs_of(b), start=(b == 0),
                                          stop=(b == BT - 1))
                        return r
                    return product

                def turn_k(w):
                    c, b = unit(w)
                    n = g * UN + w
                    if n >= 2:
                        copied(pe, k_copied_v, k_copied_a, n - 2, 0)
                    if w == 0:
                        pe.wait_ge(win_loaded, 16 * BT * (g + 1))
                    if w == BT:
                        pe.wait_ge(kv_loaded, 16 * BT * (g + 1))
                    src = wkv if c == 0 else kv
                    for j in range(4):
                        m = pe.transpose(ps[2 + n % 2][:, j * P:(j + 1) * P], src[:, b, (max(c - 1, 0) * 4 + j), 0:KV_WIDTH],
                                         ident[:, :])
                    m.then_inc(k_turned, 1)

                def score(w):
                    c, b = unit(w)
                    n = g * UN + w
                    at = g * CH + c
                    copied(pe, k_copied_v, k_copied_a, n, 0)
                    if b == 0 and at >= 2:
                        pe.wait_ge(chunk_taken, at - 1)
                    pe.matmul(ps[at % 2][:, :], lhsT=q_rot[:, g * BT + b, :], rhs=kTs[n % 4][:, :], start=(b == 0),
                              stop=(b == BT - 1)).then_inc(k_used, 1)

                def turn_p(j):
                    br, tile, count, new = TURNS[j]
                    n = g * NT + j
                    if n >= 2:
                        copied(pe, p_copied_v, p_copied_a, n - 2, 0)
                    if br == "cmp":
                        m = pe.transpose(ps[4 + n % 2][0:NBS, 0:P], cmp_g[:, :], ident[:, :])
                    elif new:
                        m = pe.transpose(ps[4 + n % 2][0:RS, 0:P], rows_of[br][:, tile * P:tile * P + RS], ident[:, :])
                    else:
                        for i in range(count):
                            m = pe.transpose(ps[4 + n % 2][:, i * P:(i + 1) * P], rows_of[br][:, (tile + i) * P:(tile + i + 1) * P],
                                             ident[:, :])
                    m.then_inc(p_turned, 1)

                def pv(j):
                    br, tile, count, new = TURNS[j]
                    n = g * NT + j
                    copied(pe, p_copied_v, p_copied_a, n, 0)
                    for i in range(max(count, 1)):
                        for b in range(BT):
                            col = slice(b * QR, (b + 1) * QR)
                            if br == "cmp":
                                lhs, rhs = pT[n % 2][0:NBS, 0, col], cv_s[:, g * BT + b, :]
                            elif new:
                                lhs, rhs = pT[n % 2][0:RS, 0, col], v_new[:, 0 if br == "sel" else 1, :]
                            else:
                                lhs = pT[n % 2][:, i, col]
                                rhs = (wkv if br == "win" else kv)[:, b, tile + i, KV_WIDTH:2 * KV_WIDTH]
                            m = pe.matmul(ps[6][0:QR, b * P:(b + 1) * P], lhsT=lhs, rhs=rhs, start=False, stop=False,
                                          skip_group_check=True)
                    m.then_inc(p_used, 1)

                def units(a, b):
                    turn_k(a)
                    for w in range(a, b):
                        if w + 1 < b:
                            turn_k(w + 1)
                        score(w)

                if g:
                    pe.wait_ge(out_taken, g)
                pe.matmul(ps[6][0:QR, :], lhsT=zero[:, :], rhs=mask_win[:, :], start=True, stop=False, skip_group_check=True
                          ).then_inc(opened, 1)
                misc(0, over_samples(lambda b: ck_s[:, (g * BT + b) * NBS:(g * BT + b + 1) * NBS], q_plain, NBS))
                units(0, BT)
                misc(1, over_samples(lambda b: k_new[:, 1, :], q_rot, RS))
                pe.wait_ge(cmp_norm, g + 1)
                misc(2, lambda: pe.matmul(ps[7][:, 0:NBS], lhsT=same, rhs=cmp_[:, :], start=True, stop=True))
                pe.wait_ge(probs_scaled, 3 * g + 1)
                turn_p(0)
                units(BT, UN)
                misc(3, over_samples(lambda b: k_new[:, 0, :], q_rot, RS))
                pv(0)
                pe.wait_ge(probs_scaled, 3 * g + 2)
                turn_p(1)
                turn_p(2)
                pv(1)
                pv(2)
                pe.wait_ge(probs_scaled, 3 * g + 3)
                turn_p(3)
                for j in range(3, NT):
                    if j + 1 < NT:
                        turn_p(j + 1)
                    pv(j)
                pe.matmul(ps[6][0:QR, :], lhsT=zero[:, :], rhs=mask_win[:, :], start=False, stop=True, skip_group_check=True
                          ).then_inc(out_done, 1)

        def copy_k(eng, copy, count, g, w):
            n = g * UN + w
            eng.wait_ge(k_turned, n + 1)
            if n >= 4:
                eng.wait_ge(k_used, n - 3)
            copy(kTs[n % 4][:, :], ps[2 + n % 2]).then_inc(count, 1)

        def copy_p(eng, copy, count, g, j):
            n = g * NT + j
            br, tile, c, new = TURNS[j]
            eng.wait_ge(p_turned, n + 1)
            if n >= 2:
                eng.wait_ge(p_used, n - 1)
            if br == "cmp" or new:
                copy(pT[n % 2][0:RS, 0, :], ps[4 + n % 2][0:RS, 0:P]).then_inc(count, 1)
            else:
                copy(pT[n % 2][:, :, :], ps[4 + n % 2].rearrange("p (a n) -> p a n", a=4)).then_inc(count, 1)

        @block.scalar
        def _(act):
            def copy(o, x):
                return act.activation(o, x, ACT.Copy)

            for g in range(SG):
                def exp(j, rows):
                    act.wait_ge(exp_ready, 3 * g + j + 1)
                    act.activation(rows, rows, ACT.Exp, bias=stat[:, j, 0:1], scale=SCALE, accum_out=stat[:, j, 1:2]
                                   ).then_inc(exp_done, 1)
                exp(0, cmp_[:, :])
                for w in (1, 3):
                    copy_k(act, copy, k_copied_a, g, w)
                exp(1, win[:, :])
                for w in range(BT + 1, UN, 2):
                    copy_k(act, copy, k_copied_a, g, w)
                exp(2, sel[:, :])
                for j in range(NT):
                    if j % 2:
                        copy_p(act, copy, p_copied_a, g, j)

        @block.vector
        def _(dve):
            s = Steps(dve, stepped)
            dve.wait_ge(masks_loaded, 64)
            for g in range(SG):
                def take_misc(m, op):
                    dve.wait_ge(misc_summed, g * MISC + m + 1)
                    op().then_inc(misc_taken, 1)
                    dve.wait_ge(misc_taken, g * MISC + m + 1)

                def top(j, rows):
                    s.then(dve.tensor_reduce(stat[:, j, 0:1], rows, AX, ALU.max))
                    dve.tensor_scalar(stat[:, j, 0:1], stat[:, j, 0:1], -SCALE, None, ALU.mult).then_inc(exp_ready, 1)

                def weight(j, gate, rows, dst):
                    s.then(dve.reciprocal(stat[:, j, 2:3], stat[:, j, 1:2]))
                    if j == 0:
                        dve.tensor_scalar(cmp_[:, :], cmp_[:, :], stat[:, j, 2:3], None, ALU.mult).then_inc(cmp_norm, 1)
                        dve.wait_ge(cmp_norm, g + 1)
                        dve.tensor_scalar(dst, rows, gate_rows[:, g, gate:gate + 1], None, ALU.mult).then_inc(probs_scaled, 1)
                    else:
                        s.then(dve.tensor_tensor(stat[:, j, 2:3], stat[:, j, 2:3], gate_rows[:, g, gate:gate + 1], ALU.mult))
                        dve.tensor_scalar(dst, rows, stat[:, j, 2:3], None, ALU.mult).then_inc(probs_scaled, 1)

                def take_chunk(c):
                    at = g * CH + c
                    dve.wait_ge(k_used, g * UN + BT * (c + 1))
                    bank = ps[at % 2]
                    if c == 0:
                        dve.tensor_tensor(win[:, 0:WINDOW], bank, mask_win[:, :], ALU.add).then_inc(chunk_taken, 1)
                    else:
                        lay = "p (t k r) -> p t k r"
                        dve.tensor_tensor(sel[:, (c - 1) * 512:c * 512].rearrange(lay, t=4, r=4), bank.rearrange(lay, t=4, r=4),
                                          bcast(bcast(unselected[:, :], 1, 4), 3, 4), ALU.add).then_inc(chunk_taken, 1)

                if g:
                    dve.wait_ge(p_turned, NT * g)
                take_misc(0, lambda: dve.tensor_copy(cmp_[:, :], ps[7][:, 0:NBS]))
                top(0, cmp_[:, :])
                dve.wait_ge(exp_done, 3 * g + 1)
                weight(0, 0, cmp_[:, :], cmp_g[:, :])
                for w in (0, 2):
                    copy_k(dve, dve.tensor_copy, k_copied_v, g, w)
                take_chunk(0)
                take_misc(1, lambda: dve.tensor_tensor(win[:, WINDOW:NW], ps[7][:, 0:RS], mask_new[:, g, :], ALU.add))
                dve.wait_ge(chunk_taken, g * CH + 1)
                top(1, win[:, :])
                take_misc(2, lambda: dve.tensor_copy(imp[:, :], ps[7][:, 0:NBS]))
                cand = imp[:, 1:1 + NCAND]
                a, b = bcast(cand, 1, NCAND), bcast(cand, 2, NCAND)
                s.done(dve.tensor_tensor(ranks[:, 0, :, :], a, b, ALU.is_gt))
                s.then(dve.tensor_tensor(ranks[:, 1, :, :], a, b, ALU.is_equal))
                s.then(dve.tensor_tensor(ranks[:, 1, :, :], ranks[:, 1, :, :], earlier[:, :, :], ALU.mult))
                s.then(dve.tensor_tensor(ranks[:, 0, :, :], ranks[:, 0, :, :], ranks[:, 1, :, :], ALU.add))
                s.done(dve.memset(unselected[:, :], 0.0))
                s.then(dve.tensor_reduce(rank[:, :], ranks[:, 0, :, :], AX, ALU.add))
                s.then(dve.tensor_scalar(unselected[:, 1:1 + NCAND], rank[:, :], float(NFREE), NEG, ALU.is_ge, ALU.mult))
                for w in range(BT, UN):
                    if w % 2 == 0:
                        copy_k(dve, dve.tensor_copy, k_copied_v, g, w)
                    if w % BT == BT - 1:
                        take_chunk(w // BT)
                take_misc(3, lambda: dve.tensor_tensor(sel[:, PAST_LEN:NS], ps[7][:, 0:RS], mask_new[:, g, :], ALU.add))
                dve.wait_ge(exp_done, 3 * g + 2)
                weight(1, 2, win[:, :], win[:, :])
                dve.wait_ge(chunk_taken, (g + 1) * CH)
                top(2, sel[:, :])
                dve.wait_ge(exp_done, 3 * g + 3)
                weight(2, 1, sel[:, :], sel[:, :])
                for j in range(0, NT, 2):
                    copy_p(dve, dve.tensor_copy, p_copied_v, g, j)
                dve.wait_ge(out_done, g + 1)
                dve.tensor_copy(out, ps[6][0:QR, :]).then_inc(out_taken, 1)


def turn_attention(k, attn, merged, ident):
    nc, ps = k.nc, k.ps
    turned, copied_v, copied_a = k.sems("s8_turned s8_copied_v s8_copied_a")
    with nc.Block() as block:
        @block.tensor
        def _(pe):
            for t in range(TILES + 1):
                n = min(P, ROWS - t * P)
                if t >= 4:
                    pe.wait_ge(copied_a if t % 2 else copied_v, (t - 4) // 2 + 1)
                for c in range(KA):
                    m = pe.transpose(ps[t % 4][:, c * P:c * P + n], attn[0:n, t, c * P:(c + 1) * P], ident[0:n, 0:n])
                m.then_inc(turned, 1)

        def copy(eng, op, count, odd):
            for t in range(odd, TILES + 1, 2):
                n = min(P, ROWS - t * P)
                eng.wait_ge(turned, t + 1)
                op(merged[:, KR:KR + KA, t * P:t * P + n], ps[t % 4].rearrange("p (c n) -> p c n", c=KA)[:, :, 0:n]
                   ).then_inc(count, 1)

        @block.vector
        def _(dve):
            copy(dve, dve.tensor_copy, copied_v, 0)

        @block.scalar
        def _(act):
            copy(act, lambda o, x: act.activation(o, x, ACT.Copy), copied_a, 1)


def add_gated(xT, gate):
    def take(dve, s, i, p, banks, tmp):
        for g in range(NG):
            (a, b), rest = prompt_split(g)
            o = xT[:, ds(i * 2 + p, 1), a:b].rearrange("p a n -> p (a n)")
            s.done(dve.scalar_tensor_tensor(o, banks[g][:, 0:b - a], gate[:, ds(i * 2 + p, 1), 0:1].rearrange("p a n -> p (a n)"),
                                            o, ALU.mult, ALU.add))
            if rest:
                r0 = rest[0] - g * GR
                s.then(dve.tensor_tensor(tmp.rearrange("p (b s) -> p b s", s=DEC_SEQ),
                                         banks[g][:, r0:GR].rearrange("p (b s) -> p b s", s=DEC_SEQ),
                                         bcast(gate[:, ds(i * 2 + p, 1), 1:COND].rearrange("p a n -> p (a n)"), 2, DEC_SEQ),
                                         ALU.mult))
                o = xT[:, ds(i * 2 + p, 1), rest[0]:rest[1]].rearrange("p a n -> p (a n)")
                r = dve.tensor_tensor(o, o, tmp, ALU.add)
        return r
    take.n_loads, take.per = 1, 2 * (NG + 1)
    return take


def ffn_up(k, hT, hidden, space):
    nc, ps, d = k.nc, k.ps, k.dram
    loaded0, loaded1, used0, used1, gate_summed, summed, silu_done, taken = k.sems(
        "s11_loaded0 s11_loaded1 s11_used0 s11_used1 s11_gate_summed s11_summed s11_silu_done s11_taken")
    loaded, used = [loaded0, loaded1], [used0, used1]
    TRIPS = KF // 2
    BODY = 2 * NG
    views = [d[n][0].rearrange("(k p) n -> p k n", p=P) for n in ("w_gate", "w_up")]
    with ExitStack() as st:
        w = [[sb(nc, st, f"w_ff{j}_{p}", [P, KD, P]) for j in range(2)] for p in range(2)]
        act_g = [space[:, g, 0:GR] for g in range(NG)]
        block = st.enter_context(nc.Block())

        @block.sync
        def _(sp):
            with sp.Fori(0, TRIPS) as i:
                for p in range(2):
                    sp.wait_ge(used[p], i + 1)
                    for j in range(2):
                        sp.dma_start(w[p][j][:, :, :], views[j][:, :, ds(i * (2 * P) + p * P, P)]).then_inc(loaded[p], 16)

        @block.tensor
        def _(pe):
            pe.sem_inc(used[0], 1)
            pe.sem_inc(used[1], 1)
            with pe.Fori(0, TRIPS) as i:
                for p in range(2):
                    pe.wait_ge(loaded[p], i * 32 + 32)
                    for g in range(NG):
                        pe.wait_ge(taken, i * BODY + p * NG + g + 1)
                        for j in range(2):
                            for c in range(KD):
                                m = pe.matmul(ps[2 * g + j][:, 0:GR], lhsT=w[p][j][:, c, :], rhs=hT[:, c, g * GR:(g + 1) * GR],
                                              start=(c == 0), stop=(c == KD - 1))
                            if not j:
                                m.then_inc(gate_summed, 1)
                            elif g < NG - 1:
                                m.then_inc(summed, 1)
                    m.then_inc(used[p], 1)

        @block.scalar
        def _(act):
            with act.Fori(0, TRIPS) as i:
                for p in range(2):
                    for g in range(NG):
                        n = p * NG + g
                        act.wait_ge(gate_summed, i * BODY + n + 1)
                        act.wait_ge(taken, i * BODY + n + 1)
                        act.activation(act_g[g], ps[2 * g][:, 0:GR], ACT.Silu).then_inc(silu_done, 1)

        @block.vector
        def _(dve):
            dve.sem_inc(taken, NG)
            with dve.Fori(0, TRIPS) as i:
                for p in range(2):
                    for g in range(NG):
                        n = p * NG + g
                        dve.wait_ge(silu_done, i * BODY + n + 1)
                        if g < NG - 1:
                            dve.wait_ge(summed, i * (2 * (NG - 1)) + p * (NG - 1) + g + 1)
                        else:
                            dve.wait_ge(used[p], i + 2)
                        dve.tensor_tensor(hidden[:, ds(i * 2 + p, 1), g * GR:(g + 1) * GR], act_g[g].unsqueeze(1),
                                          ps[2 * g + 1][:, 0:GR].unsqueeze(1), ALU.mult).then_inc(taken, 1)
            dve.wait_ge(taken, NG + TRIPS * BODY)


def store_rows(k, yT, ident, win_copied):
    nc, ps, d = k.nc, k.ps, k.dram
    turned, copied_v, copied_a, *rows_stored = k.sems("s14_turned s14_copied_v s14_copied_a s14_stored0 s14_stored1 s14_stored2 s14_stored3")
    with ExitStack() as st:
        y = [sb(nc, st, f"y{j}", [P, D_MODEL]) for j in range(4)]
        block = st.enter_context(nc.Block())

        @block.tensor
        def _(pe):
            for t in range(TILES + 1):
                n = min(P, ROWS - t * P)
                for h in range(2):
                    step = 2 * t + h
                    if step >= 8:
                        pe.wait_ge(copied_a if h else copied_v, (step - 8) // 2 + 1)
                    for c in range(4):
                        m = pe.transpose(ps[step % 8][0:n, c * P:(c + 1) * P], yT[:, 4 * h + c, t * P:t * P + n], ident[:, :])
                    m.then_inc(turned, 1)

        def copy(eng, op, count, h):
            for t in range(TILES + 1):
                n = min(P, ROWS - t * P)
                eng.wait_ge(turned, 2 * t + h + 1)
                if t >= 4:
                    eng.wait_ge(rows_stored[t % 4], 16 * (t // 4))
                op(y[t % 4][0:n, h * 512:(h + 1) * 512], ps[(2 * t + h) % 8][0:n, :]).then_inc(count, 1)

        @block.vector
        def _(dve):
            copy(dve, dve.tensor_copy, copied_v, 0)

        @block.scalar
        def _(act):
            copy(act, lambda o, x: act.activation(o, x, ACT.Copy), copied_a, 1)

        @block.sync
        def _(sp):
            for t in range(TILES + 1):
                n = min(P, ROWS - t * P)
                sp.wait_ge(copied_v, t + 1)
                sp.wait_ge(copied_a, t + 1)
                dst = d["y_prompt"][0, t * P:(t + 1) * P, :] if t < TILES else d["y_sample"].rearrange("b s n -> (b s) n")
                sp.dma_start(dst, y[t % 4][0:n, :]).then_inc(rows_stored[t % 4], 16)
            for j in range(4):
                sp.wait_ge(rows_stored[j], 16 * ((TILES - j) // 4 + 1))
            sp.wait_ge(win_copied, 16)


def hymba_step(nc, dram):
    with ExitStack() as outer:
        k = Ctx(nc, outer, dram)
        ident = sb(nc, outer, "ident_m", [P, P])
        ones = sb(nc, outer, "ones_m", [P, P])
        eps = sb(nc, outer, "eps", [P, 1])
        vec = sb(nc, outer, "vec", [P, N_VEC])
        mods = sb(nc, outer, "mods", [P, 6 * KD, COND])
        state = sb(nc, outer, "state", [P, KR, 4 * DEC_BATCH])
        xT = sb(nc, outer, "xT", [P, KD, ROWS])
        oR = sb(nc, outer, "oR", [P, KR, ROWS])
        q_plain = sb(nc, outer, "q_plain", [P, DEC_BATCH, P])
        q_rot = sb(nc, outer, "q_rot", [P, DEC_BATCH, P])
        k_new = sb(nc, outer, "k_new", [P, 2, RS])
        v_new = sb(nc, outer, "v_new", [RS, 2, KV_WIDTH])
        gate_rows = sb(nc, outer, "gate_rows", [P, SG, 3])
        page_rows = sb(nc, outer, "page_rows", [P, SG, N_LCH], I32)
        page_parts = sb(nc, outer, "page_parts", [P, DEC_BATCH], I32)
        ck_s = sb(nc, outer, "ck_s", [P, DEC_BATCH * NBS])
        cv_s = sb(nc, outer, "cv_s", [NBS, DEC_BATCH, KV_WIDTH])
        ck_p = sb(nc, outer, "ck_p", [P, NBP])
        cv_p = sb(nc, outer, "cv_p", [NBP, KV_WIDTH])
        kv_stored, win_copied = k.sems("kv_stored win_copied")
        k.made = []
        dram["gate_scratch"] = nc.dram_tensor("gate_scratch", (RS, 3 * N_HEADS), F32, kind="Internal").ap()
        dram["attn_scratch"] = nc.dram_tensor("attn_scratch", (SG, QR, BT, KV_WIDTH), F32, kind="Internal").ap()
        V = {n: vec[:, a:b] for n, (a, b) in VEC.items()}

        def factor(j):
            return mods[:, j * KD:(j + 1) * KD, :]

        load_and_condition(k, xT, mods, vec, state, ident, ones, eps, page_rows, page_parts, win_copied)
        w_in = dram["w_in"][0].rearrange("(k p) n -> p k n", p=P)
        hT = sb(nc, outer, "hT", [P, KD, ROWS])
        attn = hT[:, :, :].rearrange("p k r -> p (k r)")[:, 0:(TILES + 1) * ATTN_WIDTH].rearrange(
            "p (t n) -> p t n", t=TILES + 1)
        with ExitStack() as mix:
            qT = sb(nc, mix, "qT", [P, KA, ROWS])
            with ExitStack() as inp:
                norm_rows(k, "n1", [list(range(KD))], lambda c: xT[:, c, :], lambda c: hT[:, c, :],
                          (V["ln1_g"], factor(1), lambda c: factor(0)[:, c, :], ones, eps))
                with ExitStack() as rec:
                    z = sb(nc, rec, "z", [P, 2 * KR, ROWS])
                    project(k, "s2", KR, KD,
                            lambda sp, i, p, w: [sp.dma_start(w[:, :, :], w_in[:, :, ds(i * (2 * P) + p * P, P)])],
                            lambda c: hT[:, c, :], copy_chunk(z))
                    rg_lru(k, z, oR, vec, state, ident)

                def load_q(sp, i, p, w):
                    return [sp.dma_start(w[:, :, h * HEAD_DIM:(h + 1) * HEAD_DIM],
                                         w_in[:, :, ds(i * (2 * HEAD_DIM) + Q_COL + p * HEAD_DIM + h * GROUP * HEAD_DIM, HEAD_DIM)])
                            for h in range(2)]
                take_q = copy_chunk(qT)
                take_q.n_loads = 2
                project(k, "s4q", KA // 2, KD, load_q, lambda c: hT[:, c, :], take_q)
                qR = sb(nc, inp, "qR", [P, KA, ROWS])
                kvn = sb(nc, inp, "kvn", [P, TILES + 1, KV_COLS])
                kT = sb(nc, inp, "kT", [P, 2, ROWS])
                gates = sb(nc, inp, "gates", [P, TILES + 1, 3 * N_HEADS])
                keys_and_values(k, hT, qT, qR, kvn, kT, gates, q_plain, q_rot, k_new, v_new, gate_rows, ident, kv_stored)
                compress(k, ck_s, cv_s, ck_p, cv_p, ident, page_rows, hT[:, :, :].rearrange("p k r -> p (k r)"))
                prompt_attention(k, qT, qR, kvn, kT, gates, ck_p, cv_p, attn, ident)
        k.recycle()
        sample_attention(k, q_plain, q_rot, k_new, v_new, gate_rows, ck_s, cv_s, page_parts, attn, ident,
                         hT[:, :, :].rearrange("p k r -> p (k r)")[:, (TILES + 1) * ATTN_WIDTH:])
        with ExitStack() as mo:
            merged = sb(nc, mo, "merged", [P, KR + KA, ROWS])
            turn_attention(k, attn, merged, ident)
            gains = vec[:, VEC["gn_rnn"][0]:VEC["gn_attn"][1]]
            norm_rows(k, "n2", [list(range(KR)), list(range(KR, KR + KA))],
                      lambda c: oR[:, c, :] if c < KR else merged[:, c, :], lambda c: merged[:, c, :],
                      (gains, None, None, ones, eps))
            w_out = dram["w_out"][0].rearrange("(k p) n -> p k n", p=P)
            project(k, "s9", KD // 2, KD,
                    lambda sp, i, p, w: [sp.dma_start(w[:, :, :], w_out[:, :, ds(i * (2 * P) + p * P, P)])],
                    lambda c: merged[:, c, :], add_gated(xT, factor(2)))
        norm_rows(k, "n3", [list(range(KD))], lambda c: xT[:, c, :], lambda c: hT[:, c, :],
                  (V["ln2_g"], factor(4), lambda c: factor(3)[:, c, :], ones, eps))
        with ExitStack() as ff:
            hidden = sb(nc, ff, "hidden", [P, KF, ROWS])
            ffn_up(k, hT, hidden, oR)
            w_down = dram["w_down"][0].rearrange("(k p) n -> p k n", p=P)
            project(k, "s12", KD // 2, KF,
                    lambda sp, i, p, w: [sp.dma_start(w[:, :, :], w_down[:, :, ds(i * (2 * P) + p * P, P)])],
                    lambda c: hidden[:, c, :], add_gated(xT, factor(5)), hT[:, :, :].rearrange("p k r -> p (k r)"))
        norm_rows(k, "n4", [list(range(KD))], lambda c: xT[:, c, :], lambda c: xT[:, c, :],
                  (V["final_g"], None, None, ones, eps))
        store_rows(k, xT, ident, win_copied)


_INS = ['x_prompt', 'x_sample', 'cache_cmp_kv', 'cache_sel_kv', 'state_win_kv', 'state_conv', 'state_lru_h',
        'page_table', 'c_prompt', 'c_sample', 'ln1_g', 'ln2_g', 'w_ada', 'b_ada', 'w_in', 'conv_w', 'conv_b',
        'lru_wa', 'lru_ba', 'lru_wx', 'lru_bx', 'lru_lambda', 'cmp_pe', 'cmp_w1', 'cmp_w2', 'gn_rnn', 'gn_attn',
        'w_out', 'w_gate', 'w_up', 'w_down', 'final_g']
_OUTS = [("y_prompt", (1, SEQ, D_MODEL)), ("y_sample", (DEC_BATCH, DEC_SEQ, D_MODEL)),
         ("new_cmp_prompt", (1, 1, SEQ, 2, N_KV, HEAD_DIM)), ("new_cmp_sample", (1, DEC_BATCH, DEC_SEQ, 2, N_KV, HEAD_DIM)),
         ("new_sel_prompt", (1, 1, SEQ, 2, N_KV, HEAD_DIM)), ("new_sel_sample", (1, DEC_BATCH, DEC_SEQ, 2, N_KV, HEAD_DIM)),
         ("new_win_prompt", (1, 1, WINDOW, 2, N_KV, HEAD_DIM)), ("new_win_sample", (1, DEC_BATCH, WINDOW, 2, N_KV, HEAD_DIM)),
         ("new_conv_prompt", (1, 1, CONV_W - 1, RNN_WIDTH)), ("new_conv_sample", (1, DEC_BATCH, CONV_W - 1, RNN_WIDTH)),
         ("new_lru_h_prompt", (1, 1, RNN_WIDTH)), ("new_lru_h_sample", (1, DEC_BATCH, RNN_WIDTH))]


def kernel(**inputs):
    import concourse.bacc as _bacc
    from concourse.bass_utils import run_bass_kernel_spmd as _run

    nc = _bacc.Bacc("TRN2", target_bir_lowering=False, num_devices=1)
    arrays, dram = {}, {}
    laid = {name: np.ascontiguousarray(inputs[name]) for name in _INS}
    laid.update(constants())
    for name, a in laid.items():
        arrays[f"in_{name}"] = a
        dram[name] = nc.dram_tensor(f"in_{name}", a.shape, mybir.dt.from_np(a.dtype), kind="ExternalInput").ap()
    for name, shape in _OUTS:
        dram[name] = nc.dram_tensor(f"out_{name}", shape, F32, kind="ExternalOutput").ap()
    hymba_step(nc, dram)
    r = _run(nc, [arrays], core_ids=[0])
    return tuple(r.results[0][f"out_{name}"] for name, _ in _OUTS)
```

```python
import math
from contextlib import ExitStack

import numpy as np

import concourse.bass as bass
from concourse import mybir

F32 = mybir.dt.float32
I32 = mybir.dt.int32
ALU = mybir.AluOpType
ACT = mybir.ActivationFunctionType
AX = mybir.AxisListType.X
ds = bass.ds

P = 128
D_MODEL = 1024
SEQ = 1024
DEC_BATCH = 8
DEC_SEQ = 4
PAST_LEN = 2048
PAGE_SIZE = 128
N_PAGES = PAST_LEN // PAGE_SIZE
HEAD_DIM = 64
N_HEADS = 8
N_KV = 2
GROUP = N_HEADS // N_KV
ATTN_WIDTH = N_HEADS * HEAD_DIM
KV_WIDTH = N_KV * HEAD_DIM
BLOCK = 64
CMP_HIDDEN = 128
N_SEL = 16
WINDOW = 512
ROT_DIM = HEAD_DIM // 4
HALF = ROT_DIM // 2
ROPE_THETA = 500000.0
RNN_WIDTH = D_MODEL - ATTN_WIDTH
RNN_BLOCK_W = RNN_WIDTH // 8
CONV_W = 4
LRU_C = 8.0
D_FF = ((8 * D_MODEL + 3 * 256 - 1) // (3 * 256)) * 256
SCALE = HEAD_DIM ** -0.5
EPS = 1e-6
NEG = -1e30

KD = D_MODEL // P
RS = DEC_BATCH * DEC_SEQ
ROWS = SEQ + RS
TILES = SEQ // P
NG = 3
GR = ROWS // NG
KR = RNN_WIDTH // P
KA = ATTN_WIDTH // P
KF = D_FF // P
COND = 1 + DEC_BATCH
KV_COLS = 6 * KV_WIDTH
NAT_COLS = KV_COLS + 3 * N_HEADS
Q_COL = 2 * RNN_WIDTH
NAT_COL = Q_COL + ATTN_WIDTH
NBP = SEQ // BLOCK
NBS = PAST_LEN // BLOCK
SG = DEC_BATCH // 4
BT = DEC_BATCH // SG
QR = N_KV * DEC_SEQ * GROUP
TP = PAST_LEN // P
WP = WINDOW // P
L_CHUNK = 8
N_LCH = BLOCK // L_CHUNK
ROWF = L_CHUNK * 2 * KV_WIDTH
NFREE = N_SEL - 3
NCAND = NBS - 2

VEC = {}
_at = 0
for _name, _n in (("b_ada", 6 * KD), ("ln1_g", KD), ("ln2_g", KD), ("final_g", KD), ("gn_rnn", KR),
                  ("gn_attn", KA), ("conv_w", CONV_W * KR), ("conv_b", KR), ("lru_ba", KR), ("lru_bx", KR),
                  ("lru_lambda", KR)):
    VEC[_name] = (_at, _at + _n)
    _at += _n
N_VEC = _at


class Steps:

    def __init__(self, eng, sem):
        self.eng, self.sem, self.base, self.n = eng, sem, 0, 0

    def done(self, ins):
        ins.then_inc(self.sem, 1)
        self.n += 1

    def fence(self):
        self.eng.wait_ge(self.sem, self.base + self.n)

    def then(self, ins):
        self.done(ins)
        self.fence()

    def enter(self, i, per):
        self.start, self.per = self.base + self.n, per
        self.base, self.n = self.start + i * per, 0

    def leave(self, trips):
        assert self.n == self.per, (self.n, self.per)
        self.base, self.n = self.start + trips * self.per, 0


def bcast(ap, axis, n):
    v = ap.unsqueeze(axis)
    shape = list(v.shape)
    shape[axis] = n
    return v.to_broadcast(shape)


def constants():
    f = np.float32
    c = {}
    c["ident"] = np.eye(P, dtype=f)
    inv = np.exp(np.arange(HALF, dtype=f) * f(-math.log(ROPE_THETA) / HALF)).astype(f)
    pos = np.concatenate([np.arange(SEQ), np.tile(PAST_LEN + np.arange(DEC_SEQ), DEC_BATCH)]).astype(f)
    ang = (pos[:, None] * inv[None, :]).astype(f)
    cos, sin = np.cos(ang.astype(np.float64)).astype(f), np.sin(ang.astype(np.float64)).astype(f)
    ct, st = np.ones((P, ROWS), f), np.zeros((P, ROWS), f)
    rot = np.zeros((P, P), f)
    for h in range(2):
        for d in range(ROT_DIM):
            ct[h * HEAD_DIM + d] = cos[:, d % HALF]
            st[h * HEAD_DIM + d] = sin[:, d % HALF]
        for d in range(HALF):
            rot[h * HEAD_DIM + d + HALF, h * HEAD_DIM + d] = -1
            rot[h * HEAD_DIM + d, h * HEAD_DIM + d + HALF] = 1
    c["cos_t"], c["sin_t"], c["rot"] = ct, st, rot
    nat = np.zeros((P, 2, TILES + 1, HALF), f)
    for t in range(TILES + 1):
        n = min(P, ROWS - t * P)
        nat[:n, 0, t], nat[:n, 1, t] = cos[t * P:t * P + n], sin[t * P:t * P + n]
    c["rope_nat"] = nat.reshape(P, -1)
    q, k = np.arange(P)[:, None], np.arange(P)[None, :]
    c["mask_diag"] = np.where(k > q, f(NEG), f(0))
    c["mask_tail"] = np.where(k <= q, f(NEG), f(0))
    qpos = np.arange(TILES)[None, :, None] * P + np.arange(P)[:, None, None]
    end = (np.arange(NBP)[None, None, :] + 1) * BLOCK - 1
    c["mask_cmp"] = np.where(end <= qpos, f(0), f(NEG)).reshape(P, -1)
    r = np.arange(P)
    rb, rs = r // QR, (r % 16) // GROUP
    col = np.arange(RS)
    m = np.zeros((P, SG, RS), f)
    for g in range(SG):
        own = (col[None, :] // DEC_SEQ == (g * BT + rb)[:, None]) & (col[None, :] % DEC_SEQ <= rs[:, None])
        m[:, g] = np.where(own, f(0), f(NEG))
    c["mask_new"] = m.reshape(P, -1)
    tok = np.arange(P)[None, None, :] * WP + np.arange(WP)[None, :, None]
    c["mask_win"] = np.where(tok > rs[:, None, None], f(0), f(NEG)).reshape(P, -1)
    c["same_query"] = (r[:, None] // GROUP == r[None, :] // GROUP).astype(f)
    j, i = np.arange(NCAND)[:, None], np.arange(NCAND)[None, :]
    c["earlier"] = np.broadcast_to((i < j).astype(f).reshape(1, -1), (P, NCAND * NCAND)).copy()
    c["row_in_block"] = (np.arange(P)[:, None] % 2 * N_LCH + np.arange(N_LCH)[None, :]).astype(np.int32)
    c["part_in_page"] = (np.arange(P)[:, None] % 8 + np.zeros((1, DEC_BATCH), int)).astype(np.int32)
    return c


class Ctx:

    def __init__(self, nc, stack, dram):
        self.nc, self.stack, self.dram, self.made = nc, stack, dram, []
        self.psum = stack.enter_context(nc.psum_tensor("banks", [P, 8 * 512], F32))
        self.ps = [self.psum[:, j * 512:(j + 1) * 512] for j in range(8)]

    def sems(self, names):
        made = [self.nc.alloc_semaphore(name=n) for n in names.split()]
        self.made += made
        return made

    def recycle(self):
        self.nc.clear_and_free_semaphores(self.made)
        self.made = []
        self.nc.all_engine_barrier()


def sb(nc, stack, name, shape, dt=F32):
    return stack.enter_context(nc.sbuf_tensor(name, shape, dt))


WC = 4
LATE_WC = 2
EARLY = 2 * KD


def factor_products(pe, bank, at, w, cT, n):
    for m in range(n):
        for c in range(KD):
            mm = pe.matmul(bank[:, ds(at * COND + m * COND, COND)], lhsT=w[:, c, m * P:(m + 1) * P], rhs=cT[:, c, :],
                           start=(c == 0), stop=(c == KD - 1))
    return mm


def load_and_condition(k, xT, mods, vec, state, cT, ident, ones, eps, page_rows, page_parts, win_copied, space):
    nc, ps, d = k.nc, k.ps, k.dram
    (ident_loaded, vec_loaded, cond_loaded, state_loaded, x_loaded0, x_loaded1, x_loaded2, w_loaded0, w_loaded1,
     cond_ready, small_turned, small_copied, x_turned, x_copied_v, x_copied_a, mods_summed0, mods_summed1,
     consts_set, pages_loaded, pages_ready) = k.sems(
        "s1_ident_loaded s1_vec_loaded s1_cond_loaded s1_state_loaded s1_x_loaded0 s1_x_loaded1 s1_x_loaded2 "
        "s1_w_loaded0 s1_w_loaded1 s1_cond_ready s1_small_turned s1_small_copied s1_x_turned s1_x_copied_v "
        "s1_x_copied_a s1_mods_summed0 s1_mods_summed1 s1_consts_set s1_pages_loaded s1_pages_ready")
    x_loaded, w_loaded = [x_loaded0, x_loaded1, x_loaded2], [w_loaded0, w_loaded1]
    mods_summed = [mods_summed0, mods_summed1]
    w_view = d["w_ada"][0].rearrange("(k p) n -> p k n", p=P)
    with ExitStack() as st:
        x_nat = sb(nc, st, "x_nat", [P, TILES + 1, D_MODEL])
        vec_nat = sb(nc, st, "vec_nat", [P, P])
        c_nat = sb(nc, st, "c_nat", [COND, D_MODEL])
        c_act = sb(nc, st, "c_act", [COND, D_MODEL])
        s_nat = sb(nc, st, "s_nat", [4 * DEC_BATCH, RNN_WIDTH])
        w = [space[:, p * KD * WC * P:(p + 1) * KD * WC * P].rearrange("p (k n) -> p k n", k=KD) for p in range(2)]
        table = sb(nc, st, "page_table", [P, SG + DEC_BATCH], I32)
        iota = sb(nc, st, "page_iota", [P, N_LCH + DEC_BATCH], I32)
        block = st.enter_context(nc.Block())

        @block.sync
        def _(sp):
            sp.dma_start(ident[:, :], d["ident"]).then_inc(ident_loaded, 16)
            sp.dma_start(c_nat[0:1, :], d["c_prompt"]).then_inc(cond_loaded, 16)
            sp.dma_start(c_nat[1:COND, :], d["c_sample"]).then_inc(cond_loaded, 16)
            for j in range(2):
                sp.dma_start(x_nat[:, 4 * j:4 * j + 4, :],
                             d["x_prompt"][0, 4 * j * P:(4 * j + 4) * P, :].rearrange("(t p) n -> p t n", p=P)
                             ).then_inc(x_loaded[j], 16)
            sp.dma_start(x_nat[0:RS, TILES, :], d["x_sample"].rearrange("b s n -> (b s) n")).then_inc(x_loaded[2], 16)
            with sp.Fori(0, EARLY // WC // 2) as i:
                for p in range(2):
                    sp.wait_ge(mods_summed[p], i + 1)
                    sp.dma_start(w[p], w_view[:, :, ds(i * (2 * WC * P) + p * WC * P, WC * P)]
                                 ).then_inc(w_loaded[p], 16)

        @block.gpsimd
        def _(pool):
            flat = d["page_table"].rearrange("b j -> (b j)")
            for g in range(SG):
                pool.dma_start(table[:, g:g + 1], bcast(flat[g * P // 2:(g + 1) * P // 2], 1, 2).unsqueeze(2),
                               allow_slow_non_contiguous=True).then_inc(pages_loaded, 16)
            for b in range(DEC_BATCH):
                pool.dma_start(table[:, SG + b:SG + b + 1], bcast(d["page_table"][b], 1, 8).unsqueeze(2),
                               allow_slow_non_contiguous=True).then_inc(pages_loaded, 16)
            pool.dma_start(iota[:, 0:N_LCH], d["row_in_block"]).then_inc(pages_loaded, 16)
            pool.dma_start(iota[:, N_LCH:], d["part_in_page"]).then_inc(pages_loaded, 16)
            pool.dma_start(d["new_win_sample"][0].rearrange("b s c h d -> b s (c h d)")[:, 0:WINDOW - DEC_SEQ, :],
                           d["state_win_kv"][0].rearrange("b s c h d -> b s (c h d)")[:, DEC_SEQ:, :]).then_inc(win_copied, 16)
            pool.memset(ones[:, :], 1.0).then_inc(consts_set, 1)
            pool.memset(eps[:, :], EPS).then_inc(consts_set, 1)
            for name, (a, b) in VEC.items():
                src = d[name]
                while len(src.shape) > 1:
                    src = src.rearrange("a b -> (a b)") if len(src.shape) == 2 else src.rearrange("a b c -> (a b c)")
                pool.dma_start(vec_nat[a:b, :], src.rearrange("(r n) -> r n", n=P)).then_inc(vec_loaded, 16)
            pool.dma_start(s_nat[0:3 * DEC_BATCH, :], d["state_conv"][0].rearrange("b w n -> (b w) n")
                           ).then_inc(state_loaded, 16)
            pool.dma_start(s_nat[3 * DEC_BATCH:4 * DEC_BATCH, :], d["state_lru_h"][0]).then_inc(state_loaded, 16)
            pool.wait_ge(consts_set, 2)

        @block.tensor
        def _(pe):
            pe.sem_inc(mods_summed[0], 1)
            pe.sem_inc(mods_summed[1], 1)
            pe.wait_ge(ident_loaded, 16)
            pe.wait_ge(vec_loaded, 16 * len(VEC))
            pe.transpose(ps[4][:, 0:N_VEC], vec_nat[0:N_VEC, :], ident[0:N_VEC, 0:N_VEC]).then_inc(small_turned, 1)
            pe.wait_ge(cond_ready, 1)
            for c in range(KD):
                t = pe.transpose(ps[5][:, c * COND:(c + 1) * COND], c_act[:, c * P:(c + 1) * P], ident[0:COND, 0:COND])
            t.then_inc(small_turned, 1)
            pe.wait_ge(state_loaded, 32)
            for c in range(KR):
                t = pe.transpose(ps[6][:, c * 32:(c + 1) * 32], s_nat[:, c * P:(c + 1) * P], ident[0:32, 0:32])
            t.then_inc(small_turned, 1)
            for t in range(TILES + 1):
                n = min(P, ROWS - t * P)
                pe.wait_ge(x_loaded[min(t // 4, 2)], 16)
                for h in range(2):
                    step = 2 * t + h
                    if step >= 4:
                        pe.wait_ge(x_copied_a if h else x_copied_v, (step - 4) // 2 + 1)
                    for c in range(4):
                        m = pe.transpose(ps[step % 4][:, c * P:c * P + n], x_nat[0:n, t, (4 * h + c) * P:(4 * h + c + 1) * P],
                                         ident[0:n, 0:n])
                    m.then_inc(x_turned, 1)
            pe.wait_ge(small_copied, 2)
            with pe.Fori(0, EARLY // WC // 2) as i:
                for p in range(2):
                    pe.wait_ge(w_loaded[p], i * 16 + 16)
                    factor_products(pe, ps[7], i * (2 * WC) + p * WC, w[p], cT, WC).then_inc(mods_summed[p], 1)

        @block.scalar
        def _(act):
            act.wait_ge(cond_loaded, 32)
            act.activation(c_act[:, :], c_nat[:, :], ACT.Silu).then_inc(cond_ready, 1)
            for t in range(TILES + 1):
                n = min(P, ROWS - t * P)
                act.wait_ge(x_turned, 2 * t + 2)
                act.activation(xT[:, 4:8, t * P:t * P + n],
                               ps[(2 * t + 1) % 4][:, :].rearrange("p (c n) -> p c n", c=4)[:, :, 0:n],
                               ACT.Copy).then_inc(x_copied_a, 1)

        @block.vector
        def _(dve):
            dve.wait_ge(small_turned, 1)
            dve.tensor_copy(vec[:, :], ps[4][:, 0:N_VEC]).then_inc(small_copied, 1)
            dve.wait_ge(small_turned, 2)
            dve.tensor_copy(cT[:, :, :], ps[5][:, 0:KD * COND].rearrange("p (c n) -> p c n", c=KD)).then_inc(small_copied, 1)
            dve.wait_ge(small_turned, 3)
            dve.tensor_copy(state[:, :, :], ps[6][:, 0:KR * 32].rearrange("p (c n) -> p c n", c=KR)).then_inc(small_copied, 1)
            for t in range(TILES + 1):
                n = min(P, ROWS - t * P)
                dve.wait_ge(x_turned, 2 * t + 1)
                dve.tensor_copy(xT[:, 0:4, t * P:t * P + n],
                                ps[(2 * t) % 4][:, :].rearrange("p (c n) -> p c n", c=4)[:, :, 0:n]
                                ).then_inc(x_copied_v, 1)
            dve.wait_ge(small_copied, 1)
            dve.wait_ge(pages_loaded, 16 * (SG + DEC_BATCH + 2))
            for g in range(SG):
                dve.scalar_tensor_tensor(page_rows[:, g, :], table[:, g:g + 1].to_broadcast([P, N_LCH]), 2 * N_LCH,
                                         iota[:, 0:N_LCH], ALU.mult, ALU.add).then_inc(pages_ready, 1)
            dve.scalar_tensor_tensor(page_parts[:, :], table[:, SG:], 8, iota[:, N_LCH:], ALU.mult, ALU.add
                                     ).then_inc(pages_ready, 1)
            dve.wait_ge(pages_ready, SG + 1)
            for q in range(2):
                dve.wait_ge(mods_summed[q], EARLY // WC // 2 + 1)
            dve.tensor_tensor(mods[:, 0:EARLY, :], ps[7][:, 0:EARLY * COND].rearrange("p (m c) -> p m c", m=EARLY),
                              bcast(vec[:, 0:EARLY], 2, COND), ALU.add)


def norm_rows(k, tag, parts, sources, outs, adaln=None):
    nc, ps = k.nc, k.ps
    g_of, factors, shifts, ones, eps = adaln
    sq_ready, sq_used0, sq_used1, summed, root_ready, stepped, scaled, done_a = k.sems(
        " ".join(f"{tag}_{n}" for n in "sq_ready sq_used0 sq_used1 summed root_ready stepped scaled done_a".split()))
    sq_used = [sq_used0, sq_used1]
    NPART = len(parts)
    with ExitStack() as st:
        sq = [sb(nc, st, f"{tag}_sq{p}", [P, ROWS]) for p in range(2)]
        rstd = [sb(nc, st, f"{tag}_rstd{n}", [P, ROWS]) for n in range(NPART)]
        gain = sb(nc, st, f"{tag}_gain", [P, KD, COND])
        block = st.enter_context(nc.Block())

        @block.scalar
        def _(act):
            n = 0
            for chunks in parts:
                for c in chunks:
                    if n >= 2:
                        act.wait_ge(sq_used[n % 2], n // 2)
                    act.activation(sq[n % 2][:, :], sources(c), ACT.Square).then_inc(sq_ready, 1)
                    n += 1
            for j, chunks in enumerate(parts):
                act.wait_ge(summed, j + 1)
                for g in range(NG):
                    r = act.activation(rstd[j][:, g * GR:(g + 1) * GR], ps[NG * j + g][:, 0:GR], ACT.Sqrt,
                                       bias=eps[:, 0:1], scale=1.0 / (P * len(chunks)))
                r.then_inc(root_ready, 1)
            if shifts is not None:
                for n, c in enumerate(c for chunks in parts for c in chunks):
                    act.wait_ge(scaled, n + 1)
                    act.activation(outs(c)[:, 0:SEQ], outs(c)[:, 0:SEQ], ACT.Identity, bias=shifts(c)[:, 0:1],
                                   scale=gain[:, c, 0:1]).then_inc(done_a, 1)
                act.wait_ge(done_a, KD)

        @block.tensor
        def _(pe):
            n = 0
            for j, chunks in enumerate(parts):
                for i, c in enumerate(chunks):
                    pe.wait_ge(sq_ready, n + 1)
                    for g in range(NG):
                        m = pe.matmul(ps[NG * j + g][:, 0:GR], lhsT=ones[:, :], rhs=sq[n % 2][:, g * GR:(g + 1) * GR],
                                      start=(i == 0), stop=(i == len(chunks) - 1))
                    m.then_inc(sq_used[n % 2], 1)
                    n += 1
                pe.wait_ge(sq_used[(n - 1) % 2], (n - 1) // 2 + 1)
                pe.sem_inc(summed, 1)

        @block.vector
        def _(dve):
            s = Steps(dve, stepped)
            if shifts is not None:
                s.done(dve.scalar_tensor_tensor(gain[:, :, :], factors, 1.0, bcast(g_of, 2, COND), ALU.add, ALU.mult))
            n = 0
            for j, chunks in enumerate(parts):
                dve.wait_ge(root_ready, j + 1)
                s.then(dve.reciprocal(rstd[j][:, :], rstd[j][:, :]))
                for c in chunks:
                    if shifts is None:
                        dve.scalar_tensor_tensor(outs(c), sources(c), g_of[:, n:n + 1], rstd[j][:, :], ALU.mult,
                                                 ALU.mult).then_inc(scaled, 1)
                    else:
                        dve.tensor_tensor(outs(c), sources(c), rstd[j][:, :], ALU.mult).then_inc(scaled, 1)
                    n += 1
            if shifts is not None:
                for n, c in enumerate(c for chunks in parts for c in chunks):
                    rows = outs(c)[:, SEQ:ROWS].rearrange("p (b s) -> p b s", b=DEC_BATCH)
                    dve.wait_ge(scaled, n + 1)
                    s.then(dve.tensor_tensor(rows, rows, bcast(gain[:, c, 1:COND], 2, DEC_SEQ), ALU.mult))
                    s.then(dve.tensor_tensor(rows, rows, bcast(shifts(c)[:, 1:COND], 2, DEC_SEQ), ALU.add))
            dve.wait_ge(scaled, sum(map(len, parts)))


def copy_chunk(dst):
    def take(dve, s, i, p, banks, tmp):
        for g in range(NG):
            r = dve.tensor_copy(dst[:, ds(i * 2 + p, 1), g * GR:(g + 1) * GR], banks[g].unsqueeze(1))
            if g < NG - 1:
                s.done(r)
        return r
    take.per = 2 * (NG - 1)
    return take


def rg_lru(k, z_in, z_gate, vec, state, mods, cT, ident):
    nc, ps, d = k.nc, k.ps, k.dram
    (cleared, loaded, conv_done, stepped, summed, act_done, rates_ready, last_ready, last_turned, last_copied, stored,
     abs_ready, decay_ready, ada_loaded0, ada_loaded1, ada_summed0, ada_summed1) = k.sems(
        "s3_cleared s3_loaded s3_conv_done s3_stepped s3_summed s3_act_done s3_rates_ready s3_last_ready s3_last_turned "
        "s3_last_copied s3_stored s3_abs_ready s3_decay_ready "
        "s3_ada_loaded0 s3_ada_loaded1 s3_ada_summed0 s3_ada_summed1")
    ada_loaded, ada_summed = [ada_loaded0, ada_loaded1], [ada_summed0, ada_summed1]
    ada_view = d["w_ada"][0].rearrange("(k p) n -> p k n", p=P)
    LATE = 6 * KD - EARLY
    PAIRS = LATE // LATE_WC // 2
    V = {n: vec[:, a:b] for n, (a, b) in VEC.items()}
    LAST = 3 + 3 * DEC_BATCH + 1 + DEC_BATCH
    with ExitStack() as st:
        wa = sb(nc, st, "wa", [P, 2, KR, P])
        r4 = sb(nc, st, "r4", [P, KR, ROWS])
        i4 = sb(nc, st, "i4", [P, KR, ROWS])
        conv = sb(nc, st, "conv", [P, KR, ROWS])
        w_ada = [sb(nc, st, f"late_ada{p}", [P, KD, LATE_WC * P]) for p in range(2)]
        a4 = z_in[:, :, :]
        xs = sb(nc, st, "xs", [P, KR, DEC_BATCH, CONV_W - 1 + DEC_SEQ])
        t = sb(nc, st, "lru_small", [P, 8, KR])
        last = sb(nc, st, "last", [P, KR, LAST])
        last_nat = i4[0:LAST, 0, 0:RNN_WIDTH]
        block = st.enter_context(nc.Block())

        @block.sync
        def _(sp):
            sp.wait_ge(cleared, 1)
            for j, w in enumerate(("lru_wa", "lru_wx")):
                for h in range(2):
                    b = h * RNN_BLOCK_W
                    sp.dma_start(wa[b:b + RNN_BLOCK_W, j, :, b:b + RNN_BLOCK_W],
                                 d[w][0].rearrange("(c h) a e -> h a c e", h=2)[h]).then_inc(loaded, 16)
            with sp.Fori(0, PAIRS) as i:
                for p in range(2):
                    sp.wait_ge(ada_summed[p], i + 1)
                    sp.dma_start(w_ada[p][:, :, :], ada_view[:, :, ds(i * (2 * LATE_WC * P) + (EARLY + p * LATE_WC) * P, LATE_WC * P)]
                                 ).then_inc(ada_loaded[p], 16)
            sp.wait_ge(last_copied, 1)
            n = 3 * DEC_BATCH
            sp.dma_start(d["new_conv_prompt"][0, 0], last_nat[0:3, :]).then_inc(stored, 16)
            sp.dma_start(d["new_conv_sample"][0].rearrange("b w n -> (b w) n"), last_nat[3:3 + n, :]).then_inc(stored, 16)
            sp.dma_start(d["new_lru_h_prompt"][0], last_nat[3 + n:4 + n, :]).then_inc(stored, 16)
            sp.dma_start(d["new_lru_h_sample"][0], last_nat[4 + n:LAST, :]).then_inc(stored, 16)
            sp.wait_ge(stored, 64)

        @block.gpsimd
        def _(pool):
            pool.memset(wa[:, :, :, :], 0.0).then_inc(cleared, 1)

        @block.tensor
        def _(pe):
            def factors(i):
                for p in range(2):
                    pe.wait_ge(ada_loaded[p], i * 16 + 16)
                    factor_products(pe, ps[7], i * (2 * LATE_WC) + p * LATE_WC, w_ada[p], cT, LATE_WC
                                    ).then_inc(ada_summed[p], 1)
            pe.sem_inc(ada_summed[0], 1)
            pe.sem_inc(ada_summed[1], 1)
            pe.wait_ge(loaded, 64)
            for c in range(KR):
                pe.wait_ge(conv_done, c + 1)
                if c:
                    pe.wait_ge(act_done, 2 * c)
                for j in range(2):
                    for g in range(NG):
                        m = pe.matmul(ps[NG * j + g][:, 0:GR], lhsT=wa[:, j, c, :], rhs=conv[:, c, g * GR:(g + 1) * GR],
                                      start=True, stop=True)
                    m.then_inc(summed, 1)
                factors(c)
            with pe.Fori(0, PAIRS - KR) as i:
                factors(i + KR)
            pe.wait_ge(last_ready, 1)
            for c in range(KR):
                m = pe.transpose(ps[6][0:LAST, c * P:(c + 1) * P], last[:, c, :], ident[:, :])
            m.then_inc(last_turned, 1)

        @block.scalar
        def _(act):
            s = Steps(act, act_done)
            for c in range(KR):
                for j, (dst, b) in enumerate(((r4, "lru_ba"), (i4, "lru_bx"))):
                    act.wait_ge(summed, 2 * c + j + 1)
                    for g in range(NG):
                        r = act.activation(dst[:, c, g * GR:(g + 1) * GR], ps[NG * j + g][:, 0:GR], ACT.Sigmoid,
                                           bias=V[b][:, c:c + 1])
                    s.done(r)
            act.wait_ge(abs_ready, 1)
            act.activation(t[:, 1, :], t[:, 0, :], ACT.Exp).then_inc(rates_ready, 1)
            s.fence()
            act.wait_ge(decay_ready, 1)
            for c in range(KR):
                s.done(act.activation(a4[:, c, :], r4[:, c, :], ACT.Exp, scale=t[:, 6, c:c + 1]))
                s.fence()
                s.done(act.activation(r4[:, c, :], r4[:, c, :], ACT.Tanh, scale=t[:, 7, c:c + 1]))
            for c in range(KR):
                act.wait_ge(rates_ready, 2 + c)
                s.done(act.activation(r4[:, c, :], r4[:, c, :], ACT.Sqrt, scale=2.0))
            for c in range(KR):
                s.done(act.activation(z_gate[:, c, :], z_gate[:, c, :], ACT.Gelu_apprx_tanh))

        @block.vector
        def _(dve):
            s = Steps(dve, stepped)
            lam = V["lru_lambda"]
            s.then(dve.tensor_scalar(t[:, 2, :], lam, -1.0, None, ALU.mult))
            dve.tensor_tensor(t[:, 0, :], lam, t[:, 2, :], ALU.min).then_inc(abs_ready, 1)
            s.done(dve.tensor_copy(xs[:, :, :, 0:3], state[:, :, 0:3 * DEC_BATCH].rearrange("p c (b w) -> p c b w", w=3)))
            s.then(dve.tensor_copy(xs[:, :, :, 3:], z_in[:, :, SEQ:ROWS].rearrange("p c (b s) -> p c b s", s=DEC_SEQ)))
            s.done(dve.tensor_copy(last[:, :, 0:3], z_in[:, :, SEQ - 3:SEQ]))
            s.done(dve.tensor_copy(last[:, :, 3:3 + 3 * DEC_BATCH].rearrange("p c (b w) -> p c b w", w=3), xs[:, :, :, DEC_SEQ:]))
            for c in range(KR):
                x, o = z_in[:, c, :], conv[:, c, :]
                so = o[:, SEQ:ROWS].rearrange("p (b s) -> p b s", s=DEC_SEQ)
                w = [V["conv_w"][:, j * KR + c:j * KR + c + 1] for j in range(CONV_W)]
                b = V["conv_b"][:, c:c + 1]
                s.done(dve.tensor_scalar(o[:, 0:SEQ], x[:, 0:SEQ], w[3], b, ALU.mult, ALU.add))
                s.then(dve.tensor_scalar(so, xs[:, c, :, 3:3 + DEC_SEQ], w[3], b, ALU.mult, ALU.add))
                for j in (2, 1, 0):
                    lag = 3 - j
                    s.done(dve.scalar_tensor_tensor(o[:, lag:SEQ], x[:, 0:SEQ - lag], w[j], o[:, lag:SEQ], ALU.mult, ALU.add))
                    r = dve.scalar_tensor_tensor(so, xs[:, c, :, j:j + DEC_SEQ], w[j], so, ALU.mult, ALU.add)
                    if j:
                        s.then(r)
                    else:
                        s.fence()
                        r.then_inc(conv_done, 1)
            dve.wait_ge(rates_ready, 1)
            s.then(dve.tensor_scalar(t[:, 3, :], t[:, 1, :], 2.0, None, ALU.add))
            s.then(dve.reciprocal(t[:, 3, :], t[:, 3, :]))
            s.then(dve.tensor_tensor(t[:, 1, :], t[:, 1, :], t[:, 3, :], ALU.mult))
            s.then(dve.tensor_tensor(t[:, 3, :], t[:, 1, :], t[:, 1, :], ALU.mult))
            s.then(dve.tensor_scalar(t[:, 4, :], t[:, 3, :], 1.0 / 17, 1.0 / 15, ALU.mult, ALU.add))
            for n in (13, 11, 9, 7, 5, 3, 1):
                s.then(dve.tensor_tensor(t[:, 4, :], t[:, 4, :], t[:, 3, :], ALU.mult))
                s.then(dve.tensor_scalar(t[:, 4, :], t[:, 4, :], 1.0 / n, None, ALU.add))
            s.then(dve.scalar_tensor_tensor(t[:, 4, :], t[:, 4, :], 2.0, t[:, 1, :], ALU.mult, ALU.mult))
            s.then(dve.scalar_tensor_tensor(t[:, 5, :], t[:, 2, :], 0.0, t[:, 4, :], ALU.max, ALU.add))
            s.then(dve.tensor_scalar(t[:, 6, :], t[:, 5, :], -LRU_C, None, ALU.mult))
            dve.tensor_scalar(t[:, 7, :], t[:, 5, :], LRU_C, None, ALU.mult).then_inc(decay_ready, 1)
            for c in range(KR):
                dve.wait_ge(act_done, 2 * KR + 2 * c + 2)
                s.then(dve.tensor_tensor(conv[:, c, :], conv[:, c, :], i4[:, c, :], ALU.mult))
                s.then(dve.tensor_scalar(i4[:, c, :], r4[:, c, :], 1.0, None, ALU.add))
                s.then(dve.reciprocal(i4[:, c, :], i4[:, c, :]))
                dve.tensor_tensor(r4[:, c, :], r4[:, c, :], i4[:, c, :], ALU.mult).then_inc(rates_ready, 1)
            for c in range(KR):
                dve.wait_ge(act_done, 4 * KR + c + 1)
                s.then(dve.tensor_tensor(r4[:, c, :], r4[:, c, :], conv[:, c, :], ALU.mult))
                first_b = r4[:, c, SEQ:ROWS:DEC_SEQ]
                first_a = a4[:, c, SEQ:ROWS:DEC_SEQ]
                s.then(dve.tensor_tensor(t[:, 0:2, :].rearrange("p a b -> p (a b)"), first_a, state[:, c, 3 * DEC_BATCH:], ALU.mult))
                s.then(dve.tensor_tensor(first_b, first_b, t[:, 0:2, :].rearrange("p a b -> p (a b)"), ALU.add))
                s.then(dve.memset(first_a, 0.0))
                s.then(dve.tensor_tensor_scan(conv[:, c, :], a4[:, c, :], r4[:, c, :], 0.0, ALU.mult, ALU.add))
                s.done(dve.tensor_copy(last[:, c, 27:28], conv[:, c, SEQ - 1:SEQ]))
                s.done(dve.tensor_copy(last[:, c, 28:36], conv[:, c, SEQ + DEC_SEQ - 1:ROWS:DEC_SEQ]))
            s.fence()
            dve.sem_inc(last_ready, 1)
            for c in range(KR):
                dve.wait_ge(act_done, 5 * KR + c + 1)
                s.done(dve.tensor_tensor(z_gate[:, c, :], conv[:, c, :], z_gate[:, c, :], ALU.mult))
            for p in range(2):
                dve.wait_ge(ada_summed[p], PAIRS + 1)
            dve.tensor_tensor(mods[:, EARLY:, :], ps[7][:, 0:LATE * COND].rearrange("p (m c) -> p m c", m=LATE),
                              bcast(vec[:, EARLY:6 * KD], 2, COND), ALU.add)
            dve.wait_ge(last_turned, 1)
            dve.tensor_copy(last_nat, ps[6][0:LAST, :]).then_inc(last_copied, 1)


def keys_and_values(k, hT, qT, qR, kvn, kT, gates, q_plain, q_rot, k_new, v_new, gate_rows, ident, kv_stored):
    nc, ps, d = k.nc, k.ps, k.dram
    (w_loaded, tabs_loaded, rot_summed, turned_taken, nat_summed, nat_v, nat_a, stepped, keys_ready, gates_ready,
     scratch_stored, gates_loaded, staged_clear, queries_rotated) = k.sems(
        "s4_w_loaded s4_tabs_loaded s4_rot_summed s4_turned_taken s4_nat_summed s4_nat_v s4_nat_a s4_stepped "
        "s4_keys_ready s4_gates_ready s4_scratch_stored s4_gates_loaded s4_staged_clear s4_queries_rotated")
    HN = NAT_COLS // 2
    T9 = TILES + 1
    with ExitStack() as st:
        w = sb(nc, st, "w_nat", [P, KD, NAT_COLS])
        tables = kvn[:, 0:3, :].rearrange("p t n -> p (t n)")
        cos_t, sin_t = tables[:, 0:ROWS], tables[:, ROWS:2 * ROWS]
        rot = sb(nc, st, "rot_m", [P, P])
        rope = sb(nc, st, "rope_nat", [P, 2, T9, HALF])
        tmp = sb(nc, st, "rope_tmp", [P, 4, T9 * N_KV * HALF])
        qtmp = sb(nc, st, "q_tmp", [P, 2, GR])
        block = st.enter_context(nc.Block())

        def rows_of(t):
            return min(P, ROWS - t * P)

        @block.sync
        def _(sp):
            sp.dma_start(rot[:, :], d["rot"]).then_inc(tabs_loaded, 16)
            sp.dma_start(cos_t, d["cos_t"]).then_inc(tabs_loaded, 16)
            sp.dma_start(sin_t, d["sin_t"]).then_inc(tabs_loaded, 16)
            sp.dma_start(rope[:, :, :, :].rearrange("p a t n -> p (a t n)"), d["rope_nat"]).then_inc(tabs_loaded, 16)
            sp.dma_start(w[:, :, :], d["w_in"][0, :, NAT_COL:NAT_COL + NAT_COLS].rearrange("(k p) n -> p k n", p=P)
                         ).then_inc(w_loaded, 16)
            sp.wait_ge(nat_v, T9)
            sp.wait_ge(nat_a, T9)
            flat = {n: d[n].rearrange("x b s c h d -> (x b s) (c h d)") for n in
                    ("new_cmp_prompt", "new_cmp_sample", "new_sel_prompt", "new_sel_sample", "new_win_prompt")}
            W2 = 2 * KV_WIDTH
            sp.dma_start(flat["new_cmp_prompt"].rearrange("(t p) n -> p t n", p=P), kvn[:, 0:TILES, 0:W2]).then_inc(kv_stored, 16)
            sp.dma_start(flat["new_cmp_sample"], kvn[0:RS, TILES, 0:W2]).then_inc(kv_stored, 16)
            sp.wait_ge(keys_ready, 1)
            sp.dma_start(flat["new_sel_prompt"].rearrange("(t p) n -> p t n", p=P), kvn[:, 0:TILES, W2:2 * W2]).then_inc(kv_stored, 16)
            sp.dma_start(flat["new_sel_sample"], kvn[0:RS, TILES, W2:2 * W2]).then_inc(kv_stored, 16)
            sp.dma_start(flat["new_win_prompt"].rearrange("(t p) n -> p t n", p=P),
                         kvn[:, TILES - WINDOW // P:TILES, 2 * W2:3 * W2]).then_inc(kv_stored, 16)
            for b in range(DEC_BATCH):
                sp.dma_start(d["new_win_sample"][0, b].rearrange("s c h d -> s (c h d)")[WINDOW - DEC_SEQ:WINDOW, :],
                             kvn[b * DEC_SEQ:(b + 1) * DEC_SEQ, TILES, 2 * W2:3 * W2]).then_inc(kv_stored, 16)
            sp.wait_ge(kv_stored, 16 * (5 + DEC_BATCH))

        @block.gpsimd
        def _(pool):
            pool.wait_ge(gates_ready, T9)
            scratch = d["gate_scratch"]
            pool.dma_start(scratch, gates[0:RS, TILES, :]).then_inc(scratch_stored, 16)
            pool.wait_ge(scratch_stored, 16)
            for g in range(SG):
                for b in range(BT):
                    for h in range(N_KV):
                        r0 = b * QR + h * DEC_SEQ * GROUP
                        row = (g * BT + b) * DEC_SEQ
                        src = scratch[row:row + DEC_SEQ, :].rearrange("s (br k g) -> k s g br", br=3, k=N_KV)[h]
                        for s in range(DEC_SEQ):
                            pool.dma_start(gate_rows[r0 + s * GROUP:r0 + (s + 1) * GROUP, g, :], src[s],
                                           allow_slow_non_contiguous=True).then_inc(gates_loaded, 16)
            pool.wait_ge(gates_loaded, 16 * SG * BT * N_KV * DEC_SEQ)

        @block.tensor
        def _(pe):
            pe.wait_ge(tabs_loaded, 64)
            step = 0
            for c in range(KA):
                for g in range(NG):
                    if step >= 4:
                        pe.wait_ge(turned_taken, step - 3)
                    pe.matmul(ps[4 + step % 4][:, 0:GR], lhsT=rot[:, :], rhs=qT[:, c, g * GR:(g + 1) * GR], start=True,
                              stop=True).then_inc(rot_summed, 1)
                    step += 1
            pe.wait_ge(w_loaded, 16)
            for t in range(T9):
                n = rows_of(t)
                if t >= 2:
                    pe.wait_ge(nat_v, t - 1)
                    pe.wait_ge(nat_a, t - 1)
                for h in range(2):
                    for c in range(KD):
                        m = pe.matmul(ps[2 * (t % 2) + h][0:n, 0:HN], lhsT=hT[:, c, t * P:t * P + n],
                                      rhs=w[:, c, h * HN:(h + 1) * HN], start=(c == 0), stop=(c == KD - 1))
                m.then_inc(nat_summed, 1)
            pe.wait_ge(keys_ready, 1)
            for kind in range(2):
                col = 2 * KV_WIDTH * (1 + kind)
                for half in range(3):
                    pe.wait_ge(turned_taken, step - 3)
                    tiles = range(4 * half, min(4 * half + 4, T9))
                    for j, t in enumerate(tiles):
                        n = rows_of(t)
                        m = pe.transpose(ps[4 + step % 4][:, j * P:j * P + n], kvn[0:n, t, col:col + KV_WIDTH], ident[0:n, 0:n])
                    m.then_inc(rot_summed, 1)
                    step += 1

        @block.scalar
        def _(act):
            for t in range(T9):
                n = rows_of(t)
                act.wait_ge(nat_summed, t + 1)
                bank = ps[2 * (t % 2) + 1]
                if t == 0:
                    act.wait_ge(queries_rotated, 1)
                if t == TILES:
                    act.wait_ge(staged_clear, 2)
                act.activation(gates[0:n, t, :], bank[0:n, KV_COLS - HN:HN], ACT.Sigmoid).then_inc(gates_ready, 1)
                act.activation(kvn[0:n, t, HN:KV_COLS], bank[0:n, 0:KV_COLS - HN], ACT.Copy).then_inc(nat_a, 1)
            act.wait_ge(gates_ready, T9)

        @block.vector
        def _(dve):
            s = Steps(dve, stepped)
            dve.memset(kvn[:, TILES, :], 0.0).then_inc(staged_clear, 1)
            dve.memset(gates[:, TILES, :], 0.0).then_inc(staged_clear, 1)
            s.done(dve.memset(q_plain[:, :, :], 0.0))
            s.done(dve.memset(q_rot[:, :, :], 0.0))
            dve.wait_ge(tabs_loaded, 64)
            step = 0
            for c in range(KA):
                for g in range(NG):
                    cols = slice(g * GR, (g + 1) * GR)
                    s.done(dve.tensor_tensor(qR[:, c, cols], qT[:, c, cols], cos_t[:, cols], ALU.mult))
                    dve.wait_ge(rot_summed, step + 1)
                    dve.tensor_tensor(qtmp[:, step % 2, :], ps[4 + step % 4][:, 0:GR], sin_t[:, cols], ALU.mult
                                      ).then_inc(turned_taken, 1)
                    dve.wait_ge(turned_taken, step + 1)
                    s.fence()
                    s.done(dve.tensor_tensor(qR[:, c, cols], qR[:, c, cols], qtmp[:, step % 2, :], ALU.add))
                    step += 1
            s.fence()
            dve.sem_inc(queries_rotated, 1)
            for b in range(BT):
                for h in range(N_KV):
                    part = slice(h * HEAD_DIM, (h + 1) * HEAD_DIM)
                    c0 = b * QR + h * DEC_SEQ * GROUP
                    for dst, src in ((q_plain, qT), (q_rot, qR)):
                        for g in range(SG):
                            row = SEQ + (g * BT + b) * DEC_SEQ
                            s.done(dve.tensor_copy(
                                dst[part, g * BT + b, c0:c0 + DEC_SEQ * GROUP].rearrange("p (s g) -> p s g", g=GROUP),
                                src[part, :, row:row + DEC_SEQ].rearrange("p g s -> p s g")))
            dve.wait_ge(staged_clear, 2)
            for t in range(T9):
                n = rows_of(t)
                dve.wait_ge(nat_summed, t + 1)
                dve.tensor_copy(kvn[0:n, t, 0:HN], ps[2 * (t % 2)][0:n, 0:HN]).then_inc(nat_v, 1)
            dve.wait_ge(nat_v, T9)
            dve.wait_ge(nat_a, T9)
            cos, sin = bcast(rope[:, 0, :, :], 2, N_KV), bcast(rope[:, 1, :, :], 2, N_KV)
            T = [tmp[:, j, :].rearrange("p (t h n) -> p t h n", h=N_KV, n=HALF) for j in range(4)]
            for kind in range(2):
                col = 2 * KV_WIDTH * (1 + kind)
                heads = kvn[:, :, col:col + KV_WIDTH].rearrange("p t (h n) -> p t h n", h=N_KV)
                x1, x2 = heads[:, :, :, 0:HALF], heads[:, :, :, HALF:ROT_DIM]
                s.done(dve.tensor_tensor(T[0], x1, cos, ALU.mult))
                s.done(dve.tensor_tensor(T[1], x2, sin, ALU.mult))
                s.done(dve.tensor_tensor(T[2], x1, sin, ALU.mult))
                s.then(dve.tensor_tensor(T[3], x2, cos, ALU.mult))
                s.done(dve.tensor_tensor(x1, T[0], T[1], ALU.subtract))
                s.then(dve.tensor_tensor(x2, T[2], T[3], ALU.add))
            dve.sem_inc(keys_ready, 1)
            for kind in range(2):
                for half in range(3):
                    dve.wait_ge(rot_summed, step + 1)
                    n = min(4 * P, ROWS - half * 4 * P)
                    dve.tensor_copy(kT[:, kind, half * 4 * P:half * 4 * P + n], ps[4 + step % 4][:, 0:n]).then_inc(turned_taken, 1)
                    step += 1
                col = 2 * KV_WIDTH * (1 + kind)
                s.done(dve.tensor_copy(v_new[:, kind, :], kvn[0:RS, TILES, col + KV_WIDTH:col + 2 * KV_WIDTH]))
                dve.wait_ge(turned_taken, step)
                s.done(dve.tensor_copy(k_new[:, kind, :], kT[:, kind, SEQ:ROWS]))
            s.fence()


def compress(k, ck_s, cv_s, ck_p, cv_p, ident, page_rows, space):
    nc, ps, d = k.nc, k.ps, k.dram
    (w1_loaded0, w1_loaded1, rows_loaded00, rows_loaded01, rows_loaded10, rows_loaded11, p_loaded0, p_loaded1, multiplied,
     turned, copied_v, copied_a, zero_set, all_summed, bias_ready, hid_ready, w2_loaded, w2_clear, out_summed,
     out_taken) = k.sems(
        " ".join("s5_" + n for n in ("w1_loaded0 w1_loaded1 rows_loaded00 rows_loaded01 rows_loaded10 rows_loaded11 p_loaded0 "
                                     "p_loaded1 multiplied turned copied_v copied_a zero_set all_summed bias_ready hid_ready "
                                     "w2_loaded w2_clear out_summed out_taken").split()))
    w1_loaded, p_loaded = [w1_loaded0, w1_loaded1], [p_loaded0, p_loaded1]
    rows_loaded = [[rows_loaded00, rows_loaded01], [rows_loaded10, rows_loaded11]]
    NPB = NBP + 1
    counts = [P, P, NPB]
    LP = L_CHUNK // 2
    STEPS = (SG + 1) * LP
    TRIPS = N_LCH // 2
    AHEAD = STEPS + 1
    cmp_rows = d["cache_cmp_kv"][0].rearrange("a (r l) c h d -> (a r) (l c h d)", l=L_CHUNK)
    prompt_rows = d["new_cmp_prompt"][0, 0].rearrange("(n l) c h d -> n (l c h d)", l=BLOCK)
    w1_view = d["cmp_w1"][0].rearrange("c (l m) d f -> (m d) c l f", m=2)
    with ExitStack() as st:
        w1 = [sb(nc, st, f"w1_{p}", [P, 2, LP, CMP_HIDDEN]) for p in range(2)]
        rows = [[space[:, (2 * g + p) * ROWF:(2 * g + p + 1) * ROWF] for p in range(2)] for g in range(SG)]
        prows = [sb(nc, st, f"prompt_rows{p}", [NPB, ROWF]) for p in range(2)]
        zt = [sb(nc, st, f"zt{p}", [P, 2, 2 * P]) for p in range(2)]
        zero = sb(nc, st, "zero", [P, 512])
        bias = sb(nc, st, "cmp_bias", [P, 2])
        hid = sb(nc, st, "hid", [P, 2, SG, 2 * P])
        hid_p = sb(nc, st, "hid_p", [P, 2, 2 * NPB])
        w2k = sb(nc, st, "w2k", [P, N_KV, P])
        w2v = sb(nc, st, "w2v", [P, HEAD_DIM])
        block = st.enter_context(nc.Block())

        def turn_of(v):
            return v // LP, v % LP

        def source(v, p):
            g, l = turn_of(v)
            n = counts[g]
            buf = (rows[g][p] if g < SG else prows[p][:, :])[0:n, :].rearrange("p (l c n) -> p l c n", c=2, n=KV_WIDTH)
            return buf[:, 2 * l:2 * l + 2], n

        def sums(g, c):
            n = 2 * counts[g]
            return ps[c][:, g * n:(g + 1) * n] if g < SG else ps[2][:, c * n:(c + 1) * n]

        @block.sync
        def _(sp):
            for j in range(N_KV):
                sp.dma_start(w2v[:, :], d["cmp_w2"][0, 1]).then_inc(w2_loaded, 16) if j == 0 else None
                if j == 0:
                    sp.wait_ge(w2_clear, 1)
                sp.dma_start(w2k[:, j, j * HEAD_DIM:(j + 1) * HEAD_DIM], d["cmp_w2"][0, 0]).then_inc(w2_loaded, 16)
            pe_enc = d["cmp_pe"][0].rearrange("c l d -> l c d")
            with sp.Fori(0, TRIPS) as i:
                for p in range(2):
                    sp.wait_ge(multiplied, i * (2 * STEPS) + (p - 1) * STEPS + AHEAD)
                    for c in range(2):
                        sp.dma_start(w1[p][:, c, :, :], w1_view[:, c, ds(i * (2 * LP) + p * LP, LP), :]).then_inc(w1_loaded[p], 16)
                    sp.dma_start(prows[p][0:NBP, :], prompt_rows[:, ds(i * (2 * ROWF) + p * ROWF, ROWF)]).then_inc(p_loaded[p], 16)
                    for h in range(N_KV):
                        sp.dma_start(prows[p][NBP:NPB, :].rearrange("p (l c h d) -> p l c h d", c=2, h=N_KV, d=HEAD_DIM)[:, :, :, h],
                                     pe_enc[ds(i * (2 * L_CHUNK) + p * L_CHUNK, L_CHUNK)].unsqueeze(0)).then_inc(p_loaded[p], 16)

        @block.gpsimd
        def _(pool):
            pool.memset(zero[:, :], 0.0).then_inc(zero_set, 1)
            pool.memset(w2k[:, :, :], 0.0).then_inc(w2_clear, 1)
            for n in range(N_LCH):
                p = n % 2
                if n >= 2:
                    pool.wait_ge(multiplied, (n - 1) * STEPS + AHEAD)
                for g in range(SG):
                    pool.indirect_dma_start(rows[g][p], None, cmp_rows,
                                            bass.IndirectOffsetOnAxis(ap=page_rows[:, g, n:n + 1], axis=0)
                                            ).then_inc(rows_loaded[g][p], 16)

        @block.tensor
        def _(pe):
            pe.wait_ge(zero_set, 1)
            for b in range(3):
                pe.matmul(ps[b][:, :], lhsT=zero[:, 0:P], rhs=zero[:, :], start=True, stop=False, skip_group_check=True)
            pe.sem_inc(multiplied, AHEAD)
            with pe.Fori(0, TRIPS) as i:
                for p in range(2):
                    def turn(v):
                        at = p * STEPS + v
                        src, n = source(v, p)
                        if v == 0:
                            pe.wait_ge(w1_loaded[p], i * 32 + 32)
                            pe.wait_ge(rows_loaded[0][p], i * 16 + 16)
                        if v == LP:
                            pe.wait_ge(rows_loaded[1][p], i * 16 + 16)
                        for e in range(2):
                            for c in range(2):
                                m = pe.transpose(ps[4 + 2 * (at % 2) + e][:, c * n:(c + 1) * n], src[:, e, c, :], ident[0:n, 0:n])
                        m.then_inc(turned, 1)

                    def multiply(v):
                        at = p * STEPS + v
                        g, l = turn_of(v)
                        n = 2 * counts[g]
                        if v == 2 * LP - 2:
                            pe.wait_ge(p_loaded[p], i * 48 + 48)
                        pe.wait_ge(copied_v, i * (4 * STEPS) + 2 * at + 2)
                        pe.wait_ge(copied_a, i * (4 * STEPS) + 2 * at + 2)
                        for c in range(2):
                            m = pe.matmul(sums(g, c), lhsT=w1[p][:, c, l, :], rhs=zt[at % 2][:, c, 0:n],
                                          start=False, stop=False, skip_group_check=True)
                        return m
                    turn(0)
                    for v in range(STEPS):
                        if v + 1 < STEPS:
                            turn(v + 1)
                        multiply(v).then_inc(multiplied, 1)
            for b in range(3):
                m = pe.matmul(ps[b][:, :], lhsT=zero[:, 0:P], rhs=zero[:, :], start=False, stop=True, skip_group_check=True)
            m.then_inc(all_summed, 1)
            pe.wait_ge(w2_loaded, 48)
            pe.wait_ge(hid_ready, 6)
            for g in range(SG):
                for h in range(N_KV):
                    pe.matmul(ps[6][:, g * P:(g + 1) * P], lhsT=w2k[:, h, :], rhs=hid[:, 0, g, h * P:(h + 1) * P],
                              start=(h == 0), stop=(h == 1))
            for h in range(N_KV):
                pe.matmul(ps[6][:, 2 * P:2 * P + NBP], lhsT=w2k[:, h, :], rhs=hid_p[:, 0, h * NPB:h * NPB + NBP],
                          start=(h == 0), stop=(h == 1))
            for h in range(N_KV):
                m = pe.matmul(ps[7][0:NBP, h * HEAD_DIM:(h + 1) * HEAD_DIM], lhsT=hid_p[:, 1, h * NPB:h * NPB + NBP], rhs=w2v[:, :],
                              start=True, stop=True)
            m.then_inc(out_summed, 1)
            for b in range(DEC_BATCH):
                g, r = b // BT, (b % BT) * NBS
                for h in range(N_KV):
                    m = pe.matmul(ps[g][0:NBS, (b % BT) * KV_WIDTH + h * HEAD_DIM:(b % BT) * KV_WIDTH + (h + 1) * HEAD_DIM],
                                  lhsT=hid[:, 1, g, h * P + r:h * P + r + NBS], rhs=w2v[:, :], start=True, stop=True)
                if b % BT == BT - 1:
                    m.then_inc(out_summed, 1)

        def copy_turn(eng, copy, copied, e, i, p, v):
            at = p * STEPS + v
            n = counts[turn_of(v)[0]]
            eng.wait_ge(turned, i * (2 * STEPS) + at + 1)
            eng.wait_ge(multiplied, i * (2 * STEPS) + at - 1 + AHEAD)
            for h in range(N_KV):
                copy(zt[at % 2][e * HEAD_DIM:(e + 1) * HEAD_DIM, :, h * n:(h + 1) * n],
                     ps[4 + 2 * (at % 2) + e][h * HEAD_DIM:(h + 1) * HEAD_DIM, 0:2 * n].rearrange("p (c n) -> p c n", c=2)
                     ).then_inc(copied, 1)

        @block.scalar
        def _(act):
            with act.Fori(0, TRIPS) as i:
                for p in range(2):
                    for v in range(STEPS):
                        copy_turn(act, lambda o, x: act.activation(o, x, ACT.Copy), copied_a, 1, i, p, v)
            act.wait_ge(bias_ready, 1)
            for c in range(2):
                for g in range(SG + 1):
                    dst = hid[:, c, g, :] if g < SG else hid_p[:, c, :]
                    act.activation(dst, sums(g, c), ACT.Gelu_apprx_tanh, bias=bias[:, c:c + 1]
                                   ).then_inc(hid_ready, 1)

        @block.vector
        def _(dve):
            with dve.Fori(0, TRIPS) as i:
                for p in range(2):
                    for v in range(STEPS):
                        copy_turn(dve, dve.tensor_copy, copied_v, 0, i, p, v)
            dve.wait_ge(all_summed, 1)
            for c in range(2):
                m = dve.tensor_copy(bias[:, c:c + 1], sums(SG, c)[:, NBP:NPB])
            m.then_inc(bias_ready, 1)
            dve.wait_ge(out_summed, 1)
            dve.tensor_copy(ck_s[:, :], ps[6][:, 0:SG * P]).then_inc(out_taken, 1)
            dve.tensor_copy(ck_p[:, :], ps[6][:, SG * P:SG * P + NBP]).then_inc(out_taken, 1)
            dve.tensor_copy(cv_p[:, :], ps[7][0:NBP, 0:KV_WIDTH]).then_inc(out_taken, 1)
            for g in range(SG):
                dve.wait_ge(out_summed, g + 2)
                dve.tensor_copy(cv_s[:, g * BT:(g + 1) * BT, :], ps[g][0:NBS, :].rearrange("p (b n) -> p b n", b=BT)
                                ).then_inc(out_taken, 1)
            dve.wait_ge(out_taken, 5)


def prompt_attention(k, qT, qR, kvn, kT, gates, ck_p, cv_p, attn, ident):
    nc, ps, psum, d = k.nc, k.ps, k.psum, k.dram
    (masks_loaded, v_clear, v_spread, staged, scored, max_ready, probs_ready, turned0, turned1, copied0, copied1,
     out_summed, merged, stepped, cmp_scored, cmp_shifted, cmp_exp, cmp_probs, cmp_turned, cmp_copied, cmp_summed,
     cmp_merged, merged_half) = k.sems(" ".join("s6_" + n for n in (
         "masks_loaded v_clear v_spread staged scored max_ready probs_ready turned0 turned1 copied0 copied1 out_summed "
         "merged stepped cmp_scored cmp_shifted cmp_exp cmp_probs cmp_turned cmp_copied cmp_summed cmp_merged merged_half").split()))
    WT = WINDOW // P
    units = [(t, h, br) for t in range(TILES) for h in range(N_KV) for br in (1, 2)]
    tiles_of = [list(range(t + 1)) if br == 1 else list(range(max(0, t - WT), t + 1)) for t, h, br in units]
    U = len(units)
    second = [len(x) > 4 for x in tiles_of]
    upto = [sum(second[:u + 1]) for u in range(U)]
    C1 = upto[-1]
    HT = TILES // 2
    with ExitStack() as st:
        diag = sb(nc, st, "mask_diag", [P, P])
        tail = sb(nc, st, "mask_tail", [P, P])
        cmask = sb(nc, st, "mask_cmp", [P, TILES, NBP])
        vx = sb(nc, st, "v_spread", [P, HT * N_KV, HEAD_DIM])
        Q = [sb(nc, st, f"q_rot{h}", [P, SEQ]) for h in range(N_KV)]
        QC = [sb(nc, st, f"q_plain{h}", [P, SEQ]) for h in range(N_KV)]
        probs = [sb(nc, st, f"probs{p}", [P, SEQ]) for p in range(2)]
        pT = [sb(nc, st, f"probsT{p}", [P, SEQ]) for p in range(2)]
        nmax = sb(nc, st, "neg_max", [P, 4])
        den = sb(nc, st, "den", [P, 4])
        coef = sb(nc, st, "coef", [P, 4])
        gsel = sb(nc, st, "gate_pair", [P, TILES, 3, N_KV])
        cs = sb(nc, st, "cmp_probs", [P, TILES, N_KV, NBP])
        cst = sb(nc, st, "cmp_stat", [P, 2, TILES, N_KV])
        cT = pT[1][:, SEQ - 2 * P:SEQ].rearrange("p (a n) -> p a n", a=2)
        block = st.enter_context(nc.Block())

        @block.sync
        def _(sp):
            sp.dma_start(diag[:, :], d["mask_diag"]).then_inc(masks_loaded, 16)
            sp.dma_start(tail[:, :], d["mask_tail"]).then_inc(masks_loaded, 16)
            sp.dma_start(cmask[:, :, :].rearrange("p t n -> p (t n)"), d["mask_cmp"]).then_inc(masks_loaded, 16)
            sp.wait_ge(v_clear, 1)
            for j in range(HT * N_KV):
                sp.dma_start(vx[j * NBP:(j + 1) * NBP, j, :], cv_p[:, (j % N_KV) * HEAD_DIM:(j % N_KV + 1) * HEAD_DIM]
                             ).then_inc(v_spread, 16)

        @block.gpsimd
        def _(pool):
            pool.memset(vx[:, :, :], 0.0).then_inc(v_clear, 1)

        @block.tensor
        def _(pe):
            pe.wait_ge(masks_loaded, 48)
            pe.wait_ge(v_spread, 16 * HT * N_KV)
            with pe.Fori(0, KA) as i:
                def qk(u):
                    t, h, br = units[u]
                    if u == 0:
                        pe.wait_ge(staged, i * 4 + 4)
                    if u >= 2:
                        pe.wait_ge(probs_ready, i * U + u - 1)
                    base, k0, n = (u % 2) * 1024, tiles_of[u][0] * P, len(tiles_of[u]) * P
                    q = Q[h][:, t * P:(t + 1) * P]
                    masks = {n - P: diag}
                    if br == 2 and t >= WT:
                        masks[0] = tail
                    for a in range(0, n, 512):
                        b = min(a + 512, n)
                        own = [(x, m) for x, m in masks.items() if a <= x < b]
                        m = pe.matmul(psum[:, base + a:base + b], lhsT=q, rhs=kT[:, br - 1, k0 + a:k0 + b],
                                      start=True, stop=not own, skip_group_check=True)
                        for x, mask in own:
                            m = pe.matmul(psum[:, base + x:base + x + P], lhsT=ident[:, :], rhs=mask[:, :],
                                          start=False, stop=(x, mask) == own[-1], skip_group_check=True)
                    m.then_inc(scored, 1)

                def turn(u):
                    pe.wait_ge(probs_ready, i * U + u + 1)
                    n = len(tiles_of[u])
                    if u >= 1:
                        pe.wait_ge(copied0, i * U + u)
                    for j in range(min(n, 4)):
                        m = pe.transpose(ps[4][:, j * P:(j + 1) * P], probs[u % 2][:, j * P:(j + 1) * P], ident[:, :])
                    m.then_inc(turned0, 1)
                    if second[u]:
                        if upto[u] >= 2:
                            pe.wait_ge(copied1, i * C1 + upto[u] - 1)
                        for j in range(4, n):
                            m = pe.transpose(ps[5][:, (j - 4) * P:(j - 3) * P], probs[u % 2][:, j * P:(j + 1) * P], ident[:, :])
                        m.then_inc(turned1, 1)

                def pv(u):
                    t, h, br = units[u]
                    pe.wait_ge(copied0, i * U + u + 1)
                    if second[u]:
                        pe.wait_ge(copied1, i * C1 + upto[u])
                    if u >= 2:
                        pe.wait_ge(merged, i * U + u - 1)
                    elif u == 0:
                        pe.wait_ge(cmp_merged, i * 2 + 2)
                    col = 2 * KV_WIDTH * br + KV_WIDTH + h * HEAD_DIM
                    for j, kt in enumerate(tiles_of[u]):
                        m = pe.matmul(ps[6 + u % 2][:, 0:HEAD_DIM], lhsT=pT[u % 2][:, j * P:(j + 1) * P],
                                      rhs=kvn[:, kt, col:col + HEAD_DIM], start=(j == 0), stop=(j == len(tiles_of[u]) - 1))
                    m.then_inc(out_summed, 1)

                pe.wait_ge(staged, i * 4 + 4)
                for t in range(TILES):
                    for h in range(N_KV):
                        m = pe.matmul(ps[6][:, (t * N_KV + h) * NBP:(t * N_KV + h + 1) * NBP], lhsT=QC[h][:, t * P:(t + 1) * P],
                                      rhs=ck_p[:, :], start=True, stop=True)
                m.then_inc(cmp_scored, 1)
                qk(0)
                qk(1)
                pe.wait_ge(cmp_probs, i + 1)
                flat = cs[:, :, :, :].rearrange("p t h n -> p (t h n)")
                for j in range(2):
                    m = pe.transpose(ps[7][:, j * P:(j + 1) * P], flat[:, j * P:(j + 1) * P], ident[:, :])
                m.then_inc(cmp_turned, 1)
                pe.wait_ge(cmp_copied, i + 1)
                for j in range(2):
                    pe.matmul(ps[6 + j][:, :], lhsT=cT[:, j, :], rhs=vx[:, :, :].rearrange("p j n -> p (j n)"), start=True,
                              stop=True).then_inc(cmp_summed, 1)
                for u in range(U + 2):
                    if 2 <= u < U:
                        qk(u)
                    if 1 <= u <= U:
                        turn(u - 1)
                    if u >= 2:
                        pv(u - 2)

        @block.scalar
        def _(act):
            with act.Fori(0, KA) as i:
                def exp(u):
                    act.wait_ge(max_ready, i * U + u + 1)
                    if u >= 2:
                        act.wait_ge(turned0, i * U + u - 1)
                        if second[u - 2]:
                            act.wait_ge(turned1, i * C1 + upto[u - 2])
                    n = len(tiles_of[u]) * P
                    if u >= 4:
                        act.wait_ge(merged, i * U + u - 3)
                    act.activation(probs[u % 2][:, 0:n], psum[:, (u % 2) * 1024:(u % 2) * 1024 + n], ACT.Exp,
                                   bias=nmax[:, u % 4:u % 4 + 1], accum_out=den[:, u % 4:u % 4 + 1]).then_inc(probs_ready, 1)

                def copy(u):
                    act.wait_ge(turned0, i * U + u + 1)
                    if u >= 2:
                        act.wait_ge(out_summed, i * U + u - 1)
                    n = min(len(tiles_of[u]), 4) * P
                    act.activation(pT[u % 2][:, 0:n], ps[4][:, 0:n], ACT.Copy).then_inc(copied0, 1)

                act.wait_ge(cmp_shifted, i + 1)
                act.activation(cs[:, :, :, :], cs[:, :, :, :], ACT.Exp).then_inc(cmp_exp, 1)
                for u in range(U + 1):
                    if u < U:
                        exp(u)
                    if u >= 1:
                        copy(u - 1)

        @block.vector
        def _(dve):
            s = Steps(dve, stepped)
            for h in range(N_KV):
                other = slice((1 - h) * HEAD_DIM, (2 - h) * HEAD_DIM)
                s.done(dve.memset(Q[h][other, :], 0.0))
                s.done(dve.memset(QC[h][other, :], 0.0))
            s.fence()
            dve.wait_ge(masks_loaded, 48)
            per = 2 + 7 + 2 * U
            with dve.Fori(0, KA) as i:
                s.enter(i, per)

                def top(u):
                    dve.wait_ge(scored, i * U + u + 1)
                    if u >= 4:
                        dve.wait_ge(probs_ready, i * U + u - 3)
                    n = len(tiles_of[u]) * P
                    dve.tensor_reduce(nmax[:, u % 4:u % 4 + 1], psum[:, (u % 2) * 1024:(u % 2) * 1024 + n], AX, ALU.max,
                                      negate=True).then_inc(max_ready, 1)

                def copy(u):
                    if second[u]:
                        dve.wait_ge(turned1, i * C1 + upto[u])
                        if u >= 2:
                            dve.wait_ge(out_summed, i * U + u - 1)
                        n = len(tiles_of[u]) * P
                        dve.tensor_copy(pT[u % 2][:, 512:n], ps[5][:, 0:n - 512]).then_inc(copied1, 1)

                def merge(u):
                    t, h, br = units[u]
                    j = slice(u % 4, u % 4 + 1)
                    dve.wait_ge(probs_ready, i * U + u + 1)
                    s.then(dve.reciprocal(coef[:, j], den[:, j]))
                    s.then(dve.tensor_tensor(coef[:, j], coef[:, j], gsel[:, t, br, h:h + 1], ALU.mult))
                    dve.wait_ge(out_summed, i * U + u + 1)
                    out = attn[:, t, ds(i * HEAD_DIM + h * GROUP * HEAD_DIM, HEAD_DIM)]
                    if u:
                        dve.wait_ge(merged, i * U + u)
                    dve.scalar_tensor_tensor(out, ps[6 + u % 2][:, 0:HEAD_DIM], coef[:, j], out, ALU.mult, ALU.add
                                             ).then_inc(merged, 1)

                for h in range(N_KV):
                    part = slice(h * HEAD_DIM, (h + 1) * HEAD_DIM)
                    for dst, src in ((Q, qR), (QC, qT)):
                        dve.tensor_scalar(dst[h][part, :], src[part, ds(i, 1), 0:SEQ].rearrange("p a n -> p (a n)"), SCALE,
                                          None, ALU.mult).then_inc(staged, 1)
                for h in range(N_KV):
                    s.done(dve.tensor_copy(gsel[:, :, :, h], gates[:, 0:TILES, :].rearrange("p t (b h) -> p t b h", b=3)[
                        :, :, :, ds(i + h * GROUP, 1)].rearrange("p t b h -> p t (b h)")))
                dve.wait_ge(cmp_scored, i + 1)
                scores = ps[6][:, 0:TILES * N_KV * NBP].rearrange("p (t h n) -> p t h n", h=N_KV, n=NBP)
                s.then(dve.tensor_tensor(cs[:, :, :, :], scores, bcast(cmask[:, :, :], 2, N_KV), ALU.add))
                s.then(dve.tensor_reduce(cst[:, 0, :, :], cs[:, :, :, :], AX, ALU.max))
                s.then(dve.tensor_scalar(cst[:, 0, :, :], cst[:, 0, :, :], -1e29, None, ALU.max))
                dve.tensor_tensor(cs[:, :, :, :], cs[:, :, :, :], bcast(cst[:, 0, :, :], 3, NBP), ALU.subtract
                                  ).then_inc(cmp_shifted, 1)
                dve.wait_ge(cmp_exp, i + 1)
                s.then(dve.tensor_reduce(cst[:, 1, :, :], cs[:, :, :, :], AX, ALU.add))
                s.then(dve.tensor_scalar(cst[:, 1, :, :], cst[:, 1, :, :], 1e-30, None, ALU.max))
                s.then(dve.reciprocal(cst[:, 1, :, :], cst[:, 1, :, :]))
                s.then(dve.tensor_tensor(cst[:, 1, :, :], cst[:, 1, :, :], gsel[:, :, 0, :], ALU.mult))
                dve.tensor_tensor(cs[:, :, :, :], cs[:, :, :, :], bcast(cst[:, 1, :, :], 3, NBP), ALU.mult
                                  ).then_inc(cmp_probs, 1)
                top(0)
                top(1)
                dve.wait_ge(cmp_turned, i + 1)
                dve.tensor_copy(cT[:, :, :], ps[7][:, 0:2 * P].rearrange("p (a n) -> p a n", a=2)).then_inc(cmp_copied, 1)
                for j in range(2):
                    dve.wait_ge(cmp_summed, i * 2 + j + 1)
                    for h in range(N_KV):
                        r = dve.tensor_copy(attn[:, j * HT:(j + 1) * HT, ds(i * HEAD_DIM + h * GROUP * HEAD_DIM, HEAD_DIM)],
                                            ps[6 + j][:, :].rearrange("p (t h n) -> p t h n", h=N_KV, n=HEAD_DIM)[:, :, h, :])
                        r.then_inc(cmp_merged if h else merged_half, 1)
                dve.wait_ge(cmp_merged, i * 2 + 2)
                dve.wait_ge(merged_half, i * 2 + 2)
                for u in range(U + 2):
                    if 2 <= u < U:
                        top(u)
                    if 1 <= u <= U:
                        copy(u - 1)
                    if u >= 2:
                        merge(u - 2)
                s.leave(KA)
            dve.wait_ge(merged, KA * U)


def sample_attention(k, q_plain, q_rot, k_new, v_new, gate_rows, ck_s, cv_s, page_parts, attn, ident, space, win_space,
                     score_space):
    nc, ps, d = k.nc, k.ps, k.dram
    (masks_loaded, kv_loaded, win_loaded, consts_set, misc_summed, misc_taken, k_turned, k_copied_v, k_copied_a, k_used,
     chunk_taken, exp_ready, exp_done, cmp_norm, probs_scaled, p_turned, p_copied_v, p_copied_a, p_used, opened, out_done,
     out_taken, out_stored, out_back, stepped) = k.sems(" ".join("s7_" + n for n in (
         "masks_loaded kv_loaded win_loaded consts_set misc_summed misc_taken k_turned k_copied_v k_copied_a k_used "
         "chunk_taken exp_ready exp_done cmp_norm probs_scaled p_turned p_copied_v p_copied_a p_used opened out_done "
         "out_taken out_stored out_back stepped").split()))
    NS, NW = PAST_LEN + RS, WINDOW + RS
    CH = 5
    UN = CH * BT
    TURNS = [("cmp", 0, 0, False), ("win", 0, 4, False), ("win", 4, 1, True)] + [
        ("sel", 4 * j, 4, False) for j in range(4)] + [("sel", 16, 1, True)]
    NT = len(TURNS)
    MISC = 4
    runs = d["cache_sel_kv"][0].rearrange("a (r t) c h d -> (a r) (t c h d)", t=TP)
    with ExitStack() as st:
        kv = sb(nc, st, "past_kv", [P, BT, TP, 2 * KV_WIDTH])
        wkv = win_space[:, 0:BT * WP * 2 * KV_WIDTH].rearrange("p (b t n) -> p b t n", b=BT, t=WP)
        kTs = [sb(nc, st, f"kTs{j}", [P, 512]) for j in range(4)]
        sel, win = score_space[:, 0:NS], score_space[:, NS:NS + NW]
        cmp_ = sb(nc, st, "cmp_scores", [P, NBS])
        cmp_g = sb(nc, st, "cmp_gated", [P, NBS])
        pT = [score_space[:, NS + NW + j * 4 * P:NS + NW + (j + 1) * 4 * P].rearrange("p (t n) -> p t n", t=4)
              for j in range(2)]
        zero = sb(nc, st, "s_zero", [P, QR])
        mask_new = sb(nc, st, "mask_new", [P, SG, RS])
        at = NS + NW + 2 * 4 * P
        mask_win = score_space[:, at:at + WP * P]
        square = NCAND * NCAND
        earlier = space[:, 0:square].rearrange("p (a b) -> p a b", a=NCAND)
        ranks = space[:, square:3 * square].rearrange("p (x a b) -> p x a b", x=2, a=NCAND)
        same = space[:, 3 * square:3 * square + P]
        out = space[0:QR, 3 * square + P:3 * square + P + 512]
        imp = sb(nc, st, "importance", [P, NBS])
        rank = sb(nc, st, "rank", [P, NCAND])
        unselected = sb(nc, st, "unselected", [P, NBS])
        stat = sb(nc, st, "s_stat", [P, 3, 3])
        block = st.enter_context(nc.Block())
        rows_of = {"cmp": cmp_g, "win": win, "sel": sel}

        def unit(w):
            return w // BT, w % BT

        def copied(eng, count_v, count_a, n, base):
            eng.wait_ge(count_a if n % 2 else count_v, base + n // 2 + 1)

        @block.sync
        def _(sp):
            for dst, name in ((mask_new[:, :, :].rearrange("p g n -> p (g n)"), "mask_new"), (mask_win[:, :], "mask_win"),
                              (same, "same_query"), (space[:, 0:square], "earlier")):
                sp.dma_start(dst, d[name]).then_inc(masks_loaded, 16)
            for g in range(SG):
                if g:
                    sp.wait_ge(p_used, NT * g)
                for b in range(BT):
                    sp.dma_start(wkv[:, b, :, :], d["state_win_kv"][0, g * BT + b].rearrange("(p t) c h d -> p t (c h d)", p=P)
                                 ).then_inc(win_loaded, 16)
                sp.wait_ge(out_taken, g + 1)
                sp.dma_start(d["attn_scratch"][g].rearrange("r b n -> r (b n)"), out).then_inc(out_stored, 16)
                sp.wait_ge(out_stored, 16 * (g + 1))
                for b in range(BT):
                    for h in range(N_KV):
                        src = d["attn_scratch"][g, h * DEC_SEQ * GROUP:(h + 1) * DEC_SEQ * GROUP, b,
                                                h * HEAD_DIM:(h + 1) * HEAD_DIM].rearrange("(s q) n -> s q n", q=GROUP)
                        row = (g * BT + b) * DEC_SEQ
                        sp.dma_start(attn[row:row + DEC_SEQ, TILES, h * GROUP * HEAD_DIM:(h + 1) * GROUP * HEAD_DIM].rearrange(
                            "s (q n) -> s q n", q=GROUP), src).then_inc(out_back, 16)
            sp.wait_ge(out_back, 16 * SG * BT * N_KV)

        @block.gpsimd
        def _(pool):
            pool.memset(zero[:, :], 0.0).then_inc(consts_set, 1)
            for g in range(SG):
                if g:
                    pool.wait_ge(p_used, NT * g)
                for b in range(BT):
                    n = g * BT + b
                    pool.indirect_dma_start(kv[:, b, :, :].rearrange("p t n -> p (t n)"), None, runs,
                                            bass.IndirectOffsetOnAxis(ap=page_parts[:, n:n + 1], axis=0)).then_inc(kv_loaded, 16)
            pool.wait_ge(kv_loaded, 16 * DEC_BATCH)

        @block.tensor
        def _(pe):
            pe.wait_ge(consts_set, 1)
            pe.wait_ge(masks_loaded, 64)
            for g in range(SG):
                def misc(m, product):
                    if g * MISC + m:
                        pe.wait_ge(misc_taken, g * MISC + m)
                    product().then_inc(misc_summed, 1)

                def over_samples(rhs_of, lhs, cols):
                    def product():
                        for b in range(BT):
                            r = pe.matmul(ps[7][:, 0:cols], lhsT=lhs[:, g * BT + b, :], rhs=rhs_of(b), start=(b == 0),
                                          stop=(b == BT - 1))
                        return r
                    return product

                def turn_k(w):
                    c, b = unit(w)
                    n = g * UN + w
                    if n >= 2:
                        copied(pe, k_copied_v, k_copied_a, n - 2, 0)
                    if w == 0:
                        pe.wait_ge(win_loaded, 16 * BT * (g + 1))
                    if w == BT:
                        pe.wait_ge(kv_loaded, 16 * BT * (g + 1))
                    src = wkv if c == 0 else kv
                    for j in range(4):
                        m = pe.transpose(ps[2 + n % 2][:, j * P:(j + 1) * P], src[:, b, (max(c - 1, 0) * 4 + j), 0:KV_WIDTH],
                                         ident[:, :])
                    m.then_inc(k_turned, 1)

                def score(w):
                    c, b = unit(w)
                    n = g * UN + w
                    at = g * CH + c
                    copied(pe, k_copied_v, k_copied_a, n, 0)
                    if b == 0 and at >= 2:
                        pe.wait_ge(chunk_taken, at - 1)
                    pe.matmul(ps[at % 2][:, :], lhsT=q_rot[:, g * BT + b, :], rhs=kTs[n % 4][:, :], start=(b == 0),
                              stop=(b == BT - 1)).then_inc(k_used, 1)

                def turn_p(j):
                    br, tile, count, new = TURNS[j]
                    n = g * NT + j
                    if n >= 2:
                        copied(pe, p_copied_v, p_copied_a, n - 2, 0)
                    if br == "cmp":
                        m = pe.transpose(ps[4 + n % 2][0:NBS, 0:P], cmp_g[:, :], ident[:, :])
                    elif new:
                        m = pe.transpose(ps[4 + n % 2][0:RS, 0:P], rows_of[br][:, tile * P:tile * P + RS], ident[:, :])
                    else:
                        for i in range(count):
                            m = pe.transpose(ps[4 + n % 2][:, i * P:(i + 1) * P], rows_of[br][:, (tile + i) * P:(tile + i + 1) * P],
                                             ident[:, :])
                    m.then_inc(p_turned, 1)

                def pv(j):
                    br, tile, count, new = TURNS[j]
                    n = g * NT + j
                    copied(pe, p_copied_v, p_copied_a, n, 0)
                    for i in range(max(count, 1)):
                        for b in range(BT):
                            col = slice(b * QR, (b + 1) * QR)
                            if br == "cmp":
                                lhs, rhs = pT[n % 2][0:NBS, 0, col], cv_s[:, g * BT + b, :]
                            elif new:
                                lhs, rhs = pT[n % 2][0:RS, 0, col], v_new[:, 0 if br == "sel" else 1, :]
                            else:
                                lhs = pT[n % 2][:, i, col]
                                rhs = (wkv if br == "win" else kv)[:, b, tile + i, KV_WIDTH:2 * KV_WIDTH]
                            m = pe.matmul(ps[6][0:QR, b * P:(b + 1) * P], lhsT=lhs, rhs=rhs, start=False, stop=False,
                                          skip_group_check=True)
                    m.then_inc(p_used, 1)

                def units(a, b):
                    turn_k(a)
                    for w in range(a, b):
                        if w + 1 < b:
                            turn_k(w + 1)
                        score(w)

                if g:
                    pe.wait_ge(out_taken, g)
                pe.matmul(ps[6][0:QR, :], lhsT=zero[:, :], rhs=mask_win[:, :], start=True, stop=False, skip_group_check=True
                          ).then_inc(opened, 1)
                misc(0, over_samples(lambda b: ck_s[:, (g * BT + b) * NBS:(g * BT + b + 1) * NBS], q_plain, NBS))
                units(0, BT)
                misc(1, over_samples(lambda b: k_new[:, 1, :], q_rot, RS))
                pe.wait_ge(cmp_norm, g + 1)
                misc(2, lambda: pe.matmul(ps[7][:, 0:NBS], lhsT=same, rhs=cmp_[:, :], start=True, stop=True))
                pe.wait_ge(probs_scaled, 3 * g + 1)
                turn_p(0)
                units(BT, UN)
                misc(3, over_samples(lambda b: k_new[:, 0, :], q_rot, RS))
                pv(0)
                pe.wait_ge(probs_scaled, 3 * g + 2)
                turn_p(1)
                turn_p(2)
                pv(1)
                pv(2)
                pe.wait_ge(probs_scaled, 3 * g + 3)
                turn_p(3)
                for j in range(3, NT):
                    if j + 1 < NT:
                        turn_p(j + 1)
                    pv(j)
                pe.matmul(ps[6][0:QR, :], lhsT=zero[:, :], rhs=mask_win[:, :], start=False, stop=True, skip_group_check=True
                          ).then_inc(out_done, 1)

        def copy_k(eng, copy, count, g, w):
            n = g * UN + w
            eng.wait_ge(k_turned, n + 1)
            if n >= 4:
                eng.wait_ge(k_used, n - 3)
            copy(kTs[n % 4][:, :], ps[2 + n % 2]).then_inc(count, 1)

        def copy_p(eng, copy, count, g, j):
            n = g * NT + j
            br, tile, c, new = TURNS[j]
            eng.wait_ge(p_turned, n + 1)
            if n >= 2:
                eng.wait_ge(p_used, n - 1)
            if br == "cmp" or new:
                copy(pT[n % 2][0:RS, 0, :], ps[4 + n % 2][0:RS, 0:P]).then_inc(count, 1)
            else:
                copy(pT[n % 2][:, :, :], ps[4 + n % 2].rearrange("p (a n) -> p a n", a=4)).then_inc(count, 1)

        @block.scalar
        def _(act):
            def copy(o, x):
                return act.activation(o, x, ACT.Copy)

            for g in range(SG):
                def exp(j, rows):
                    act.wait_ge(exp_ready, 3 * g + j + 1)
                    act.activation(rows, rows, ACT.Exp, bias=stat[:, j, 0:1], scale=SCALE, accum_out=stat[:, j, 1:2]
                                   ).then_inc(exp_done, 1)
                exp(0, cmp_[:, :])
                for w in (1, 3):
                    copy_k(act, copy, k_copied_a, g, w)
                exp(1, win[:, :])
                for w in range(BT + 1, UN, 2):
                    copy_k(act, copy, k_copied_a, g, w)
                exp(2, sel[:, :])
                for j in range(NT):
                    if j % 2:
                        copy_p(act, copy, p_copied_a, g, j)

        @block.vector
        def _(dve):
            s = Steps(dve, stepped)
            dve.wait_ge(masks_loaded, 64)
            for g in range(SG):
                def take_misc(m, op):
                    dve.wait_ge(misc_summed, g * MISC + m + 1)
                    op().then_inc(misc_taken, 1)
                    dve.wait_ge(misc_taken, g * MISC + m + 1)

                def top(j, rows):
                    s.then(dve.tensor_reduce(stat[:, j, 0:1], rows, AX, ALU.max))
                    dve.tensor_scalar(stat[:, j, 0:1], stat[:, j, 0:1], -SCALE, None, ALU.mult).then_inc(exp_ready, 1)

                def weight(j, gate, rows, dst):
                    s.then(dve.reciprocal(stat[:, j, 2:3], stat[:, j, 1:2]))
                    if j == 0:
                        dve.tensor_scalar(cmp_[:, :], cmp_[:, :], stat[:, j, 2:3], None, ALU.mult).then_inc(cmp_norm, 1)
                        dve.wait_ge(cmp_norm, g + 1)
                        dve.tensor_scalar(dst, rows, gate_rows[:, g, gate:gate + 1], None, ALU.mult).then_inc(probs_scaled, 1)
                    else:
                        s.then(dve.tensor_tensor(stat[:, j, 2:3], stat[:, j, 2:3], gate_rows[:, g, gate:gate + 1], ALU.mult))
                        dve.tensor_scalar(dst, rows, stat[:, j, 2:3], None, ALU.mult).then_inc(probs_scaled, 1)

                def take_chunk(c):
                    at = g * CH + c
                    dve.wait_ge(k_used, g * UN + BT * (c + 1))
                    bank = ps[at % 2]
                    if c == 0:
                        dve.tensor_tensor(win[:, 0:WINDOW], bank, mask_win[:, :], ALU.add).then_inc(chunk_taken, 1)
                    else:
                        lay = "p (t k r) -> p t k r"
                        dve.tensor_tensor(sel[:, (c - 1) * 512:c * 512].rearrange(lay, t=4, r=4), bank.rearrange(lay, t=4, r=4),
                                          bcast(bcast(unselected[:, :], 1, 4), 3, 4), ALU.add).then_inc(chunk_taken, 1)

                if g:
                    dve.wait_ge(p_turned, NT * g)
                take_misc(0, lambda: dve.tensor_copy(cmp_[:, :], ps[7][:, 0:NBS]))
                top(0, cmp_[:, :])
                dve.wait_ge(exp_done, 3 * g + 1)
                weight(0, 0, cmp_[:, :], cmp_g[:, :])
                for w in (0, 2):
                    copy_k(dve, dve.tensor_copy, k_copied_v, g, w)
                take_chunk(0)
                take_misc(1, lambda: dve.tensor_tensor(win[:, WINDOW:NW], ps[7][:, 0:RS], mask_new[:, g, :], ALU.add))
                dve.wait_ge(chunk_taken, g * CH + 1)
                top(1, win[:, :])
                take_misc(2, lambda: dve.tensor_copy(imp[:, :], ps[7][:, 0:NBS]))
                cand = imp[:, 1:1 + NCAND]
                a, b = bcast(cand, 1, NCAND), bcast(cand, 2, NCAND)
                s.done(dve.tensor_tensor(ranks[:, 0, :, :], a, b, ALU.is_gt))
                s.then(dve.tensor_tensor(ranks[:, 1, :, :], a, b, ALU.is_equal))
                s.then(dve.tensor_tensor(ranks[:, 1, :, :], ranks[:, 1, :, :], earlier[:, :, :], ALU.mult))
                s.then(dve.tensor_tensor(ranks[:, 0, :, :], ranks[:, 0, :, :], ranks[:, 1, :, :], ALU.add))
                s.done(dve.memset(unselected[:, :], 0.0))
                s.then(dve.tensor_reduce(rank[:, :], ranks[:, 0, :, :], AX, ALU.add))
                s.then(dve.tensor_scalar(unselected[:, 1:1 + NCAND], rank[:, :], float(NFREE), NEG, ALU.is_ge, ALU.mult))
                for w in range(BT, UN):
                    if w % 2 == 0:
                        copy_k(dve, dve.tensor_copy, k_copied_v, g, w)
                    if w % BT == BT - 1:
                        take_chunk(w // BT)
                take_misc(3, lambda: dve.tensor_tensor(sel[:, PAST_LEN:NS], ps[7][:, 0:RS], mask_new[:, g, :], ALU.add))
                dve.wait_ge(exp_done, 3 * g + 2)
                weight(1, 2, win[:, :], win[:, :])
                dve.wait_ge(chunk_taken, (g + 1) * CH)
                top(2, sel[:, :])
                dve.wait_ge(exp_done, 3 * g + 3)
                weight(2, 1, sel[:, :], sel[:, :])
                for j in range(0, NT, 2):
                    copy_p(dve, dve.tensor_copy, p_copied_v, g, j)
                dve.wait_ge(out_done, g + 1)
                dve.tensor_copy(out, ps[6][0:QR, :]).then_inc(out_taken, 1)


def turn_attention(k, attn, merged, ident):
    nc, ps = k.nc, k.ps
    turned, copied_v, copied_a = k.sems("s8_turned s8_copied_v s8_copied_a")
    with nc.Block() as block:
        @block.tensor
        def _(pe):
            for t in range(TILES + 1):
                n = min(P, ROWS - t * P)
                if t >= 4:
                    pe.wait_ge(copied_a if t % 2 else copied_v, (t - 4) // 2 + 1)
                for c in range(KA):
                    m = pe.transpose(ps[t % 4][:, c * P:c * P + n], attn[0:n, t, c * P:(c + 1) * P], ident[0:n, 0:n])
                m.then_inc(turned, 1)

        def copy(eng, op, count, odd):
            for t in range(odd, TILES + 1, 2):
                n = min(P, ROWS - t * P)
                eng.wait_ge(turned, t + 1)
                op(merged[:, KR:KR + KA, t * P:t * P + n], ps[t % 4].rearrange("p (c n) -> p c n", c=KA)[:, :, 0:n]
                   ).then_inc(count, 1)

        @block.vector
        def _(dve):
            copy(dve, dve.tensor_copy, copied_v, 0)

        @block.scalar
        def _(act):
            copy(act, lambda o, x: act.activation(o, x, ACT.Copy), copied_a, 1)


def add_gated(xT, gate):
    def take(dve, s, i, p, banks, tmp):
        for g in range(NG):
            (a, b), rest = prompt_split(g)
            o = xT[:, ds(i * 2 + p, 1), a:b].rearrange("p a n -> p (a n)")
            s.done(dve.scalar_tensor_tensor(o, banks[g][:, 0:b - a], gate[:, ds(i * 2 + p, 1), 0:1].rearrange("p a n -> p (a n)"),
                                            o, ALU.mult, ALU.add))
            if rest:
                r0 = rest[0] - g * GR
                s.then(dve.tensor_tensor(tmp.rearrange("p (b s) -> p b s", s=DEC_SEQ),
                                         banks[g][:, r0:GR].rearrange("p (b s) -> p b s", s=DEC_SEQ),
                                         bcast(gate[:, ds(i * 2 + p, 1), 1:COND].rearrange("p a n -> p (a n)"), 2, DEC_SEQ),
                                         ALU.mult))
                o = xT[:, ds(i * 2 + p, 1), rest[0]:rest[1]].rearrange("p a n -> p (a n)")
                r = dve.tensor_tensor(o, o, tmp, ALU.add)
        return r
    take.n_loads, take.per = 1, 2 * (NG + 1)
    return take


def ffn_up(k, hT, hidden, space):
    nc, ps, d = k.nc, k.ps, k.dram
    loaded0, loaded1, used0, used1, gate_summed, summed, silu_done, taken = k.sems(
        "s11_loaded0 s11_loaded1 s11_used0 s11_used1 s11_gate_summed s11_summed s11_silu_done s11_taken")
    loaded, used = [loaded0, loaded1], [used0, used1]
    TRIPS = KF // 2
    BODY = 2 * NG
    views = [d[n][0].rearrange("(k p) n -> p k n", p=P) for n in ("w_gate", "w_up")]
    with ExitStack() as st:
        w = [[sb(nc, st, f"w_ff{j}_{p}", [P, KD, P]) for j in range(2)] for p in range(2)]
        act_g = [space[:, g, 0:GR] for g in range(NG)]
        block = st.enter_context(nc.Block())

        @block.sync
        def _(sp):
            with sp.Fori(0, TRIPS) as i:
                for p in range(2):
                    sp.wait_ge(used[p], i + 1)
                    for j in range(2):
                        sp.dma_start(w[p][j][:, :, :], views[j][:, :, ds(i * (2 * P) + p * P, P)]).then_inc(loaded[p], 16)

        @block.tensor
        def _(pe):
            pe.sem_inc(used[0], 1)
            pe.sem_inc(used[1], 1)
            with pe.Fori(0, TRIPS) as i:
                for p in range(2):
                    pe.wait_ge(loaded[p], i * 32 + 32)
                    for g in range(NG):
                        pe.wait_ge(taken, i * BODY + p * NG + g + 1)
                        for j in range(2):
                            for c in range(KD):
                                m = pe.matmul(ps[2 * g + j][:, 0:GR], lhsT=w[p][j][:, c, :], rhs=hT[:, c, g * GR:(g + 1) * GR],
                                              start=(c == 0), stop=(c == KD - 1))
                            if not j:
                                m.then_inc(gate_summed, 1)
                            elif g < NG - 1:
                                m.then_inc(summed, 1)
                    m.then_inc(used[p], 1)

        @block.scalar
        def _(act):
            with act.Fori(0, TRIPS) as i:
                for p in range(2):
                    for g in range(NG):
                        n = p * NG + g
                        act.wait_ge(gate_summed, i * BODY + n + 1)
                        act.wait_ge(taken, i * BODY + n + 1)
                        act.activation(act_g[g], ps[2 * g][:, 0:GR], ACT.Silu).then_inc(silu_done, 1)

        @block.vector
        def _(dve):
            dve.sem_inc(taken, NG)
            with dve.Fori(0, TRIPS) as i:
                for p in range(2):
                    for g in range(NG):
                        n = p * NG + g
                        dve.wait_ge(silu_done, i * BODY + n + 1)
                        if g < NG - 1:
                            dve.wait_ge(summed, i * (2 * (NG - 1)) + p * (NG - 1) + g + 1)
                        else:
                            dve.wait_ge(used[p], i + 2)
                        dve.tensor_tensor(hidden[:, ds(i * 2 + p, 1), g * GR:(g + 1) * GR], act_g[g].unsqueeze(1),
                                          ps[2 * g + 1][:, 0:GR].unsqueeze(1), ALU.mult).then_inc(taken, 1)
            dve.wait_ge(taken, NG + TRIPS * BODY)


def store_rows(k, yT, ident, win_copied):
    nc, ps, d = k.nc, k.ps, k.dram
    turned, copied_v, copied_a, *rows_stored = k.sems("s14_turned s14_copied_v s14_copied_a s14_stored0 s14_stored1 s14_stored2 s14_stored3")
    with ExitStack() as st:
        y = [sb(nc, st, f"y{j}", [P, D_MODEL]) for j in range(4)]
        block = st.enter_context(nc.Block())

        @block.tensor
        def _(pe):
            for t in range(TILES + 1):
                n = min(P, ROWS - t * P)
                for h in range(2):
                    step = 2 * t + h
                    if step >= 8:
                        pe.wait_ge(copied_a if h else copied_v, (step - 8) // 2 + 1)
                    for c in range(4):
                        m = pe.transpose(ps[step % 8][0:n, c * P:(c + 1) * P], yT[:, 4 * h + c, t * P:t * P + n], ident[:, :])
                    m.then_inc(turned, 1)

        def copy(eng, op, count, h):
            for t in range(TILES + 1):
                n = min(P, ROWS - t * P)
                eng.wait_ge(turned, 2 * t + h + 1)
                if t >= 4:
                    eng.wait_ge(rows_stored[t % 4], 16 * (t // 4))
                op(y[t % 4][0:n, h * 512:(h + 1) * 512], ps[(2 * t + h) % 8][0:n, :]).then_inc(count, 1)

        @block.vector
        def _(dve):
            copy(dve, dve.tensor_copy, copied_v, 0)

        @block.scalar
        def _(act):
            copy(act, lambda o, x: act.activation(o, x, ACT.Copy), copied_a, 1)

        @block.sync
        def _(sp):
            for t in range(TILES + 1):
                n = min(P, ROWS - t * P)
                sp.wait_ge(copied_v, t + 1)
                sp.wait_ge(copied_a, t + 1)
                dst = d["y_prompt"][0, t * P:(t + 1) * P, :] if t < TILES else d["y_sample"].rearrange("b s n -> (b s) n")
                sp.dma_start(dst, y[t % 4][0:n, :]).then_inc(rows_stored[t % 4], 16)
            for j in range(4):
                sp.wait_ge(rows_stored[j], 16 * ((TILES - j) // 4 + 1))
            sp.wait_ge(win_copied, 16)


F32R = mybir.dt.float32r


def split_hi(act, hi, raw):
    return act.activation(hi, raw, ACT.Copy)


def split_lo(dve, lo, raw, hi):
    return dve.tensor_tensor(lo, raw, hi.bitcast(F32), ALU.subtract)


def three_passes(pe, out, w_hi, w_lo, x_hi, x_lo, first, last):
    pe.matmul(out, lhsT=w_hi, rhs=x_hi, start=first, stop=False)
    pe.matmul(out, lhsT=w_hi, rhs=x_lo, start=False, stop=False)
    return pe.matmul(out, lhsT=w_lo, rhs=x_hi, start=False, stop=last)


def project_split(k, tag, KC, H, loads, x_hi, x_lo, source, groups, take, space=None):
    nc, ps = k.nc, k.ps
    KB, NGR = KC // H, len(groups)
    trips, n_dma = sum(n for n, _, _ in loads), loads[0][1]
    names = "loaded0 loaded1 hi_done lo_done used x_hi_done x_lo_done taken0 taken1 stepped"
    loaded0, loaded1, hi_done, lo_done, used, x_hi_done, x_lo_done, taken0, taken1, stepped = k.sems(
        " ".join(f"{tag}_{n}" for n in names.split()))
    loaded, taken = [loaded0, loaded1], [taken0, taken1]
    BODY = 2 * H
    with ExitStack() as st:
        if space is None:
            space = sb(nc, st, f"{tag}_raw", [P, 2 * KB * P])
        raw = [space[:, q * KB * P:(q + 1) * KB * P].rearrange("p (k n) -> p k n", k=KB) for q in range(2)]
        w_hi = [sb(nc, st, f"{tag}_hi{q}", [P, KB, P], F32R) for q in range(2)]
        w_lo = [sb(nc, st, f"{tag}_lo{q}", [P, KB, P], F32R) for q in range(2)]
        tmp = sb(nc, st, f"{tag}_tmp", [P, 2, RS])
        block = st.enter_context(nc.Block())

        @block.sync
        def _(sp):
            start = 0
            for n_trips, _, load in loads:
                with sp.Fori(0, n_trips) as i:
                    for n in range(BODY):
                        sp.wait_ge(lo_done, i * BODY + start * BODY + n + 1)
                        for x in load(sp, i, n // H, n % H, raw[n % 2]):
                            x.then_inc(loaded[n % 2], 16)
                start += n_trips

        @block.tensor
        def _(pe):
            if source is not None:
                pe.wait_ge(x_lo_done, KC)
            pe.sem_inc(used, 2)
            with pe.Fori(0, trips) as i:
                for n in range(BODY):
                    p, h = n // H, n % H
                    pe.wait_ge(lo_done, i * BODY + n + 3)
                    if h == 0:
                        pe.wait_ge(taken[p], i + 1)
                    for j, (a, b) in enumerate(groups):
                        for c in range(KB):
                            cc = h * KB + c
                            m = three_passes(pe, ps[NGR * p + j][:, 0:b - a], w_hi[n % 2][:, c, :], w_lo[n % 2][:, c, :],
                                             x_hi[:, cc, a:b], x_lo[:, cc, a:b], cc == 0, cc == KC - 1)
                    m.then_inc(used, 1)

        @block.scalar
        def _(act):
            def hi(i, n):
                act.wait_ge(loaded[n % 2], (i * H + n // 2) * (16 * n_dma) + 16 * n_dma)
                act.wait_ge(used, i * BODY + n + 1)
                split_hi(act, w_hi[n % 2][:, :, :], raw[n % 2]).then_inc(hi_done, 1)
            if source is not None:
                for c in range(KC):
                    split_hi(act, x_hi[:, c, :], source(c)).then_inc(x_hi_done, 1)
            with act.Fori(0, trips) as i:
                for n in range(BODY):
                    hi(i, n)

        @block.vector
        def _(dve):
            s = Steps(dve, stepped)

            def lo(i, n):
                dve.wait_ge(hi_done, i * BODY + n + 1)
                split_lo(dve, w_lo[n % 2][:, :, :], raw[n % 2], w_hi[n % 2][:, :, :]).then_inc(lo_done, 1)

            def trip(i, last):
                s.enter(i, take.per) if not last else None
                for n in range(BODY):
                    if not (last and n == BODY - 1):
                        lo(i + (n + 1) // BODY, (n + 1) % BODY)
                    if n % H == H - 1:
                        p = n // H
                        dve.wait_ge(used, i * BODY + n + 3)
                        take(dve, s, i, p, [ps[NGR * p + j][:, 0:b - a] for j, (a, b) in enumerate(groups)], tmp[:, p, :]
                             ).then_inc(taken[p], 1)
                s.leave(trips - 1) if not last else None
            dve.sem_inc(lo_done, 2)
            dve.sem_inc(taken[0], 1)
            dve.sem_inc(taken[1], 1)
            if source is not None:
                for c in range(KC):
                    dve.wait_ge(x_hi_done, c + 1)
                    split_lo(dve, x_lo[:, c, :], source(c), x_hi[:, c, :]).then_inc(x_lo_done, 1)
            lo(0, 0)
            with dve.Fori(0, trips - 1) as i:
                trip(i, False)
            trip(trips - 1, True)
            for p in range(2):
                dve.wait_ge(taken[p], trips + 1)


def add_gated_rows(xT, gate, groups):
    def take(dve, s, i, p, banks, tmp):
        at = i * 2 + p
        for bank, (x0, x1) in zip(banks, groups):
            x2 = min(x1, SEQ)
            o = xT[:, ds(at, 1), x0:x2].rearrange("p a n -> p (a n)")
            r = dve.scalar_tensor_tensor(o, bank[:, 0:x2 - x0], gate[:, ds(at, 1), 0:1].rearrange("p a n -> p (a n)"), o,
                                         ALU.mult, ALU.add)
            if x1 > SEQ:
                s.done(r)
                s.then(dve.tensor_tensor(tmp.rearrange("p (b s) -> p b s", s=DEC_SEQ),
                                         bank[:, SEQ - x0:x1 - x0].rearrange("p (b s) -> p b s", s=DEC_SEQ),
                                         bcast(gate[:, ds(at, 1), 1:COND].rearrange("p a n -> p (a n)"), 2, DEC_SEQ), ALU.mult))
                o = xT[:, ds(at, 1), SEQ:x1].rearrange("p a n -> p (a n)")
                r = dve.tensor_tensor(o, o, tmp, ALU.add)
            elif (x0, x1) != groups[-1]:
                s.done(r)
        return r
    take.per = 2 * (len(groups) - 1 + (2 if groups[-1][1] > SEQ else 0))
    return take


def ffn_up_split(k, g, hT, hid_hi, hid_lo, space):
    nc, ps, d = k.nc, k.ps, k.dram
    (loaded0, loaded1, hi_done, lo_done, used, h_hi_done, h_lo_done, gate_summed, silu_done, mixed, hid_hi_done,
     hid_lo_done) = k.sems(" ".join(f"s11g{g}_{n}" for n in (
         "loaded0 loaded1 hi_done lo_done used h_hi_done h_lo_done gate_summed silu_done mixed hid_hi_done hid_lo_done").split()))
    loaded = [loaded0, loaded1]
    TRIPS = KF // 2
    rows = slice(g * GR, (g + 1) * GR)
    views = [d[n][0].rearrange("(k p) n -> p k n", p=P) for n in ("w_gate", "w_up")]
    with ExitStack() as st:
        h_hi = sb(nc, st, f"h_hi{g}", [P, KD, GR], F32R)
        h_lo = sb(nc, st, f"h_lo{g}", [P, KD, GR], F32R)
        raw = [space[:, p * 2 * KD * P:(p + 1) * 2 * KD * P].rearrange("p (j k n) -> p j k n", j=2, k=KD) for p in range(2)]
        w_hi = [sb(nc, st, f"ff_hi{g}_{p}", [P, 2, KD, P], F32R) for p in range(2)]
        w_lo = [sb(nc, st, f"ff_lo{g}_{p}", [P, 2, KD, P], F32R) for p in range(2)]
        silu = [sb(nc, st, f"silu{g}_{p}", [P, GR]) for p in range(2)]
        block = st.enter_context(nc.Block())

        @block.sync
        def _(sp):
            with sp.Fori(0, TRIPS) as i:
                for p in range(2):
                    sp.wait_ge(lo_done, i * 2 + p + 1)
                    for j in range(2):
                        sp.dma_start(raw[p][:, j], views[j][:, :, ds(i * (2 * P) + p * P, P)]).then_inc(loaded[p], 16)

        @block.tensor
        def _(pe):
            pe.wait_ge(h_lo_done, KD)
            pe.sem_inc(used, 2)
            with pe.Fori(0, TRIPS) as i:
                for p in range(2):
                    pe.wait_ge(lo_done, i * 2 + p + 3)
                    pe.wait_ge(mixed, i * 2 + p + 1)
                    for j in range(2):
                        for c in range(KD):
                            m = three_passes(pe, ps[2 * p + j][:, 0:GR], w_hi[p][:, j, c, :], w_lo[p][:, j, c, :],
                                             h_hi[:, c, :], h_lo[:, c, :], c == 0, c == KD - 1)
                        m.then_inc(used if j else gate_summed, 1)

        @block.scalar
        def _(act):
            def hi(i, p):
                act.wait_ge(loaded[p], i * 32 + 32)
                act.wait_ge(used, i * 2 + p + 1)
                split_hi(act, w_hi[p][:, :, :, :], raw[p]).then_inc(hi_done, 1)

            def trip(i, last):
                for p in range(2):
                    if not (last and p):
                        hi(i + p, 1 - p)
                    act.wait_ge(gate_summed, i * 2 + p + 1)
                    act.wait_ge(hid_lo_done, i * 2 + p + 1)
                    act.activation(silu[p][:, :], ps[2 * p][:, 0:GR], ACT.Silu).then_inc(silu_done, 1)
                    act.wait_ge(mixed, i * 2 + p + 3)
                    split_hi(act, hid_hi[:, ds(i * 2 + p, 1), :], silu[p][:, :].unsqueeze(1)).then_inc(hid_hi_done, 1)
            for c in range(KD):
                split_hi(act, h_hi[:, c, :], hT[:, c, rows]).then_inc(h_hi_done, 1)
            hi(0, 0)
            with act.Fori(0, TRIPS - 1) as i:
                trip(i, False)
            trip(TRIPS - 1, True)

        @block.vector
        def _(dve):
            def lo(i, p):
                dve.wait_ge(hi_done, i * 2 + p + 1)
                split_lo(dve, w_lo[p][:, :, :, :], raw[p], w_hi[p][:, :, :, :]).then_inc(lo_done, 1)

            def trip(i, last):
                for p in range(2):
                    if not (last and p):
                        lo(i + p, 1 - p)
                    dve.wait_ge(silu_done, i * 2 + p + 1)
                    dve.wait_ge(used, i * 2 + p + 3)
                    dve.tensor_tensor(silu[p][:, :], silu[p][:, :], ps[2 * p + 1][:, 0:GR], ALU.mult).then_inc(mixed, 1)
                    dve.wait_ge(hid_hi_done, i * 2 + p + 1)
                    split_lo(dve, hid_lo[:, ds(i * 2 + p, 1), :], silu[p][:, :].unsqueeze(1), hid_hi[:, ds(i * 2 + p, 1), :]
                             ).then_inc(hid_lo_done, 1)
            dve.sem_inc(lo_done, 2)
            dve.sem_inc(mixed, 2)
            dve.sem_inc(hid_lo_done, 2)
            for c in range(KD):
                dve.wait_ge(h_hi_done, c + 1)
                split_lo(dve, h_lo[:, c, :], hT[:, c, rows], h_hi[:, c, :]).then_inc(h_lo_done, 1)
            lo(0, 0)
            with dve.Fori(0, TRIPS - 1) as i:
                trip(i, False)
            trip(TRIPS - 1, True)
            dve.wait_ge(hid_lo_done, KF + 2)


def hymba_step(nc, dram):
    with ExitStack() as outer:
        k = Ctx(nc, outer, dram)
        ident = sb(nc, outer, "ident_m", [P, P])
        ones = sb(nc, outer, "ones_m", [P, P])
        eps = sb(nc, outer, "eps", [P, 1])
        vec = sb(nc, outer, "vec", [P, N_VEC])
        mods = sb(nc, outer, "mods", [P, 6 * KD, COND])
        state = sb(nc, outer, "state", [P, KR, 4 * DEC_BATCH])
        xT = sb(nc, outer, "xT", [P, KD, ROWS])
        cT = sb(nc, outer, "cT", [P, KD, COND])
        kv_stored, win_copied = k.sems("kv_stored win_copied")
        k.made = []
        dram["gate_scratch"] = nc.dram_tensor("gate_scratch", (RS, 3 * N_HEADS), F32, kind="Internal").ap()
        dram["attn_scratch"] = nc.dram_tensor("attn_scratch", (SG, QR, BT, KV_WIDTH), F32, kind="Internal").ap()
        V = {n: vec[:, a:b] for n, (a, b) in VEC.items()}

        def factor(j):
            return mods[:, j * KD:(j + 1) * KD, :]

        w_in = dram["w_in"][0].rearrange("(k p) n -> p k n", p=P)
        hT = sb(nc, outer, "hT", [P, KD, ROWS])
        mixers = ExitStack()
        streams = sb(nc, mixers, "streams", [P, 2 * KR + KA, ROWS])
        z_in, z_gate, qT = streams[:, 0:KR], streams[:, KR:2 * KR], streams[:, 2 * KR:]
        qR, merged = z_in, streams[:, KR:]
        samp = ExitStack()
        q_plain = sb(nc, samp, "q_plain", [P, DEC_BATCH, P])
        q_rot = sb(nc, samp, "q_rot", [P, DEC_BATCH, P])
        k_new = sb(nc, samp, "k_new", [P, 2, RS])
        v_new = sb(nc, samp, "v_new", [RS, 2, KV_WIDTH])
        gate_rows = sb(nc, samp, "gate_rows", [P, SG, 3])
        page_rows = sb(nc, samp, "page_rows", [P, SG, N_LCH], I32)
        page_parts = sb(nc, samp, "page_parts", [P, DEC_BATCH], I32)
        attn = hT[:, :, :].rearrange("p k r -> p (k r)")[:, 0:(TILES + 1) * ATTN_WIDTH].rearrange(
            "p (t n) -> p t n", t=TILES + 1)
        load_and_condition(k, xT, mods, vec, state, cT, ident, ones, eps, page_rows, page_parts, win_copied,
                           hT[:, :, :].rearrange("p k r -> p (k r)"))
        norm_rows(k, "n1", [list(range(KD))], lambda c: xT[:, c, :], lambda c: hT[:, c, :],
                  (V["ln1_g"], factor(1), lambda c: factor(0)[:, c, :], ones, eps))
        all_rows = [(g * GR, (g + 1) * GR) for g in range(NG)]
        KB = KD // 2

        def load_z(sp, i, p, h, w):
            at = i * (2 * P) + p * P
            return [sp.dma_start(w[:, q * KB // 2:(q + 1) * KB // 2, :],
                                 w_in[:, h * KB + q * KB // 2:h * KB + (q + 1) * KB // 2, ds(at, P)]) for q in range(2)]

        def load_q(sp, i, p, h, w):
            at = i * (2 * HEAD_DIM) + Q_COL + p * HEAD_DIM
            return [sp.dma_start(w[:, :, q * HEAD_DIM:(q + 1) * HEAD_DIM],
                                 w_in[:, h * KB:(h + 1) * KB, ds(at + q * GROUP * HEAD_DIM, HEAD_DIM)]) for q in range(2)]
        with ExitStack() as inp:
            h_hi = sb(nc, inp, "h_hi", [P, KD, ROWS], F32R)
            h_lo = sb(nc, inp, "h_lo", [P, KD, ROWS], F32R)
            project_split(k, "s2", KD, 2, [(KR, 2, load_z), (KA // 2, 2, load_q)], h_hi, h_lo, lambda c: hT[:, c, :],
                          all_rows, copy_chunk(streams))
        rg_lru(k, z_in, z_gate, vec, state, mods, cT, ident)
        compressed = ExitStack()
        ck_s = sb(nc, compressed, "ck_s", [P, DEC_BATCH * NBS])
        cv_s = sb(nc, compressed, "cv_s", [NBS, DEC_BATCH, KV_WIDTH])
        ck_p = sb(nc, compressed, "ck_p", [P, NBP])
        cv_p = sb(nc, compressed, "cv_p", [NBP, KV_WIDTH])
        with ExitStack() as inp:
            kvn = sb(nc, inp, "kvn", [P, TILES + 1, KV_COLS])
            kT = sb(nc, inp, "kT", [P, 2, ROWS])
            gates = sb(nc, inp, "gates", [P, TILES + 1, 3 * N_HEADS])
            keys_and_values(k, hT, qT, qR, kvn, kT, gates, q_plain, q_rot, k_new, v_new, gate_rows, ident, kv_stored)
            compress(k, ck_s, cv_s, ck_p, cv_p, ident, page_rows, hT[:, :, :].rearrange("p k r -> p (k r)"))
            prompt_attention(k, qT, qR, kvn, kT, gates, ck_p, cv_p, attn, ident)
        k.recycle()
        sample_attention(k, q_plain, q_rot, k_new, v_new, gate_rows, ck_s, cv_s, page_parts, attn, ident,
                         hT[:, :, :].rearrange("p k r -> p (k r)")[:, (TILES + 1) * ATTN_WIDTH:],
                         qR.rearrange("p k r -> p (k r)"), qT.rearrange("p k r -> p (k r)"))
        compressed.close()
        samp.close()
        with ExitStack() as mo:
            turn_attention(k, attn, merged, ident)
            gains = vec[:, VEC["gn_rnn"][0]:VEC["gn_attn"][1]]
            norm_rows(k, "n2", [list(range(KR)), list(range(KR, KR + KA))],
                      lambda c: merged[:, c, :], lambda c: merged[:, c, :],
                      (gains, None, None, ones, eps))
            w_out = dram["w_out"][0].rearrange("(k p) n -> p k n", p=P)
            m_hi = sb(nc, mo, "merged_hi", [P, KD, ROWS], F32R)
            m_lo = sb(nc, mo, "merged_lo", [P, KD, ROWS], F32R)
            project_split(k, "s9", KD, 1,
                          [(KD // 2, 1, lambda sp, i, p, h, w: [sp.dma_start(w, w_out[:, :, ds(i * (2 * P) + p * P, P)])])],
                          m_hi, m_lo, lambda c: merged[:, c, :], all_rows, add_gated_rows(xT, factor(2), all_rows),
                          hT[:, :, :].rearrange("p k r -> p (k r)"))
        mixers.close()
        norm_rows(k, "n3", [list(range(KD))], lambda c: xT[:, c, :], lambda c: hT[:, c, :],
                  (V["ln2_g"], factor(4), lambda c: factor(3)[:, c, :], ones, eps))
        w_down = dram["w_down"][0].rearrange("(k p) n -> p k n", p=P)
        HB = KF // 2

        def load_down(sp, i, p, h, w):
            return [sp.dma_start(w, w_down[:, h * HB:(h + 1) * HB, ds(i * (2 * P) + p * P, P)])]
        for g in range(NG):
            with ExitStack() as ff:
                hid_hi = sb(nc, ff, f"hid_hi{g}", [P, KF, GR], F32R)
                hid_lo = sb(nc, ff, f"hid_lo{g}", [P, KF, GR], F32R)
                space = sb(nc, ff, f"raw{g}", [P, 4 * KD * P])
                ffn_up_split(k, g, hT, hid_hi, hid_lo, space)
                project_split(k, f"s12g{g}", KF, 2, [(KD // 2, 1, load_down)], hid_hi, hid_lo, None, [(0, GR)],
                              add_gated_rows(xT, factor(5), [(g * GR, (g + 1) * GR)]), space)
        norm_rows(k, "n4", [list(range(KD))], lambda c: xT[:, c, :], lambda c: xT[:, c, :],
                  (V["final_g"], None, None, ones, eps))
        store_rows(k, xT, ident, win_copied)


_INS = ['x_prompt', 'x_sample', 'cache_cmp_kv', 'cache_sel_kv', 'state_win_kv', 'state_conv', 'state_lru_h',
        'page_table', 'c_prompt', 'c_sample', 'ln1_g', 'ln2_g', 'w_ada', 'b_ada', 'w_in', 'conv_w', 'conv_b',
        'lru_wa', 'lru_ba', 'lru_wx', 'lru_bx', 'lru_lambda', 'cmp_pe', 'cmp_w1', 'cmp_w2', 'gn_rnn', 'gn_attn',
        'w_out', 'w_gate', 'w_up', 'w_down', 'final_g']
_OUTS = [("y_prompt", (1, SEQ, D_MODEL)), ("y_sample", (DEC_BATCH, DEC_SEQ, D_MODEL)),
         ("new_cmp_prompt", (1, 1, SEQ, 2, N_KV, HEAD_DIM)), ("new_cmp_sample", (1, DEC_BATCH, DEC_SEQ, 2, N_KV, HEAD_DIM)),
         ("new_sel_prompt", (1, 1, SEQ, 2, N_KV, HEAD_DIM)), ("new_sel_sample", (1, DEC_BATCH, DEC_SEQ, 2, N_KV, HEAD_DIM)),
         ("new_win_prompt", (1, 1, WINDOW, 2, N_KV, HEAD_DIM)), ("new_win_sample", (1, DEC_BATCH, WINDOW, 2, N_KV, HEAD_DIM)),
         ("new_conv_prompt", (1, 1, CONV_W - 1, RNN_WIDTH)), ("new_conv_sample", (1, DEC_BATCH, CONV_W - 1, RNN_WIDTH)),
         ("new_lru_h_prompt", (1, 1, RNN_WIDTH)), ("new_lru_h_sample", (1, DEC_BATCH, RNN_WIDTH))]


def kernel(**inputs):
    import concourse.bacc as _bacc
    from concourse.bass_utils import run_bass_kernel_spmd as _run

    nc = _bacc.Bacc("TRN2", target_bir_lowering=False, num_devices=1)
    arrays, dram = {}, {}
    laid = {name: np.ascontiguousarray(inputs[name]) for name in _INS}
    laid.update(constants())
    for name, a in laid.items():
        arrays[f"in_{name}"] = a
        dram[name] = nc.dram_tensor(f"in_{name}", a.shape, mybir.dt.from_np(a.dtype), kind="ExternalInput").ap()
    for name, shape in _OUTS:
        dram[name] = nc.dram_tensor(f"out_{name}", shape, F32, kind="ExternalOutput").ap()
    hymba_step(nc, dram)
    r = _run(nc, [arrays], core_ids=[0])
    return tuple(r.results[0][f"out_{name}"] for name, _ in _OUTS)
```

```python
import math
from contextlib import ExitStack

import numpy as np

import concourse.bass as bass
from concourse import mybir

F32 = mybir.dt.float32
F32R = mybir.dt.float32r
I32 = mybir.dt.int32
ALU = mybir.AluOpType
ACT = mybir.ActivationFunctionType
AX = mybir.AxisListType.X
ds = bass.ds

P = 128
D_MODEL = 1024
SEQ = 1024
DEC_BATCH = 8
DEC_SEQ = 4
PAST_LEN = 2048
PAGE_SIZE = 128
N_PAGES = PAST_LEN // PAGE_SIZE
HEAD_DIM = 64
N_HEADS = 8
N_KV = 2
GROUP = N_HEADS // N_KV
ATTN_WIDTH = N_HEADS * HEAD_DIM
KV_WIDTH = N_KV * HEAD_DIM
BLOCK = 64
CMP_HIDDEN = 128
N_SEL = 16
WINDOW = 512
ROT_DIM = HEAD_DIM // 4
HALF = ROT_DIM // 2
ROPE_THETA = 500000.0
RNN_WIDTH = D_MODEL - ATTN_WIDTH
RNN_BLOCK_W = RNN_WIDTH // 8
CONV_W = 4
LRU_C = 8.0
D_FF = ((8 * D_MODEL + 3 * 256 - 1) // (3 * 256)) * 256
SCALE = HEAD_DIM ** -0.5
EPS = 1e-6
NEG = -1e30

KD = D_MODEL // P
RS = DEC_BATCH * DEC_SEQ
ROWS = SEQ + RS
TILES = SEQ // P
NG = 3
GR = ROWS // NG
KR = RNN_WIDTH // P
KA = ATTN_WIDTH // P
KF = D_FF // P
COND = 1 + DEC_BATCH
KV_COLS = 6 * KV_WIDTH
NAT_COLS = KV_COLS + 3 * N_HEADS
Q_COL = 2 * RNN_WIDTH
NAT_COL = Q_COL + ATTN_WIDTH
NBP = SEQ // BLOCK
NBS = PAST_LEN // BLOCK
SG = DEC_BATCH // 4
BT = DEC_BATCH // SG
QR = N_KV * DEC_SEQ * GROUP
TP = PAST_LEN // P
WP = WINDOW // P
L_CHUNK = 8
N_LCH = BLOCK // L_CHUNK
ROWF = L_CHUNK * 2 * KV_WIDTH
NFREE = N_SEL - 3
NCAND = NBS - 2

VEC = {}
_at = 0
for _name, _n in (("b_ada", 6 * KD), ("ln1_g", KD), ("ln2_g", KD), ("final_g", KD), ("gn_rnn", KR),
                  ("gn_attn", KA), ("conv_w", CONV_W * KR), ("conv_b", KR), ("lru_ba", KR), ("lru_bx", KR),
                  ("lru_lambda", KR)):
    VEC[_name] = (_at, _at + _n)
    _at += _n
N_VEC = _at


class Steps:

    def __init__(self, eng, sem):
        self.eng, self.sem, self.base, self.n = eng, sem, 0, 0

    def done(self, ins):
        ins.then_inc(self.sem, 1)
        self.n += 1

    def fence(self):
        self.eng.wait_ge(self.sem, self.base + self.n)

    def then(self, ins):
        self.done(ins)
        self.fence()

    def enter(self, i, per):
        self.start, self.per = self.base + self.n, per
        self.base, self.n = self.start + i * per, 0

    def leave(self, trips):
        assert self.n == self.per, (self.n, self.per)
        self.base, self.n = self.start + trips * self.per, 0


def bcast(ap, axis, n):
    v = ap.unsqueeze(axis)
    shape = list(v.shape)
    shape[axis] = n
    return v.to_broadcast(shape)


def constants():
    f = np.float32
    c = {}
    c["ident"] = np.eye(P, dtype=f)
    inv = np.exp(np.arange(HALF, dtype=f) * f(-math.log(ROPE_THETA) / HALF)).astype(f)
    pos = np.concatenate([np.arange(SEQ), np.tile(PAST_LEN + np.arange(DEC_SEQ), DEC_BATCH)]).astype(f)
    ang = (pos[:, None] * inv[None, :]).astype(f)
    cos, sin = np.cos(ang.astype(np.float64)).astype(f), np.sin(ang.astype(np.float64)).astype(f)
    ct, st = np.ones((P, ROWS), f), np.zeros((P, ROWS), f)
    rot = np.zeros((P, P), f)
    for h in range(2):
        for d in range(ROT_DIM):
            ct[h * HEAD_DIM + d] = cos[:, d % HALF]
            st[h * HEAD_DIM + d] = sin[:, d % HALF]
        for d in range(HALF):
            rot[h * HEAD_DIM + d + HALF, h * HEAD_DIM + d] = -1
            rot[h * HEAD_DIM + d, h * HEAD_DIM + d + HALF] = 1
    c["cos_t"], c["sin_t"], c["rot"] = ct, st, rot
    nat = np.zeros((P, 2, TILES + 1, HALF), f)
    for t in range(TILES + 1):
        n = min(P, ROWS - t * P)
        nat[:n, 0, t], nat[:n, 1, t] = cos[t * P:t * P + n], sin[t * P:t * P + n]
    c["rope_nat"] = nat.reshape(P, -1)
    q, k = np.arange(P)[:, None], np.arange(P)[None, :]
    c["mask_diag"] = np.where(k > q, f(NEG), f(0))
    c["mask_tail"] = np.where(k <= q, f(NEG), f(0))
    qpos = np.arange(TILES)[None, :, None] * P + np.arange(P)[:, None, None]
    end = (np.arange(NBP)[None, None, :] + 1) * BLOCK - 1
    c["mask_cmp"] = np.where(end <= qpos, f(0), f(NEG)).reshape(P, -1)
    r = np.arange(P)
    rb, rs = r // QR, (r % 16) // GROUP
    col = np.arange(RS)
    m = np.zeros((P, SG, RS), f)
    for g in range(SG):
        own = (col[None, :] // DEC_SEQ == (g * BT + rb)[:, None]) & (col[None, :] % DEC_SEQ <= rs[:, None])
        m[:, g] = np.where(own, f(0), f(NEG))
    c["mask_new"] = m.reshape(P, -1)
    tok = np.arange(P)[None, None, :] * WP + np.arange(WP)[None, :, None]
    c["mask_win"] = np.where(tok > rs[:, None, None], f(0), f(NEG)).reshape(P, -1)
    c["same_query"] = (r[:, None] // GROUP == r[None, :] // GROUP).astype(f)
    j, i = np.arange(NCAND)[:, None], np.arange(NCAND)[None, :]
    c["earlier"] = np.broadcast_to((i < j).astype(f).reshape(1, -1), (P, NCAND * NCAND)).copy()
    c["row_in_block"] = (np.arange(P)[:, None] % 2 * N_LCH + np.arange(N_LCH)[None, :]).astype(np.int32)
    c["part_in_page"] = (np.arange(P)[:, None] % 8 + np.zeros((1, DEC_BATCH), int)).astype(np.int32)
    return c


class Ctx:

    def __init__(self, nc, stack, dram):
        self.nc, self.stack, self.dram, self.made = nc, stack, dram, []
        self.psum = stack.enter_context(nc.psum_tensor("banks", [P, 8 * 512], F32))
        self.ps = [self.psum[:, j * 512:(j + 1) * 512] for j in range(8)]

    def sems(self, names):
        made = [self.nc.alloc_semaphore(name=n) for n in names.split()]
        self.made += made
        return made

    def recycle(self):
        self.nc.clear_and_free_semaphores(self.made)
        self.made = []
        self.nc.all_engine_barrier()


def sb(nc, stack, name, shape, dt=F32):
    return stack.enter_context(nc.sbuf_tensor(name, shape, dt))


WC = 4
LATE_WC = 1
EARLY = 2 * KD


def factor_sums(pe, out, w, cT):
    for c in range(KD):
        m = pe.matmul(out, lhsT=cT[:, c, :], rhs=w[:, c, :], start=(c == 0), stop=(c == KD - 1))
    return m


def turn_factors(pe, bank, at, nat, ident, n):
    for m in range(n):
        r = pe.matmul(bank[:, ds(at * COND + m * COND, COND)], lhsT=nat[:, m * P:(m + 1) * P], rhs=ident[0:COND, 0:COND],
                      start=True, stop=True)
    return r


def load_and_condition(k, xT, mods, vec, state, cT, ident, ones, eps, page_rows, page_parts, win_copied, spaces):
    nc, ps, d = k.nc, k.ps, k.dram
    (ident_loaded, vec_loaded, cond_loaded, state_loaded, x_loaded0, x_loaded1, x_loaded2, w_loaded0, w_loaded1, w_loaded2, w_loaded3,
     cond_ready, small_turned, small_copied, x_turned, x_copied_v, x_copied_a, mods_summed, mods_copied, mods_turned,
     consts_set, pages_loaded, pages_ready) = k.sems(
        "s1_ident_loaded s1_vec_loaded s1_cond_loaded s1_state_loaded s1_x_loaded0 s1_x_loaded1 s1_x_loaded2 "
        "s1_w_loaded0 s1_w_loaded1 s1_w_loaded2 s1_w_loaded3 s1_cond_ready s1_small_turned s1_small_copied s1_x_turned s1_x_copied_v "
        "s1_x_copied_a s1_mods_summed s1_mods_copied s1_mods_turned s1_consts_set s1_pages_loaded s1_pages_ready")
    x_loaded, w_loaded = [x_loaded0, x_loaded1, x_loaded2], [w_loaded0, w_loaded1, w_loaded2, w_loaded3]
    w_view = d["w_ada"][0].rearrange("(k p) n -> p k n", p=P)
    with ExitStack() as st:
        x_nat = sb(nc, st, "x_nat", [P, TILES + 1, D_MODEL])
        vec_nat = sb(nc, st, "vec_nat", [P, P])
        c_nat = sb(nc, st, "c_nat", [COND, D_MODEL])
        c_act = sb(nc, st, "c_act", [COND, D_MODEL])
        s_nat = sb(nc, st, "s_nat", [4 * DEC_BATCH, RNN_WIDTH])
        w = [space[:, p * KD * WC * P:(p + 1) * KD * WC * P].rearrange("p (k n) -> p k n", k=KD)
             for space in spaces for p in range(2)]
        assert len(w) * WC == EARLY
        f_nat = sb(nc, st, "early_nat", [COND, EARLY // WC, WC * P])
        table = sb(nc, st, "page_table", [P, SG + DEC_BATCH], I32)
        iota = sb(nc, st, "page_iota", [P, N_LCH + DEC_BATCH], I32)
        block = st.enter_context(nc.Block())

        @block.sync
        def _(sp):
            sp.dma_start(ident[:, :], d["ident"]).then_inc(ident_loaded, 16)
            sp.dma_start(c_nat[0:1, :], d["c_prompt"]).then_inc(cond_loaded, 16)
            sp.dma_start(c_nat[1:COND, :], d["c_sample"]).then_inc(cond_loaded, 16)
            for j in range(2):
                sp.dma_start(x_nat[:, 4 * j:4 * j + 4, :],
                             d["x_prompt"][0, 4 * j * P:(4 * j + 4) * P, :].rearrange("(t p) n -> p t n", p=P)
                             ).then_inc(x_loaded[j], 16)
            sp.dma_start(x_nat[0:RS, TILES, :], d["x_sample"].rearrange("b s n -> (b s) n")).then_inc(x_loaded[2], 16)
            for q in range(EARLY // WC):
                sp.dma_start(w[q], w_view[:, :, q * WC * P:(q + 1) * WC * P]).then_inc(w_loaded[q], 16)

        @block.gpsimd
        def _(pool):
            pool.memset(ones[:, :], 1.0).then_inc(consts_set, 1)
            pool.memset(eps[:, :], EPS).then_inc(consts_set, 1)
            for name, (a, b) in VEC.items():
                src = d[name]
                while len(src.shape) > 1:
                    src = src.rearrange("a b -> (a b)") if len(src.shape) == 2 else src.rearrange("a b c -> (a b c)")
                pool.dma_start(vec_nat[a:b, :], src.rearrange("(r n) -> r n", n=P)).then_inc(vec_loaded, 16)
            pool.dma_start(s_nat[0:3 * DEC_BATCH, :], d["state_conv"][0].rearrange("b w n -> (b w) n")
                           ).then_inc(state_loaded, 16)
            pool.dma_start(s_nat[3 * DEC_BATCH:4 * DEC_BATCH, :], d["state_lru_h"][0]).then_inc(state_loaded, 16)
            pool.dma_start(d["new_win_sample"][0].rearrange("b s c h d -> b s (c h d)")[:, 0:WINDOW - DEC_SEQ, :],
                           d["state_win_kv"][0].rearrange("b s c h d -> b s (c h d)")[:, DEC_SEQ:, :]).then_inc(win_copied, 16)
            pool.wait_ge(consts_set, 2)

        @block.tensor
        def _(pe):
            pe.wait_ge(ident_loaded, 16)
            pe.wait_ge(cond_ready, 1)
            for c in range(KD):
                t = pe.transpose(ps[5][:, c * COND:(c + 1) * COND], c_act[:, c * P:(c + 1) * P], ident[0:COND, 0:COND])
            t.then_inc(small_turned, 1)
            for t in range(TILES + 1):
                n = min(P, ROWS - t * P)
                pe.wait_ge(x_loaded[min(t // 4, 2)], 16)
                for h in range(2):
                    step = 2 * t + h
                    if step >= 4:
                        pe.wait_ge(x_copied_a if h else x_copied_v, (step - 4) // 2 + 1)
                    for c in range(4):
                        m = pe.transpose(ps[step % 4][:, c * P:c * P + n], x_nat[0:n, t, (4 * h + c) * P:(4 * h + c + 1) * P],
                                         ident[0:n, 0:n])
                    m.then_inc(x_turned, 1)
            pe.wait_ge(small_copied, 1)
            for q in range(EARLY // WC):
                pe.wait_ge(w_loaded[q], 16)
                if q == 0:
                    pe.wait_ge(x_copied_v, TILES + 1)
                    pe.wait_ge(x_copied_a, TILES + 1)
                factor_sums(pe, ps[q][0:COND, :], w[q], cT).then_inc(mods_summed, 1)
                if q:
                    pe.wait_ge(mods_copied, q)
                    turn_factors(pe, ps[7], (q - 1) * WC, f_nat[:, q - 1, :], ident, WC)
            pe.wait_ge(mods_copied, EARLY // WC)
            turn_factors(pe, ps[7], EARLY - WC, f_nat[:, EARLY // WC - 1, :], ident, WC).then_inc(mods_turned, 1)
            pe.wait_ge(vec_loaded, 16 * len(VEC))
            pe.transpose(ps[4][:, 0:N_VEC], vec_nat[0:N_VEC, :], ident[0:N_VEC, 0:N_VEC]).then_inc(small_turned, 1)
            pe.wait_ge(state_loaded, 32)
            for c in range(KR):
                t = pe.transpose(ps[6][:, c * 32:(c + 1) * 32], s_nat[:, c * P:(c + 1) * P], ident[0:32, 0:32])
            t.then_inc(small_turned, 1)

        @block.scalar
        def _(act):
            flat = d["page_table"].rearrange("b j -> (b j)")
            for g in range(SG):
                act.dma_start(table[:, g:g + 1], bcast(flat[g * P // 2:(g + 1) * P // 2], 1, 2).unsqueeze(2),
                               allow_slow_non_contiguous=True).then_inc(pages_loaded, 16)
            for b in range(DEC_BATCH):
                act.dma_start(table[:, SG + b:SG + b + 1], bcast(d["page_table"][b], 1, 8).unsqueeze(2),
                               allow_slow_non_contiguous=True).then_inc(pages_loaded, 16)
            act.dma_start(iota[:, 0:N_LCH], d["row_in_block"]).then_inc(pages_loaded, 16)
            act.dma_start(iota[:, N_LCH:], d["part_in_page"]).then_inc(pages_loaded, 16)
            act.wait_ge(cond_loaded, 32)
            act.activation(c_act[:, :], c_nat[:, :], ACT.Silu).then_inc(cond_ready, 1)
            for t in range(TILES + 1):
                n = min(P, ROWS - t * P)
                act.wait_ge(x_turned, 2 * t + 2)
                act.activation(xT[:, 4:8, t * P:t * P + n],
                               ps[(2 * t + 1) % 4][:, :].rearrange("p (c n) -> p c n", c=4)[:, :, 0:n],
                               ACT.Copy).then_inc(x_copied_a, 1)

        @block.vector
        def _(dve):
            dve.wait_ge(small_turned, 1)
            dve.tensor_copy(cT[:, :, :], ps[5][:, 0:KD * COND].rearrange("p (c n) -> p c n", c=KD)).then_inc(small_copied, 1)
            for t in range(TILES + 1):
                n = min(P, ROWS - t * P)
                dve.wait_ge(x_turned, 2 * t + 1)
                dve.tensor_copy(xT[:, 0:4, t * P:t * P + n],
                                ps[(2 * t) % 4][:, :].rearrange("p (c n) -> p c n", c=4)[:, :, 0:n]
                                ).then_inc(x_copied_v, 1)
            for q in range(EARLY // WC):
                dve.wait_ge(mods_summed, q + 1)
                dve.tensor_copy(f_nat[:, q, :], ps[q][0:COND, :]).then_inc(mods_copied, 1)
            dve.wait_ge(small_turned, 2)
            dve.tensor_copy(vec[:, :], ps[4][:, 0:N_VEC]).then_inc(small_copied, 1)
            dve.wait_ge(small_turned, 3)
            dve.tensor_copy(state[:, :, :], ps[6][:, 0:KR * 32].rearrange("p (c n) -> p c n", c=KR)).then_inc(small_copied, 1)
            dve.wait_ge(small_copied, 3)
            dve.wait_ge(pages_loaded, 16 * (SG + DEC_BATCH + 2))
            for g in range(SG):
                dve.scalar_tensor_tensor(page_rows[:, g, :], table[:, g:g + 1].to_broadcast([P, N_LCH]), 2 * N_LCH,
                                         iota[:, 0:N_LCH], ALU.mult, ALU.add).then_inc(pages_ready, 1)
            dve.scalar_tensor_tensor(page_parts[:, :], table[:, SG:], 8, iota[:, N_LCH:], ALU.mult, ALU.add
                                     ).then_inc(pages_ready, 1)
            dve.wait_ge(pages_ready, SG + 1)
            dve.wait_ge(mods_turned, 1)
            dve.tensor_tensor(mods[:, 0:EARLY, :], ps[7][:, 0:EARLY * COND].rearrange("p (m c) -> p m c", m=EARLY),
                              bcast(vec[:, 0:EARLY], 2, COND), ALU.add)


def norm_rows(k, tag, parts, sources, outs, adaln=None):
    nc, ps = k.nc, k.ps
    g_of, factors, shifts, ones, eps = adaln
    sq_ready, sq_used0, sq_used1, summed, root_ready, stepped, scaled, done_a = k.sems(
        " ".join(f"{tag}_{n}" for n in "sq_ready sq_used0 sq_used1 summed root_ready stepped scaled done_a".split()))
    sq_used = [sq_used0, sq_used1]
    NPART = len(parts)
    with ExitStack() as st:
        sq = [sb(nc, st, f"{tag}_sq{p}", [P, ROWS]) for p in range(2)]
        rstd = [sb(nc, st, f"{tag}_rstd{n}", [P, ROWS]) for n in range(NPART)]
        gain = sb(nc, st, f"{tag}_gain", [P, KD, COND])
        block = st.enter_context(nc.Block())

        @block.scalar
        def _(act):
            n = 0
            for chunks in parts:
                for c in chunks:
                    if n >= 2:
                        act.wait_ge(sq_used[n % 2], n // 2)
                    act.activation(sq[n % 2][:, :], sources(c), ACT.Square).then_inc(sq_ready, 1)
                    n += 1
            for j, chunks in enumerate(parts):
                act.wait_ge(summed, j + 1)
                for g in range(NG):
                    r = act.activation(rstd[j][:, g * GR:(g + 1) * GR], ps[NG * j + g][:, 0:GR], ACT.Sqrt,
                                       bias=eps[:, 0:1], scale=1.0 / (P * len(chunks)))
                r.then_inc(root_ready, 1)
            if shifts is not None:
                for n, c in enumerate(c for chunks in parts for c in chunks):
                    act.wait_ge(scaled, n + 1)
                    act.activation(outs(c)[:, 0:SEQ], outs(c)[:, 0:SEQ], ACT.Identity, bias=shifts(c)[:, 0:1],
                                   scale=gain[:, c, 0:1]).then_inc(done_a, 1)
                act.wait_ge(done_a, KD)

        @block.tensor
        def _(pe):
            n = 0
            for j, chunks in enumerate(parts):
                for i, c in enumerate(chunks):
                    pe.wait_ge(sq_ready, n + 1)
                    for g in range(NG):
                        m = pe.matmul(ps[NG * j + g][:, 0:GR], lhsT=ones[:, :], rhs=sq[n % 2][:, g * GR:(g + 1) * GR],
                                      start=(i == 0), stop=(i == len(chunks) - 1))
                    m.then_inc(sq_used[n % 2], 1)
                    n += 1
                pe.wait_ge(sq_used[(n - 1) % 2], (n - 1) // 2 + 1)
                pe.sem_inc(summed, 1)

        @block.vector
        def _(dve):
            s = Steps(dve, stepped)
            if shifts is not None:
                s.done(dve.scalar_tensor_tensor(gain[:, :, :], factors, 1.0, bcast(g_of, 2, COND), ALU.add, ALU.mult))
            n = 0
            for j, chunks in enumerate(parts):
                dve.wait_ge(root_ready, j + 1)
                s.then(dve.reciprocal(rstd[j][:, :], rstd[j][:, :]))
                for c in chunks:
                    if shifts is None:
                        dve.scalar_tensor_tensor(outs(c), sources(c), g_of[:, n:n + 1], rstd[j][:, :], ALU.mult,
                                                 ALU.mult).then_inc(scaled, 1)
                    else:
                        dve.tensor_tensor(outs(c), sources(c), rstd[j][:, :], ALU.mult).then_inc(scaled, 1)
                    n += 1
            if shifts is not None:
                for n, c in enumerate(c for chunks in parts for c in chunks):
                    rows = outs(c)[:, SEQ:ROWS].rearrange("p (b s) -> p b s", b=DEC_BATCH)
                    dve.wait_ge(scaled, n + 1)
                    s.then(dve.tensor_tensor(rows, rows, bcast(gain[:, c, 1:COND], 2, DEC_SEQ), ALU.mult))
                    s.then(dve.tensor_tensor(rows, rows, bcast(shifts(c)[:, 1:COND], 2, DEC_SEQ), ALU.add))
            dve.wait_ge(scaled, sum(map(len, parts)))


def copy_chunk(dst):
    def take(dve, s, i, p, banks, tmp):
        for g in range(NG):
            r = dve.tensor_copy(dst[:, ds(i * 2 + p, 1), g * GR:(g + 1) * GR], banks[g].unsqueeze(1))
            if g < NG - 1:
                s.done(r)
        return r
    take.per = 2 * (NG - 1)
    return take


def rg_lru(k, z_in, z_gate, vec, state, mods, cT, ident):
    nc, ps, d = k.nc, k.ps, k.dram
    SLOTS = KR
    (cleared, loaded, conv_done, stepped, summed, act_done, rates_ready, last_ready, last_turned, last_copied, stored,
     abs_ready, decay_ready, ada_summed, ada_copied, ada_turned, *ada_loaded) = k.sems(
        "s3_cleared s3_loaded s3_conv_done s3_stepped s3_summed s3_act_done s3_rates_ready s3_last_ready s3_last_turned "
        "s3_last_copied s3_stored s3_abs_ready s3_decay_ready "
        "s3_ada_summed s3_ada_copied s3_ada_turned s3_ada_loaded0 s3_ada_loaded1 s3_ada_loaded2 s3_ada_loaded3")
    ada_view = d["w_ada"][0].rearrange("(k p) n -> p k n", p=P)
    LATE = 6 * KD - EARLY
    ROUNDS = LATE // LATE_WC // SLOTS
    V = {n: vec[:, a:b] for n, (a, b) in VEC.items()}
    LAST = 3 + 3 * DEC_BATCH + 1 + DEC_BATCH
    with ExitStack() as st:
        wa = sb(nc, st, "wa", [P, 2, KR, P])
        r4 = sb(nc, st, "r4", [P, KR, ROWS])
        i4 = sb(nc, st, "i4", [P, KR, ROWS])
        conv = sb(nc, st, "conv", [P, KR, ROWS])
        w_ada = [sb(nc, st, f"late_ada{p}", [P, KD, LATE_WC * P]) for p in range(SLOTS)]
        f_nat = sb(nc, st, "late_nat", [COND, SLOTS, LATE_WC * P])
        a4 = z_in[:, :, :]
        xs = sb(nc, st, "xs", [P, KR, DEC_BATCH, CONV_W - 1 + DEC_SEQ])
        t = sb(nc, st, "lru_small", [P, 8, KR])
        last = sb(nc, st, "last", [P, KR, LAST])
        last_nat = i4[0:LAST, 0, 0:RNN_WIDTH]
        block = st.enter_context(nc.Block())

        @block.sync
        def _(sp):
            sp.wait_ge(cleared, 1)
            for j, w in enumerate(("lru_wa", "lru_wx")):
                for h in range(2):
                    b = h * RNN_BLOCK_W
                    sp.dma_start(wa[b:b + RNN_BLOCK_W, j, :, b:b + RNN_BLOCK_W],
                                 d[w][0].rearrange("(c h) a e -> h a c e", h=2)[h]).then_inc(loaded, 16)
            with sp.Fori(0, ROUNDS) as i:
                for p in range(SLOTS):
                    sp.wait_ge(ada_summed, i * SLOTS + p + 1)
                    sp.dma_start(w_ada[p][:, :, :], ada_view[:, :, ds(i * (SLOTS * LATE_WC * P) + (EARLY + p * LATE_WC) * P, LATE_WC * P)]
                                 ).then_inc(ada_loaded[p], 16)
            sp.wait_ge(last_copied, 1)
            n = 3 * DEC_BATCH
            sp.dma_start(d["new_conv_prompt"][0, 0], last_nat[0:3, :]).then_inc(stored, 16)
            sp.dma_start(d["new_conv_sample"][0].rearrange("b w n -> (b w) n"), last_nat[3:3 + n, :]).then_inc(stored, 16)
            sp.dma_start(d["new_lru_h_prompt"][0], last_nat[3 + n:4 + n, :]).then_inc(stored, 16)
            sp.dma_start(d["new_lru_h_sample"][0], last_nat[4 + n:LAST, :]).then_inc(stored, 16)
            sp.wait_ge(stored, 64)

        @block.gpsimd
        def _(pool):
            pool.memset(wa[:, :, :, :], 0.0).then_inc(cleared, 1)

        @block.tensor
        def _(pe):
            def factors(i, p):
                pe.wait_ge(ada_loaded[p], i * 16 + 16)
                pe.wait_ge(ada_copied, i * SLOTS + p + 1)
                factor_sums(pe, ps[6][p % 2 * 32:p % 2 * 32 + COND, 0:LATE_WC * P], w_ada[p], cT).then_inc(ada_summed, 1)

            def turn(i, p):
                pe.wait_ge(ada_copied, i * SLOTS + p + 3)
                turn_factors(pe, ps[7], i * (SLOTS * LATE_WC) + p * LATE_WC, f_nat[:, p, :], ident, LATE_WC).then_inc(ada_turned, 1)
            pe.sem_inc(ada_summed, SLOTS)
            pe.sem_inc(ada_turned, SLOTS)
            pe.wait_ge(loaded, 64)
            for c in range(KR):
                pe.wait_ge(conv_done, c + 1)
                if c:
                    pe.wait_ge(act_done, 2 * c)
                for j in range(2):
                    for g in range(NG):
                        m = pe.matmul(ps[NG * j + g][:, 0:GR], lhsT=wa[:, j, c, :], rhs=conv[:, c, g * GR:(g + 1) * GR],
                                      start=True, stop=True)
                    m.then_inc(summed, 1)
                for n in (2 * c, 2 * c + 1):
                    factors(n // SLOTS, n % SLOTS)
                    if n:
                        turn((n - 1) // SLOTS, (n - 1) % SLOTS)
            turn(2 * KR // SLOTS - 1, SLOTS - 1)
            with pe.Fori(0, ROUNDS - 2 * KR // SLOTS) as i:
                for p in range(SLOTS):
                    factors(i + 2 * KR // SLOTS, p)
                    if p:
                        turn(i + 2 * KR // SLOTS, p - 1)
                turn(i + 2 * KR // SLOTS, SLOTS - 1)
            pe.wait_ge(last_ready, 1)
            for c in range(KR):
                m = pe.transpose(ps[6][0:LAST, c * P:(c + 1) * P], last[:, c, :], ident[:, :])
            m.then_inc(last_turned, 1)

        @block.scalar
        def _(act):
            s = Steps(act, act_done)
            blocks = iter(range(ROUNDS * SLOTS))

            def take_factors(count):
                for _ in range(count):
                    n = next(blocks)
                    act.wait_ge(ada_summed, SLOTS + n + 1)
                    act.wait_ge(ada_turned, n + 1)
                    act.activation(f_nat[:, n % SLOTS, :], ps[6][n % 2 * 32:n % 2 * 32 + COND, 0:LATE_WC * P], ACT.Copy
                                   ).then_inc(ada_copied, 1)
            for c in range(KR):
                for j, (dst, b) in enumerate(((r4, "lru_ba"), (i4, "lru_bx"))):
                    act.wait_ge(summed, 2 * c + j + 1)
                    for g in range(NG):
                        r = act.activation(dst[:, c, g * GR:(g + 1) * GR], ps[NG * j + g][:, 0:GR], ACT.Sigmoid,
                                           bias=V[b][:, c:c + 1])
                    s.done(r)
                take_factors(2)
            act.wait_ge(abs_ready, 1)
            act.activation(t[:, 1, :], t[:, 0, :], ACT.Exp).then_inc(rates_ready, 1)
            s.fence()
            act.wait_ge(decay_ready, 1)
            for c in range(KR):
                s.done(act.activation(a4[:, c, :], r4[:, c, :], ACT.Exp, scale=t[:, 6, c:c + 1]))
                s.fence()
                s.done(act.activation(r4[:, c, :], r4[:, c, :], ACT.Tanh, scale=t[:, 7, c:c + 1]))
                take_factors(2)
            for c in range(KR):
                act.wait_ge(rates_ready, 2 + c)
                s.done(act.activation(r4[:, c, :], r4[:, c, :], ACT.Sqrt))
                take_factors(1)
            for c in range(KR):
                s.done(act.activation(z_gate[:, c, :], z_gate[:, c, :], ACT.Gelu_apprx_tanh))
                take_factors(3)
            assert next(blocks, None) is None

        @block.vector
        def _(dve):
            s = Steps(dve, stepped)
            dve.sem_inc(ada_copied, 2)
            lam = V["lru_lambda"]
            s.then(dve.tensor_scalar(t[:, 2, :], lam, -1.0, None, ALU.mult))
            dve.tensor_tensor(t[:, 0, :], lam, t[:, 2, :], ALU.min).then_inc(abs_ready, 1)
            s.done(dve.tensor_copy(xs[:, :, :, 0:3], state[:, :, 0:3 * DEC_BATCH].rearrange("p c (b w) -> p c b w", w=3)))
            s.then(dve.tensor_copy(xs[:, :, :, 3:], z_in[:, :, SEQ:ROWS].rearrange("p c (b s) -> p c b s", s=DEC_SEQ)))
            s.done(dve.tensor_copy(last[:, :, 0:3], z_in[:, :, SEQ - 3:SEQ]))
            s.done(dve.tensor_copy(last[:, :, 3:3 + 3 * DEC_BATCH].rearrange("p c (b w) -> p c b w", w=3), xs[:, :, :, DEC_SEQ:]))
            for c in range(KR):
                x, o = z_in[:, c, :], conv[:, c, :]
                so = o[:, SEQ:ROWS].rearrange("p (b s) -> p b s", s=DEC_SEQ)
                w = [V["conv_w"][:, j * KR + c:j * KR + c + 1] for j in range(CONV_W)]
                b = V["conv_b"][:, c:c + 1]
                s.done(dve.tensor_scalar(o[:, 0:SEQ], x[:, 0:SEQ], w[3], b, ALU.mult, ALU.add))
                s.then(dve.tensor_scalar(so, xs[:, c, :, 3:3 + DEC_SEQ], w[3], b, ALU.mult, ALU.add))
                for j in (2, 1, 0):
                    lag = 3 - j
                    s.done(dve.scalar_tensor_tensor(o[:, lag:SEQ], x[:, 0:SEQ - lag], w[j], o[:, lag:SEQ], ALU.mult, ALU.add))
                    r = dve.scalar_tensor_tensor(so, xs[:, c, :, j:j + DEC_SEQ], w[j], so, ALU.mult, ALU.add)
                    if j:
                        s.then(r)
                    else:
                        s.fence()
                        r.then_inc(conv_done, 1)
            dve.wait_ge(rates_ready, 1)
            s.then(dve.tensor_scalar(t[:, 3, :], t[:, 1, :], 2.0, None, ALU.add))
            s.then(dve.reciprocal(t[:, 3, :], t[:, 3, :]))
            s.then(dve.tensor_tensor(t[:, 1, :], t[:, 1, :], t[:, 3, :], ALU.mult))
            s.then(dve.tensor_tensor(t[:, 3, :], t[:, 1, :], t[:, 1, :], ALU.mult))
            s.then(dve.tensor_scalar(t[:, 4, :], t[:, 3, :], 1.0 / 17, 1.0 / 15, ALU.mult, ALU.add))
            for n in (13, 11, 9, 7, 5, 3, 1):
                s.then(dve.tensor_tensor(t[:, 4, :], t[:, 4, :], t[:, 3, :], ALU.mult))
                s.then(dve.tensor_scalar(t[:, 4, :], t[:, 4, :], 1.0 / n, None, ALU.add))
            s.then(dve.scalar_tensor_tensor(t[:, 4, :], t[:, 4, :], 2.0, t[:, 1, :], ALU.mult, ALU.mult))
            s.then(dve.scalar_tensor_tensor(t[:, 5, :], t[:, 2, :], 0.0, t[:, 4, :], ALU.max, ALU.add))
            s.then(dve.tensor_scalar(t[:, 6, :], t[:, 5, :], -LRU_C, None, ALU.mult))
            dve.tensor_scalar(t[:, 7, :], t[:, 5, :], LRU_C, None, ALU.mult).then_inc(decay_ready, 1)
            for c in range(KR):
                dve.wait_ge(act_done, 2 * KR + 2 * c + 2)
                s.then(dve.tensor_tensor(conv[:, c, :], conv[:, c, :], i4[:, c, :], ALU.mult))
                s.then(dve.tensor_tensor(i4[:, c, :], a4[:, c, :], a4[:, c, :], ALU.mult))
                dve.scalar_tensor_tensor(r4[:, c, :], i4[:, c, :], 1.0, r4[:, c, :], ALU.add, ALU.mult).then_inc(rates_ready, 1)
            for c in range(KR):
                dve.wait_ge(act_done, 4 * KR + c + 1)
                s.then(dve.tensor_tensor(r4[:, c, :], r4[:, c, :], conv[:, c, :], ALU.mult))
                first_b = r4[:, c, SEQ:ROWS:DEC_SEQ]
                first_a = a4[:, c, SEQ:ROWS:DEC_SEQ]
                s.then(dve.tensor_tensor(t[:, 0:2, :].rearrange("p a b -> p (a b)"), first_a, state[:, c, 3 * DEC_BATCH:], ALU.mult))
                s.then(dve.tensor_tensor(first_b, first_b, t[:, 0:2, :].rearrange("p a b -> p (a b)"), ALU.add))
                s.then(dve.memset(first_a, 0.0))
                s.then(dve.tensor_tensor_scan(conv[:, c, :], a4[:, c, :], r4[:, c, :], 0.0, ALU.mult, ALU.add))
                s.done(dve.tensor_copy(last[:, c, 27:28], conv[:, c, SEQ - 1:SEQ]))
                s.done(dve.tensor_copy(last[:, c, 28:36], conv[:, c, SEQ + DEC_SEQ - 1:ROWS:DEC_SEQ]))
            s.fence()
            dve.sem_inc(last_ready, 1)
            for c in range(KR):
                dve.wait_ge(act_done, 5 * KR + c + 1)
                s.done(dve.tensor_tensor(z_gate[:, c, :], conv[:, c, :], z_gate[:, c, :], ALU.mult))
            dve.wait_ge(ada_turned, (ROUNDS + 1) * SLOTS)
            dve.tensor_tensor(mods[:, EARLY:, :], ps[7][:, 0:LATE * COND].rearrange("p (m c) -> p m c", m=LATE),
                              bcast(vec[:, EARLY:6 * KD], 2, COND), ALU.add)
            dve.wait_ge(last_turned, 1)
            dve.tensor_copy(last_nat, ps[6][0:LAST, :]).then_inc(last_copied, 1)


def keys_and_values(k, hT, qT, qR, kvn, kT, gates, q_plain, q_rot, k_new, v_new, gate_rows, ident, kv_stored):
    nc, ps, d = k.nc, k.ps, k.dram
    (w_loaded, tabs_loaded, rot_summed, turned_taken, nat_summed, nat_v, nat_a, stepped, keys_ready, gates_ready,
     scratch_stored, gates_loaded, staged_clear, queries_rotated) = k.sems(
        "s4_w_loaded s4_tabs_loaded s4_rot_summed s4_turned_taken s4_nat_summed s4_nat_v s4_nat_a s4_stepped "
        "s4_keys_ready s4_gates_ready s4_scratch_stored s4_gates_loaded s4_staged_clear s4_queries_rotated")
    HN = NAT_COLS // 2
    T9 = TILES + 1
    with ExitStack() as st:
        w = sb(nc, st, "w_nat", [P, KD, NAT_COLS])
        tables = kvn[:, 0:3, :].rearrange("p t n -> p (t n)")
        cos_t, sin_t = tables[:, 0:ROWS], tables[:, ROWS:2 * ROWS]
        rot = sb(nc, st, "rot_m", [P, P])
        rope = sb(nc, st, "rope_nat", [P, 2, T9, HALF])
        tmp = sb(nc, st, "rope_tmp", [P, 4, T9 * N_KV * HALF])
        qtmp = sb(nc, st, "q_tmp", [P, 2, GR])
        block = st.enter_context(nc.Block())

        def rows_of(t):
            return min(P, ROWS - t * P)

        @block.sync
        def _(sp):
            sp.dma_start(rot[:, :], d["rot"]).then_inc(tabs_loaded, 16)
            sp.dma_start(cos_t, d["cos_t"]).then_inc(tabs_loaded, 16)
            sp.dma_start(sin_t, d["sin_t"]).then_inc(tabs_loaded, 16)
            sp.dma_start(rope[:, :, :, :].rearrange("p a t n -> p (a t n)"), d["rope_nat"]).then_inc(tabs_loaded, 16)
            sp.dma_start(w[:, :, :], d["w_in"][0, :, NAT_COL:NAT_COL + NAT_COLS].rearrange("(k p) n -> p k n", p=P)
                         ).then_inc(w_loaded, 16)
            sp.wait_ge(nat_v, T9)
            sp.wait_ge(nat_a, T9)
            flat = {n: d[n].rearrange("x b s c h d -> (x b s) (c h d)") for n in
                    ("new_cmp_prompt", "new_cmp_sample", "new_sel_prompt", "new_sel_sample", "new_win_prompt")}
            W2 = 2 * KV_WIDTH
            sp.dma_start(flat["new_cmp_prompt"].rearrange("(t p) n -> p t n", p=P), kvn[:, 0:TILES, 0:W2]).then_inc(kv_stored, 16)
            sp.dma_start(flat["new_cmp_sample"], kvn[0:RS, TILES, 0:W2]).then_inc(kv_stored, 16)
            sp.wait_ge(keys_ready, 1)
            sp.dma_start(flat["new_sel_prompt"].rearrange("(t p) n -> p t n", p=P), kvn[:, 0:TILES, W2:2 * W2]).then_inc(kv_stored, 16)
            sp.dma_start(flat["new_sel_sample"], kvn[0:RS, TILES, W2:2 * W2]).then_inc(kv_stored, 16)
            sp.dma_start(flat["new_win_prompt"].rearrange("(t p) n -> p t n", p=P),
                         kvn[:, TILES - WINDOW // P:TILES, 2 * W2:3 * W2]).then_inc(kv_stored, 16)
            for b in range(DEC_BATCH):
                sp.dma_start(d["new_win_sample"][0, b].rearrange("s c h d -> s (c h d)")[WINDOW - DEC_SEQ:WINDOW, :],
                             kvn[b * DEC_SEQ:(b + 1) * DEC_SEQ, TILES, 2 * W2:3 * W2]).then_inc(kv_stored, 16)
            sp.wait_ge(kv_stored, 16 * (5 + DEC_BATCH))

        @block.tensor
        def _(pe):
            pe.wait_ge(tabs_loaded, 64)
            step = 0
            for c in range(KA):
                for g in range(NG):
                    if step >= 4:
                        pe.wait_ge(turned_taken, step - 3)
                    pe.matmul(ps[4 + step % 4][:, 0:GR], lhsT=rot[:, :], rhs=qT[:, c, g * GR:(g + 1) * GR], start=True,
                              stop=True).then_inc(rot_summed, 1)
                    step += 1
            pe.wait_ge(w_loaded, 16)
            for t in range(T9):
                n = rows_of(t)
                if t >= 2:
                    pe.wait_ge(nat_v, t - 1)
                    pe.wait_ge(nat_a, t - 1)
                for h in range(2):
                    for c in range(KD):
                        m = pe.matmul(ps[2 * (t % 2) + h][0:n, 0:HN], lhsT=hT[:, c, t * P:t * P + n],
                                      rhs=w[:, c, h * HN:(h + 1) * HN], start=(c == 0), stop=(c == KD - 1))
                m.then_inc(nat_summed, 1)
            pe.wait_ge(keys_ready, 1)
            for kind in range(2):
                col = 2 * KV_WIDTH * (1 + kind)
                for half in range(3):
                    pe.wait_ge(turned_taken, step - 3)
                    tiles = range(4 * half, min(4 * half + 4, T9))
                    for j, t in enumerate(tiles):
                        n = rows_of(t)
                        m = pe.transpose(ps[4 + step % 4][:, j * P:j * P + n], kvn[0:n, t, col:col + KV_WIDTH], ident[0:n, 0:n])
                    m.then_inc(rot_summed, 1)
                    step += 1

        @block.scalar
        def _(act):
            for t in range(T9):
                n = rows_of(t)
                act.wait_ge(nat_summed, t + 1)
                bank = ps[2 * (t % 2) + 1]
                if t == 0:
                    act.wait_ge(queries_rotated, 1)
                if t == TILES:
                    act.wait_ge(staged_clear, 2)
                dst, src = gates[0:n, t, :], bank[0:n, KV_COLS - HN:HN]
                if t == TILES:
                    dst = dst.rearrange("p (k g x) -> p k g x", k=N_KV, x=3)
                    src = src.rearrange("p (x k g) -> p k g x", k=N_KV, x=3)
                act.activation(dst, src, ACT.Sigmoid).then_inc(gates_ready, 1)
                act.activation(kvn[0:n, t, HN:KV_COLS], bank[0:n, 0:KV_COLS - HN], ACT.Copy).then_inc(nat_a, 1)
            act.wait_ge(gates_ready, T9)
            scratch = d["gate_scratch"]
            for h in range(N_KV):
                act.dma_start(scratch[h], gates[0:RS, TILES, h * 3 * GROUP:(h + 1) * 3 * GROUP]).then_inc(scratch_stored, 16)
            act.wait_ge(scratch_stored, 16 * N_KV)
            for g in range(SG):
                for b in range(BT):
                    for h in range(N_KV):
                        r0, row = b * QR + h * DEC_SEQ * GROUP, (g * BT + b) * DEC_SEQ
                        act.dma_start(gate_rows[r0:r0 + DEC_SEQ * GROUP, g, :],
                                      scratch[h, row:row + DEC_SEQ, :].rearrange("s (g x) -> (s g) x", x=3)
                                      ).then_inc(gates_loaded, 16)
            act.wait_ge(gates_loaded, 16 * SG * BT * N_KV)

        @block.vector
        def _(dve):
            s = Steps(dve, stepped)
            dve.memset(kvn[:, TILES, :], 0.0).then_inc(staged_clear, 1)
            dve.memset(gates[:, TILES, :], 0.0).then_inc(staged_clear, 1)
            s.done(dve.memset(q_plain[:, :, :], 0.0))
            s.done(dve.memset(q_rot[:, :, :], 0.0))
            dve.wait_ge(tabs_loaded, 64)
            step = 0
            for c in range(KA):
                for g in range(NG):
                    cols = slice(g * GR, (g + 1) * GR)
                    s.done(dve.tensor_tensor(qR[:, c, cols], qT[:, c, cols], cos_t[:, cols], ALU.mult))
                    dve.wait_ge(rot_summed, step + 1)
                    dve.tensor_tensor(qtmp[:, step % 2, :], ps[4 + step % 4][:, 0:GR], sin_t[:, cols], ALU.mult
                                      ).then_inc(turned_taken, 1)
                    dve.wait_ge(turned_taken, step + 1)
                    s.fence()
                    s.done(dve.tensor_tensor(qR[:, c, cols], qR[:, c, cols], qtmp[:, step % 2, :], ALU.add))
                    step += 1
            s.fence()
            dve.sem_inc(queries_rotated, 1)
            for b in range(BT):
                for h in range(N_KV):
                    part = slice(h * HEAD_DIM, (h + 1) * HEAD_DIM)
                    c0 = b * QR + h * DEC_SEQ * GROUP
                    for dst, src in ((q_plain, qT), (q_rot, qR)):
                        for g in range(SG):
                            row = SEQ + (g * BT + b) * DEC_SEQ
                            s.done(dve.tensor_copy(
                                dst[part, g * BT + b, c0:c0 + DEC_SEQ * GROUP].rearrange("p (s g) -> p s g", g=GROUP),
                                src[part, :, row:row + DEC_SEQ].rearrange("p g s -> p s g")))
            dve.wait_ge(staged_clear, 2)
            for t in range(T9):
                n = rows_of(t)
                dve.wait_ge(nat_summed, t + 1)
                dve.tensor_copy(kvn[0:n, t, 0:HN], ps[2 * (t % 2)][0:n, 0:HN]).then_inc(nat_v, 1)
            dve.wait_ge(nat_v, T9)
            dve.wait_ge(nat_a, T9)
            cos, sin = bcast(rope[:, 0, :, :], 2, N_KV), bcast(rope[:, 1, :, :], 2, N_KV)
            T = [tmp[:, j, :].rearrange("p (t h n) -> p t h n", h=N_KV, n=HALF) for j in range(4)]
            for kind in range(2):
                col = 2 * KV_WIDTH * (1 + kind)
                heads = kvn[:, :, col:col + KV_WIDTH].rearrange("p t (h n) -> p t h n", h=N_KV)
                x1, x2 = heads[:, :, :, 0:HALF], heads[:, :, :, HALF:ROT_DIM]
                s.done(dve.tensor_tensor(T[0], x1, cos, ALU.mult))
                s.done(dve.tensor_tensor(T[1], x2, sin, ALU.mult))
                s.done(dve.tensor_tensor(T[2], x1, sin, ALU.mult))
                s.then(dve.tensor_tensor(T[3], x2, cos, ALU.mult))
                s.done(dve.tensor_tensor(x1, T[0], T[1], ALU.subtract))
                s.then(dve.tensor_tensor(x2, T[2], T[3], ALU.add))
            dve.sem_inc(keys_ready, 1)
            for kind in range(2):
                for half in range(3):
                    dve.wait_ge(rot_summed, step + 1)
                    n = min(4 * P, ROWS - half * 4 * P)
                    dve.tensor_copy(kT[:, kind, half * 4 * P:half * 4 * P + n], ps[4 + step % 4][:, 0:n]).then_inc(turned_taken, 1)
                    step += 1
                col = 2 * KV_WIDTH * (1 + kind)
                s.done(dve.tensor_copy(v_new[:, kind, :], kvn[0:RS, TILES, col + KV_WIDTH:col + 2 * KV_WIDTH]))
                dve.wait_ge(turned_taken, step)
                s.done(dve.tensor_copy(k_new[:, kind, :], kT[:, kind, SEQ:ROWS]))
            s.fence()


def compress(k, ck_s, cv_s, ck_p, cv_p, ident, page_rows, space):
    nc, ps, d = k.nc, k.ps, k.dram
    (w1_loaded0, w1_loaded1, rows_loaded00, rows_loaded01, rows_loaded10, rows_loaded11, p_loaded0, p_loaded1, multiplied,
     turned, copied_v, copied_a, zero_set, all_summed, bias_ready, hid_ready, w2_loaded, w2_clear, out_summed,
     out_taken) = k.sems(
        " ".join("s5_" + n for n in ("w1_loaded0 w1_loaded1 rows_loaded00 rows_loaded01 rows_loaded10 rows_loaded11 p_loaded0 "
                                     "p_loaded1 multiplied turned copied_v copied_a zero_set all_summed bias_ready hid_ready "
                                     "w2_loaded w2_clear out_summed out_taken").split()))
    w1_loaded, p_loaded = [w1_loaded0, w1_loaded1], [p_loaded0, p_loaded1]
    rows_loaded = [[rows_loaded00, rows_loaded01], [rows_loaded10, rows_loaded11]]
    NPB = NBP + 1
    counts = [P, P, NPB]
    LP = L_CHUNK // 2
    STEPS = (SG + 1) * LP
    TRIPS = N_LCH // 2
    AHEAD = STEPS + 1
    cmp_rows = d["cache_cmp_kv"][0].rearrange("a (r l) c h d -> (a r) (l c h d)", l=L_CHUNK)
    prompt_rows = d["new_cmp_prompt"][0, 0].rearrange("(n l) c h d -> n (l c h d)", l=BLOCK)
    w1_view = d["cmp_w1"][0].rearrange("c (l m) d f -> (m d) c l f", m=2)
    with ExitStack() as st:
        w1 = [sb(nc, st, f"w1_{p}", [P, 2, LP, CMP_HIDDEN]) for p in range(2)]
        rows = [[space[:, (2 * g + p) * ROWF:(2 * g + p + 1) * ROWF] for p in range(2)] for g in range(SG)]
        prows = [sb(nc, st, f"prompt_rows{p}", [NPB, ROWF]) for p in range(2)]
        zt = [sb(nc, st, f"zt{p}", [P, 2, 2 * P]) for p in range(2)]
        zero = sb(nc, st, "zero", [P, 512])
        bias = sb(nc, st, "cmp_bias", [P, 2])
        hid = sb(nc, st, "hid", [P, 2, SG, 2 * P])
        hid_p = sb(nc, st, "hid_p", [P, 2, 2 * NPB])
        w2k = sb(nc, st, "w2k", [P, N_KV, P])
        w2v = sb(nc, st, "w2v", [P, HEAD_DIM])
        block = st.enter_context(nc.Block())

        def turn_of(v):
            return v // LP, v % LP

        def source(v, p):
            g, l = turn_of(v)
            n = counts[g]
            buf = (rows[g][p] if g < SG else prows[p][:, :])[0:n, :].rearrange("p (l c n) -> p l c n", c=2, n=KV_WIDTH)
            return buf[:, 2 * l:2 * l + 2], n

        def sums(g, c):
            n = 2 * counts[g]
            return ps[c][:, g * n:(g + 1) * n] if g < SG else ps[2][:, c * n:(c + 1) * n]

        @block.sync
        def _(sp):
            for j in range(N_KV):
                sp.dma_start(w2v[:, :], d["cmp_w2"][0, 1]).then_inc(w2_loaded, 16) if j == 0 else None
                if j == 0:
                    sp.wait_ge(w2_clear, 1)
                sp.dma_start(w2k[:, j, j * HEAD_DIM:(j + 1) * HEAD_DIM], d["cmp_w2"][0, 0]).then_inc(w2_loaded, 16)
            pe_enc = d["cmp_pe"][0].rearrange("c l d -> l c d")
            with sp.Fori(0, TRIPS) as i:
                for p in range(2):
                    sp.wait_ge(multiplied, i * (2 * STEPS) + (p - 1) * STEPS + AHEAD)
                    for c in range(2):
                        sp.dma_start(w1[p][:, c, :, :], w1_view[:, c, ds(i * (2 * LP) + p * LP, LP), :]).then_inc(w1_loaded[p], 16)
                    sp.dma_start(prows[p][0:NBP, :], prompt_rows[:, ds(i * (2 * ROWF) + p * ROWF, ROWF)]).then_inc(p_loaded[p], 16)
                    for h in range(N_KV):
                        sp.dma_start(prows[p][NBP:NPB, :].rearrange("p (l c h d) -> p l c h d", c=2, h=N_KV, d=HEAD_DIM)[:, :, :, h],
                                     pe_enc[ds(i * (2 * L_CHUNK) + p * L_CHUNK, L_CHUNK)].unsqueeze(0)).then_inc(p_loaded[p], 16)

        @block.gpsimd
        def _(pool):
            pool.memset(zero[:, :], 0.0).then_inc(zero_set, 1)
            pool.memset(w2k[:, :, :], 0.0).then_inc(w2_clear, 1)
            for n in range(N_LCH):
                p = n % 2
                if n >= 2:
                    pool.wait_ge(multiplied, (n - 1) * STEPS + AHEAD)
                for g in range(SG):
                    pool.indirect_dma_start(rows[g][p], None, cmp_rows,
                                            bass.IndirectOffsetOnAxis(ap=page_rows[:, g, n:n + 1], axis=0)
                                            ).then_inc(rows_loaded[g][p], 16)

        @block.tensor
        def _(pe):
            pe.wait_ge(zero_set, 1)
            for b in range(3):
                pe.matmul(ps[b][:, :], lhsT=zero[:, 0:P], rhs=zero[:, :], start=True, stop=False, skip_group_check=True)
            pe.sem_inc(multiplied, AHEAD)
            with pe.Fori(0, TRIPS) as i:
                for p in range(2):
                    def turn(v):
                        at = p * STEPS + v
                        src, n = source(v, p)
                        if v == 0:
                            pe.wait_ge(w1_loaded[p], i * 32 + 32)
                            pe.wait_ge(rows_loaded[0][p], i * 16 + 16)
                        if v == LP:
                            pe.wait_ge(rows_loaded[1][p], i * 16 + 16)
                        for e in range(2):
                            for c in range(2):
                                m = pe.transpose(ps[4 + 2 * (at % 2) + e][:, c * n:(c + 1) * n], src[:, e, c, :], ident[0:n, 0:n])
                        m.then_inc(turned, 1)

                    def multiply(v):
                        at = p * STEPS + v
                        g, l = turn_of(v)
                        n = 2 * counts[g]
                        if v == 2 * LP - 2:
                            pe.wait_ge(p_loaded[p], i * 48 + 48)
                        pe.wait_ge(copied_v, i * (4 * STEPS) + 2 * at + 2)
                        pe.wait_ge(copied_a, i * (4 * STEPS) + 2 * at + 2)
                        for c in range(2):
                            m = pe.matmul(sums(g, c), lhsT=w1[p][:, c, l, :], rhs=zt[at % 2][:, c, 0:n],
                                          start=False, stop=False, skip_group_check=True)
                        return m
                    turn(0)
                    for v in range(STEPS):
                        if v + 1 < STEPS:
                            turn(v + 1)
                        multiply(v).then_inc(multiplied, 1)
            for b in range(3):
                m = pe.matmul(ps[b][:, :], lhsT=zero[:, 0:P], rhs=zero[:, :], start=False, stop=True, skip_group_check=True)
            m.then_inc(all_summed, 1)
            pe.wait_ge(w2_loaded, 48)
            pe.wait_ge(hid_ready, 6)
            for g in range(SG):
                for h in range(N_KV):
                    pe.matmul(ps[6][:, g * P:(g + 1) * P], lhsT=w2k[:, h, :], rhs=hid[:, 0, g, h * P:(h + 1) * P],
                              start=(h == 0), stop=(h == 1))
            for h in range(N_KV):
                pe.matmul(ps[6][:, 2 * P:2 * P + NBP], lhsT=w2k[:, h, :], rhs=hid_p[:, 0, h * NPB:h * NPB + NBP],
                          start=(h == 0), stop=(h == 1))
            for h in range(N_KV):
                m = pe.matmul(ps[7][0:NBP, h * HEAD_DIM:(h + 1) * HEAD_DIM], lhsT=hid_p[:, 1, h * NPB:h * NPB + NBP], rhs=w2v[:, :],
                              start=True, stop=True)
            m.then_inc(out_summed, 1)
            for b in range(DEC_BATCH):
                g, r = b // BT, (b % BT) * NBS
                for h in range(N_KV):
                    m = pe.matmul(ps[g][0:NBS, (b % BT) * KV_WIDTH + h * HEAD_DIM:(b % BT) * KV_WIDTH + (h + 1) * HEAD_DIM],
                                  lhsT=hid[:, 1, g, h * P + r:h * P + r + NBS], rhs=w2v[:, :], start=True, stop=True)
                if b % BT == BT - 1:
                    m.then_inc(out_summed, 1)

        def copy_turn(eng, copy, copied, e, i, p, v):
            at = p * STEPS + v
            n = counts[turn_of(v)[0]]
            eng.wait_ge(turned, i * (2 * STEPS) + at + 1)
            eng.wait_ge(multiplied, i * (2 * STEPS) + at - 1 + AHEAD)
            for h in range(N_KV):
                copy(zt[at % 2][e * HEAD_DIM:(e + 1) * HEAD_DIM, :, h * n:(h + 1) * n],
                     ps[4 + 2 * (at % 2) + e][h * HEAD_DIM:(h + 1) * HEAD_DIM, 0:2 * n].rearrange("p (c n) -> p c n", c=2)
                     ).then_inc(copied, 1)

        @block.scalar
        def _(act):
            with act.Fori(0, TRIPS) as i:
                for p in range(2):
                    for v in range(STEPS):
                        copy_turn(act, lambda o, x: act.activation(o, x, ACT.Copy), copied_a, 1, i, p, v)
            act.wait_ge(bias_ready, 1)
            for c in range(2):
                for g in range(SG + 1):
                    dst = hid[:, c, g, :] if g < SG else hid_p[:, c, :]
                    act.activation(dst, sums(g, c), ACT.Gelu_apprx_tanh, bias=bias[:, c:c + 1]
                                   ).then_inc(hid_ready, 1)

        @block.vector
        def _(dve):
            with dve.Fori(0, TRIPS) as i:
                for p in range(2):
                    for v in range(STEPS):
                        copy_turn(dve, dve.tensor_copy, copied_v, 0, i, p, v)
            dve.wait_ge(all_summed, 1)
            for c in range(2):
                m = dve.tensor_copy(bias[:, c:c + 1], sums(SG, c)[:, NBP:NPB])
            m.then_inc(bias_ready, 1)
            dve.wait_ge(out_summed, 1)
            dve.tensor_copy(ck_s[:, :], ps[6][:, 0:SG * P]).then_inc(out_taken, 1)
            dve.tensor_copy(ck_p[:, :], ps[6][:, SG * P:SG * P + NBP]).then_inc(out_taken, 1)
            dve.tensor_copy(cv_p[:, :], ps[7][0:NBP, 0:KV_WIDTH]).then_inc(out_taken, 1)
            for g in range(SG):
                dve.wait_ge(out_summed, g + 2)
                dve.tensor_copy(cv_s[:, g * BT:(g + 1) * BT, :], ps[g][0:NBS, :].rearrange("p (b n) -> p b n", b=BT)
                                ).then_inc(out_taken, 1)
            dve.wait_ge(out_taken, 5)


def prompt_attention(k, qT, qR, kvn, kT, gates, ck_p, cv_p, attn, ident, space):
    nc, ps, psum, d = k.nc, k.ps, k.psum, k.dram
    (masks_loaded, masks_cast, k_hi_done, k_lo_done, q_hi_done, q_doubled, q_lo_done, v_clear, v_spread, staged, scored, max_ready, probs_ready, turned0, turned1, copied0, copied1,
     out_summed, merged, stepped, cmp_scored, cmp_shifted, cmp_exp, cmp_probs, cmp_turned, cmp_copied, cmp_summed,
     cmp_merged, merged_half) = k.sems(" ".join("s6_" + n for n in (
         "masks_loaded masks_cast k_hi_done k_lo_done q_hi_done q_doubled q_lo_done v_clear v_spread staged scored max_ready probs_ready turned0 turned1 copied0 copied1 out_summed "
         "merged stepped cmp_scored cmp_shifted cmp_exp cmp_probs cmp_turned cmp_copied cmp_summed cmp_merged merged_half").split()))
    WT = WINDOW // P
    units = [(t, h, br) for t in range(TILES) for h in range(N_KV) for br in (1, 2)]
    tiles_of = [list(range(t + 1)) if br == 1 else list(range(max(0, t - WT), t + 1)) for t, h, br in units]
    U = len(units)
    place = [u % 2 * 1024 + (0 if len(x) <= 4 else 512 - len(x) * P // 2) for u, x in enumerate(tiles_of)]
    second = [len(x) > 4 for x in tiles_of]
    upto = [sum(second[:u + 1]) for u in range(U)]
    C1 = upto[-1]
    HT = TILES // 2
    with ExitStack() as st:
        diag_b, tail_b, ident_b = [sb(nc, st, n, [P, P], mybir.dt.bfloat16) for n in ("diag_b", "tail_b", "ident_b")]
        at = 0

        def take_space(n):
            nonlocal at
            at += n
            return space[:, at - n:at]
        cmask = take_space(TILES * NBP).rearrange("p (t n) -> p t n", t=TILES)
        vx = take_space(HT * N_KV * HEAD_DIM).rearrange("p (j n) -> p j n", n=HEAD_DIM)
        QC = [take_space(SEQ) for h in range(N_KV)]
        probs = [take_space(SEQ), sb(nc, st, "probs1", [P, SEQ])]
        diag, tail = probs[0][:, 0:P], probs[0][:, P:2 * P]
        flat_kT = kT[:, :, :].rearrange("p a n -> p (a n)")
        pT = [flat_kT[:, p * SEQ:(p + 1) * SEQ] for p in range(2)]
        own = [slice(h * HEAD_DIM, (h + 1) * HEAD_DIM) for h in range(N_KV)]
        KS = [sb(nc, st, f"k_halves{h}", [P, 2, SEQ], F32R) for h in range(N_KV)]
        QD = [sb(nc, st, f"q_doubled{h}", [P, SEQ], F32R) for h in range(N_KV)]
        QL = sb(nc, st, "q_lo", [P, SEQ], F32R)
        nmax = sb(nc, st, "neg_max", [P, 4])
        den = sb(nc, st, "den", [P, 4])
        coef = sb(nc, st, "coef", [P, 4])
        gsel = sb(nc, st, "gate_pair", [P, TILES, 3, N_KV])
        cs = sb(nc, st, "cmp_probs", [P, TILES, N_KV, NBP])
        cst = sb(nc, st, "cmp_stat", [P, 2, TILES, N_KV])
        cT = pT[1][:, SEQ - 2 * P:SEQ].rearrange("p (a n) -> p a n", a=2)
        block = st.enter_context(nc.Block())

        @block.sync
        def _(sp):
            sp.dma_start(diag[:, :], d["mask_diag"]).then_inc(masks_loaded, 16)
            sp.dma_start(tail[:, :], d["mask_tail"]).then_inc(masks_loaded, 16)
            sp.dma_start(space[:, 0:TILES * NBP], d["mask_cmp"]).then_inc(masks_loaded, 16)
            sp.wait_ge(v_clear, 1)
            for j in range(HT * N_KV):
                sp.dma_start(vx[j * NBP:(j + 1) * NBP, j, :], cv_p[:, (j % N_KV) * HEAD_DIM:(j % N_KV + 1) * HEAD_DIM]
                             ).then_inc(v_spread, 16)

        @block.gpsimd
        def _(pool):
            pool.memset(vx, 0.0).then_inc(v_clear, 1)

        @block.tensor
        def _(pe):
            pe.wait_ge(masks_cast, 3)
            pe.wait_ge(k_lo_done, N_KV)
            pe.wait_ge(v_spread, 16 * HT * N_KV)
            with pe.Fori(0, KA) as i:
                def qk(u):
                    t, h, br = units[u]
                    if u == 0:
                        pe.wait_ge(q_doubled, i * 2 + 2)
                        pe.wait_ge(q_lo_done, i * 2 + 2)
                    if u >= 2:
                        pe.wait_ge(probs_ready, i * U + u - 1)
                    k0, n, at = tiles_of[u][0] * P, len(tiles_of[u]) * P, place[u]
                    tile = slice(t * P, (t + 1) * P)
                    masks = {n - P: diag_b}
                    if br == 2 and t >= WT:
                        masks[0] = tail_b
                    for a, b in ([(0, max(n, 2 * P))] if n <= 512 else [(0, n // 2), (n // 2, n)]):
                        held = [(x, m) for x, m in masks.items() if a <= x < b]
                        keys = slice(k0 + a, k0 + b)
                        pe.matmul(psum[:, at + a:at + b], lhsT=QD[h][:, tile], rhs=KS[h][:, br - 1, keys],
                                  start=True, stop=False, skip_group_check=True)
                        m = pe.matmul(psum[:, at + a:at + b], lhsT=QL[own[h], tile], rhs=KS[h][own[h], br - 1, keys],
                                      start=False, stop=not held, skip_group_check=True)
                        for x, mask in held:
                            m = pe.matmul(psum[:, at + x:at + x + P], lhsT=ident_b[:, :], rhs=mask[:, :],
                                          start=False, stop=(x, mask) == held[-1], skip_group_check=True)
                    m.then_inc(scored, 1)

                def turn(u):
                    pe.wait_ge(probs_ready, i * U + u + 1)
                    n = len(tiles_of[u])
                    if u >= 1:
                        pe.wait_ge(copied0, i * U + u)
                    for j in range(min(n, 4)):
                        m = pe.transpose(ps[4][:, j * P:(j + 1) * P], probs[u % 2][:, j * P:(j + 1) * P], ident[:, :])
                    m.then_inc(turned0, 1)
                    if second[u]:
                        if upto[u] >= 2:
                            pe.wait_ge(copied1, i * C1 + upto[u] - 1)
                        for j in range(4, n):
                            m = pe.transpose(ps[5][:, (j - 4) * P:(j - 3) * P], probs[u % 2][:, j * P:(j + 1) * P], ident[:, :])
                        m.then_inc(turned1, 1)

                def pv(u):
                    t, h, br = units[u]
                    pe.wait_ge(copied0, i * U + u + 1)
                    if second[u]:
                        pe.wait_ge(copied1, i * C1 + upto[u])
                    if u >= 2:
                        pe.wait_ge(merged, i * U + u - 1)
                    elif u == 0:
                        pe.wait_ge(cmp_merged, i * 2 + 2)
                    col = 2 * KV_WIDTH * br + KV_WIDTH + h * HEAD_DIM
                    for j, kt in enumerate(tiles_of[u]):
                        m = pe.matmul(ps[6 + u % 2][:, 0:HEAD_DIM], lhsT=pT[u % 2][:, j * P:(j + 1) * P],
                                      rhs=kvn[:, kt, col:col + HEAD_DIM], start=(j == 0), stop=(j == len(tiles_of[u]) - 1))
                    m.then_inc(out_summed, 1)

                pe.wait_ge(staged, i * 2 + 2)
                for t in range(TILES):
                    for h in range(N_KV):
                        m = pe.matmul(ps[6][:, (t * N_KV + h) * NBP:(t * N_KV + h + 1) * NBP], lhsT=QC[h][:, t * P:(t + 1) * P],
                                      rhs=ck_p[:, :], start=True, stop=True)
                m.then_inc(cmp_scored, 1)
                qk(0)
                qk(1)
                pe.wait_ge(cmp_probs, i + 1)
                flat = cs[:, :, :, :].rearrange("p t h n -> p (t h n)")
                for j in range(2):
                    m = pe.transpose(ps[7][:, j * P:(j + 1) * P], flat[:, j * P:(j + 1) * P], ident[:, :])
                m.then_inc(cmp_turned, 1)
                pe.wait_ge(cmp_copied, i + 1)
                for j in range(2):
                    pe.matmul(ps[6 + j][:, :], lhsT=cT[:, j, :], rhs=vx.rearrange("p j n -> p (j n)"), start=True,
                              stop=True).then_inc(cmp_summed, 1)
                for u in range(2, U + 3):
                    if u < U:
                        qk(u)
                    if u < U + 2:
                        turn(u - 2)
                    if u >= 3:
                        pv(u - 3)

        @block.scalar
        def _(act):
            for h in range(N_KV):
                split_hi(act, KS[h][own[h], :, :], kT[own[h], :, 0:SEQ]).then_inc(k_hi_done, 1)
            with act.Fori(0, KA) as i:
                def exp(u):
                    act.wait_ge(max_ready, i * U + u + 1)
                    if u >= 2:
                        act.wait_ge(turned0, i * U + u - 1)
                        if second[u - 2]:
                            act.wait_ge(turned1, i * C1 + upto[u - 2])
                    n = len(tiles_of[u]) * P
                    if u >= 4:
                        act.wait_ge(merged, i * U + u - 3)
                    act.activation(probs[u % 2][:, 0:n], psum[:, place[u]:place[u] + n], ACT.Exp,
                                   bias=nmax[:, u % 4:u % 4 + 1], accum_out=den[:, u % 4:u % 4 + 1]).then_inc(probs_ready, 1)

                def copy(u):
                    act.wait_ge(turned0, i * U + u + 1)
                    if u >= 2:
                        act.wait_ge(out_summed, i * U + u - 1)
                    n = min(len(tiles_of[u]), 4) * P
                    act.activation(pT[u % 2][:, 0:n], ps[4][:, 0:n], ACT.Copy).then_inc(copied0, 1)

                for h in range(N_KV):
                    act.wait_ge(q_hi_done, i * 2 + h + 1)
                    act.activation(QD[h][own[1 - h], :], QD[h][own[h], :].bitcast(F32), ACT.Copy).then_inc(q_doubled, 1)
                act.wait_ge(cmp_shifted, i + 1)
                act.activation(cs[:, :, :, :], cs[:, :, :, :], ACT.Exp).then_inc(cmp_exp, 1)
                for u in range(U + 2):
                    if u >= 2:
                        copy(u - 2)
                    if u < U:
                        exp(u)

        @block.vector
        def _(dve):
            s = Steps(dve, stepped)
            for h in range(N_KV):
                other = slice((1 - h) * HEAD_DIM, (2 - h) * HEAD_DIM)
                s.done(dve.memset(QC[h][other, :], 0.0))
            s.fence()
            for h in range(N_KV):
                dve.wait_ge(k_hi_done, h + 1)
                split_lo(dve, KS[h][own[1 - h], :, :], kT[own[h], :, 0:SEQ], KS[h][own[h], :, :]).then_inc(k_lo_done, 1)
            dve.wait_ge(masks_loaded, 48)
            for dst, src in ((diag_b, diag), (tail_b, tail), (ident_b, ident)):
                dve.tensor_copy(dst[:, :], src[:, :]).then_inc(masks_cast, 1)
            per = 2 + 7 + 2 * U
            with dve.Fori(0, KA) as i:
                s.enter(i, per)

                def top(u):
                    dve.wait_ge(scored, i * U + u + 1)
                    if u >= 4:
                        dve.wait_ge(probs_ready, i * U + u - 3)
                    n = len(tiles_of[u]) * P
                    dve.tensor_reduce(nmax[:, u % 4:u % 4 + 1], psum[:, place[u]:place[u] + n], AX, ALU.max,
                                      negate=True).then_inc(max_ready, 1)

                def copy(u):
                    if second[u]:
                        dve.wait_ge(turned1, i * C1 + upto[u])
                        if u >= 2:
                            dve.wait_ge(out_summed, i * U + u - 1)
                        n = len(tiles_of[u]) * P
                        dve.tensor_copy(pT[u % 2][:, 512:n], ps[5][:, 0:n - 512]).then_inc(copied1, 1)

                def merge(u):
                    t, h, br = units[u]
                    j = slice(u % 4, u % 4 + 1)
                    dve.wait_ge(probs_ready, i * U + u + 1)
                    s.then(dve.reciprocal(coef[:, j], den[:, j]))
                    s.then(dve.tensor_tensor(coef[:, j], coef[:, j], gsel[:, t, br, h:h + 1], ALU.mult))
                    dve.wait_ge(out_summed, i * U + u + 1)
                    out = attn[:, t, ds(i * HEAD_DIM + h * GROUP * HEAD_DIM, HEAD_DIM)]
                    if u:
                        dve.wait_ge(merged, i * U + u)
                    dve.scalar_tensor_tensor(out, ps[6 + u % 2][:, 0:HEAD_DIM], coef[:, j], out, ALU.mult, ALU.add
                                             ).then_inc(merged, 1)

                for h in range(N_KV):
                    dve.tensor_scalar(QC[h][own[h], :], qT[own[h], ds(i, 1), 0:SEQ].rearrange("p a n -> p (a n)"), SCALE,
                                      None, ALU.mult).then_inc(staged, 1)
                for h in range(N_KV):
                    q = qR[own[h], ds(i, 1), 0:SEQ].rearrange("p a n -> p (a n)")
                    dve.tensor_scalar(QD[h][own[h], :], q, SCALE, None, ALU.mult).then_inc(q_hi_done, 1)
                for h in range(N_KV):
                    q = qR[own[h], ds(i, 1), 0:SEQ].rearrange("p a n -> p (a n)")
                    dve.wait_ge(q_hi_done, i * 2 + h + 1)
                    dve.scalar_tensor_tensor(QL[own[h], :], q, SCALE, QD[h][own[h], :].bitcast(F32), ALU.mult, ALU.subtract
                                             ).then_inc(q_lo_done, 1)
                for h in range(N_KV):
                    s.done(dve.tensor_copy(gsel[:, :, :, h], gates[:, 0:TILES, :].rearrange("p t (b h) -> p t b h", b=3)[
                        :, :, :, ds(i + h * GROUP, 1)].rearrange("p t b h -> p t (b h)")))
                dve.wait_ge(cmp_scored, i + 1)
                scores = ps[6][:, 0:TILES * N_KV * NBP].rearrange("p (t h n) -> p t h n", h=N_KV, n=NBP)
                s.then(dve.tensor_tensor(cs[:, :, :, :], scores, bcast(cmask, 2, N_KV), ALU.add))
                s.then(dve.tensor_reduce(cst[:, 0, :, :], cs[:, :, :, :], AX, ALU.max))
                s.then(dve.tensor_scalar(cst[:, 0, :, :], cst[:, 0, :, :], -1e29, None, ALU.max))
                dve.tensor_tensor(cs[:, :, :, :], cs[:, :, :, :], bcast(cst[:, 0, :, :], 3, NBP), ALU.subtract
                                  ).then_inc(cmp_shifted, 1)
                dve.wait_ge(cmp_exp, i + 1)
                s.then(dve.tensor_reduce(cst[:, 1, :, :], cs[:, :, :, :], AX, ALU.add))
                s.then(dve.tensor_scalar(cst[:, 1, :, :], cst[:, 1, :, :], 1e-30, None, ALU.max))
                s.then(dve.reciprocal(cst[:, 1, :, :], cst[:, 1, :, :]))
                s.then(dve.tensor_tensor(cst[:, 1, :, :], cst[:, 1, :, :], gsel[:, :, 0, :], ALU.mult))
                dve.tensor_tensor(cs[:, :, :, :], cs[:, :, :, :], bcast(cst[:, 1, :, :], 3, NBP), ALU.mult
                                  ).then_inc(cmp_probs, 1)
                top(0)
                top(1)
                dve.wait_ge(cmp_turned, i + 1)
                dve.tensor_copy(cT[:, :, :], ps[7][:, 0:2 * P].rearrange("p (a n) -> p a n", a=2)).then_inc(cmp_copied, 1)
                for j in range(2):
                    dve.wait_ge(cmp_summed, i * 2 + j + 1)
                    for h in range(N_KV):
                        r = dve.tensor_copy(attn[:, j * HT:(j + 1) * HT, ds(i * HEAD_DIM + h * GROUP * HEAD_DIM, HEAD_DIM)],
                                            ps[6 + j][:, :].rearrange("p (t h n) -> p t h n", h=N_KV, n=HEAD_DIM)[:, :, h, :])
                        r.then_inc(cmp_merged if h else merged_half, 1)
                dve.wait_ge(cmp_merged, i * 2 + 2)
                dve.wait_ge(merged_half, i * 2 + 2)
                for u in range(2, U + 3):
                    if u < U:
                        top(u)
                    if u < U + 2:
                        copy(u - 2)
                    if u >= 3:
                        merge(u - 3)
                s.leave(KA)
            dve.wait_ge(merged, KA * U)


def sample_attention(k, q_plain, q_rot, k_new, v_new, gate_rows, ck_s, cv_s, page_parts, attn, ident, space, win_space,
                     score_space):
    nc, ps, d = k.nc, k.ps, k.dram
    (masks_loaded, kv_loaded, win_loaded, consts_set, misc_summed, misc_taken, k_turned, k_copied_v, k_copied_a, k_used,
     chunk_taken, exp_ready, exp_done, cmp_norm, probs_scaled, p_turned, p_copied_v, p_copied_a, p_used, kv_used, opened, out_done,
     out_taken, out_stored, out_back, stepped) = k.sems(" ".join("s7_" + n for n in (
         "masks_loaded kv_loaded win_loaded consts_set misc_summed misc_taken k_turned k_copied_v k_copied_a k_used "
         "chunk_taken exp_ready exp_done cmp_norm probs_scaled p_turned p_copied_v p_copied_a p_used kv_used opened out_done "
         "out_taken out_stored out_back stepped").split()))
    NS, NW = PAST_LEN + RS, WINDOW + RS
    CH = 5
    UN = CH * BT
    TURNS = [("cmp", 0, 0, False), ("win", 0, 4, False), ("win", 4, 1, True)] + [
        ("sel", 4 * j, 4, False) for j in range(4)] + [("sel", 16, 1, True)]
    NT = len(TURNS)
    SLOTTED = [0, 1, 2, NT - 1]
    NU = len(SLOTTED)
    MISC = 4
    runs = d["cache_sel_kv"][0].rearrange("a (r t) c h d -> (a r) (t c h d)", t=TP)
    with ExitStack() as st:
        kv = sb(nc, st, "past_kv", [P, BT, TP, 2 * KV_WIDTH])
        wkv = win_space[:, 0:BT * WP * 2 * KV_WIDTH].rearrange("p (b t n) -> p b t n", b=BT, t=WP)
        kTs = [sb(nc, st, f"kTs{j}", [P, 512]) for j in range(4)]
        sel, win = score_space[:, 0:NS], score_space[:, NS:NS + NW]
        cmp_ = sb(nc, st, "cmp_scores", [P, NBS])
        cmp_g = sb(nc, st, "cmp_gated", [P, NBS])
        pT = [score_space[:, NS + NW + j * 4 * P:NS + NW + (j + 1) * 4 * P].rearrange("p (t n) -> p t n", t=4)
              for j in range(2)]
        zero = sb(nc, st, "s_zero", [P, QR])
        mask_new = sb(nc, st, "mask_new", [P, SG, RS])
        at = NS + NW + 2 * 4 * P
        mask_win = score_space[:, at:at + WP * P]
        square = NCAND * NCAND
        earlier = space[:, 0:square].rearrange("p (a b) -> p a b", a=NCAND)
        ranks = space[:, square:3 * square].rearrange("p (x a b) -> p x a b", x=2, a=NCAND)
        same = space[:, 3 * square:3 * square + P]
        out = space[0:QR, 3 * square + P:3 * square + P + 512]
        imp = sb(nc, st, "importance", [P, NBS])
        rank = sb(nc, st, "rank", [P, NCAND])
        unselected = sb(nc, st, "unselected", [P, NBS])
        stat = sb(nc, st, "s_stat", [P, 3, 3])
        block = st.enter_context(nc.Block())
        rows_of = {"cmp": cmp_g, "win": win, "sel": sel}

        def unit(w):
            return w // BT, w % BT

        def copied(eng, count_v, count_a, n, base):
            eng.wait_ge(count_a if n % 2 else count_v, base + n // 2 + 1)

        @block.sync
        def _(sp):
            for dst, name in ((mask_new[:, :, :].rearrange("p g n -> p (g n)"), "mask_new"), (mask_win[:, :], "mask_win"),
                              (same, "same_query"), (space[:, 0:square], "earlier")):
                sp.dma_start(dst, d[name]).then_inc(masks_loaded, 16)
            def load_window(g):
                if g:
                    sp.wait_ge(p_used, NU * (g - 1) + 3)
                for b in range(BT):
                    sp.dma_start(wkv[:, b, :, :], d["state_win_kv"][0, g * BT + b].rearrange("(p t) c h d -> p t (c h d)", p=P)
                                 ).then_inc(win_loaded, 16)
            load_window(0)
            for g in range(SG):
                if g + 1 < SG:
                    load_window(g + 1)
                sp.wait_ge(out_taken, g + 1)
                sp.dma_start(d["attn_scratch"][g].rearrange("r b n -> r (b n)"), out).then_inc(out_stored, 16)
                sp.wait_ge(out_stored, 16 * (g + 1))
                for b in range(BT):
                    for h in range(N_KV):
                        src = d["attn_scratch"][g, h * DEC_SEQ * GROUP:(h + 1) * DEC_SEQ * GROUP, b,
                                                h * HEAD_DIM:(h + 1) * HEAD_DIM].rearrange("(s q) n -> s q n", q=GROUP)
                        row = (g * BT + b) * DEC_SEQ
                        sp.dma_start(attn[row:row + DEC_SEQ, TILES, h * GROUP * HEAD_DIM:(h + 1) * GROUP * HEAD_DIM].rearrange(
                            "s (q n) -> s q n", q=GROUP), src).then_inc(out_back, 16)
            sp.wait_ge(out_back, 16 * SG * BT * N_KV)

        @block.gpsimd
        def _(pool):
            pool.memset(zero[:, :], 0.0).then_inc(consts_set, 1)
            for g in range(SG):
                for b in range(BT):
                    n = g * BT + b
                    if g:
                        pool.wait_ge(kv_used, n - BT + 1)
                    pool.indirect_dma_start(kv[:, b, :, :].rearrange("p t n -> p (t n)"), None, runs,
                                            bass.IndirectOffsetOnAxis(ap=page_parts[:, n:n + 1], axis=0)).then_inc(kv_loaded, 16)
            pool.wait_ge(kv_loaded, 16 * DEC_BATCH)

        @block.tensor
        def _(pe):
            pe.wait_ge(consts_set, 1)
            pe.wait_ge(masks_loaded, 64)
            for g in range(SG):
                def misc(m, product):
                    if g * MISC + m:
                        pe.wait_ge(misc_taken, g * MISC + m)
                    product().then_inc(misc_summed, 1)

                def over_samples(rhs_of, lhs, cols):
                    def product():
                        for b in range(BT):
                            r = pe.matmul(ps[7][:, 0:cols], lhsT=lhs[:, g * BT + b, :], rhs=rhs_of(b), start=(b == 0),
                                          stop=(b == BT - 1))
                        return r
                    return product

                def turn_k(w):
                    c, b = unit(w)
                    n = g * UN + w
                    if n >= 2:
                        copied(pe, k_copied_v, k_copied_a, n - 2, 0)
                    if w == 0:
                        pe.wait_ge(win_loaded, 16 * BT * (g + 1))
                    if w == BT:
                        pe.wait_ge(kv_loaded, 16 * BT * (g + 1))
                    src = wkv if c == 0 else kv
                    for j in range(4):
                        m = pe.transpose(ps[2 + n % 2][:, j * P:(j + 1) * P], src[:, b, (max(c - 1, 0) * 4 + j), 0:KV_WIDTH],
                                         ident[:, :])
                    m.then_inc(k_turned, 1)

                def score(w):
                    c, b = unit(w)
                    n = g * UN + w
                    at = g * CH + c
                    copied(pe, k_copied_v, k_copied_a, n, 0)
                    if b == 0 and at >= 2:
                        pe.wait_ge(chunk_taken, at - 1)
                    pe.matmul(ps[at % 2][:, :], lhsT=q_rot[:, g * BT + b, :], rhs=kTs[n % 4][:, :], start=(b == 0),
                              stop=(b == BT - 1)).then_inc(k_used, 1)

                def turn_p(j):
                    br, tile, count, new = TURNS[j]
                    n = g * NT + j
                    if n >= 2:
                        copied(pe, p_copied_v, p_copied_a, n - 2, 0)
                    if br == "cmp":
                        m = pe.transpose(ps[4 + n % 2][0:NBS, 0:P], cmp_g[:, :], ident[:, :])
                    elif new:
                        m = pe.transpose(ps[4 + n % 2][0:RS, 0:P], rows_of[br][:, tile * P:tile * P + RS], ident[:, :])
                    else:
                        for i in range(count):
                            m = pe.transpose(ps[4 + n % 2][:, i * P:(i + 1) * P], rows_of[br][:, (tile + i) * P:(tile + i + 1) * P],
                                             ident[:, :])
                    m.then_inc(p_turned, 1)

                def pv(j):
                    br, tile, count, new = TURNS[j]
                    n = g * NT + j
                    copied(pe, p_copied_v, p_copied_a, n, 0)
                    for i in range(max(count, 1)):
                        for b in range(BT):
                            col = slice(b * QR, (b + 1) * QR)
                            if br == "cmp":
                                lhs, rhs = pT[n % 2][0:NBS, 0, col], cv_s[:, g * BT + b, :]
                            elif new:
                                lhs, rhs = pT[n % 2][0:RS, 0, col], v_new[:, 0 if br == "sel" else 1, :]
                            else:
                                lhs, rhs = pT[n % 2][:, i, col], wkv[:, b, tile + i, KV_WIDTH:2 * KV_WIDTH]
                            m = pe.matmul(ps[6][0:QR, b * P:(b + 1) * P], lhsT=lhs, rhs=rhs, start=False, stop=False,
                                          skip_group_check=True)
                    m.then_inc(p_used, 1)

                def pv_past(b):
                    for i in range(TP):
                        m = pe.matmul(ps[6][0:QR, b * P:(b + 1) * P], lhsT=sel[:, i * P + b * QR:i * P + (b + 1) * QR],
                                      rhs=kv[:, b, i, KV_WIDTH:2 * KV_WIDTH], start=False, stop=False, skip_group_check=True)
                    m.then_inc(kv_used, 1)

                def units(a, b):
                    turn_k(a)
                    for w in range(a, b):
                        if w + 1 < b:
                            turn_k(w + 1)
                        score(w)

                if g:
                    pe.wait_ge(out_taken, g)
                pe.matmul(ps[6][0:QR, :], lhsT=zero[:, :], rhs=mask_win[:, :], start=True, stop=False, skip_group_check=True
                          ).then_inc(opened, 1)
                misc(0, over_samples(lambda b: ck_s[:, (g * BT + b) * NBS:(g * BT + b + 1) * NBS], q_plain, NBS))
                units(0, BT)
                misc(1, over_samples(lambda b: k_new[:, 1, :], q_rot, RS))
                pe.wait_ge(cmp_norm, g + 1)
                misc(2, lambda: pe.matmul(ps[7][:, 0:NBS], lhsT=same, rhs=cmp_[:, :], start=True, stop=True))
                pe.wait_ge(probs_scaled, 3 * g + 1)
                turn_p(0)
                units(BT, UN)
                misc(3, over_samples(lambda b: k_new[:, 0, :], q_rot, RS))
                pv(0)
                pe.wait_ge(probs_scaled, 3 * g + 2)
                turn_p(1)
                turn_p(2)
                pv(1)
                pv(2)
                pe.wait_ge(probs_scaled, 3 * g + 3)
                turn_p(3)
                for j in range(4, NT):
                    turn_p(j)
                pv(NT - 1)
                copied(pe, p_copied_v, p_copied_a, g * NT + NT - 2, 0)
                for b in range(BT):
                    pv_past(b)
                pe.matmul(ps[6][0:QR, :], lhsT=zero[:, :], rhs=mask_win[:, :], start=False, stop=True, skip_group_check=True
                          ).then_inc(out_done, 1)

        def copy_k(eng, copy, count, g, w):
            n = g * UN + w
            eng.wait_ge(k_turned, n + 1)
            if n >= 4:
                eng.wait_ge(k_used, n - 3)
            copy(kTs[n % 4][:, :], ps[2 + n % 2]).then_inc(count, 1)

        def copy_p(eng, copy, count, g, j):
            n = g * NT + j
            br, tile, c, new = TURNS[j]
            eng.wait_ge(p_turned, n + 1)
            if j in SLOTTED and g * NU + SLOTTED.index(j) >= 2:
                eng.wait_ge(p_used, g * NU + SLOTTED.index(j) - 1)
            if j not in SLOTTED:
                copy(sel[:, tile * P:(tile + c) * P], ps[4 + n % 2]).then_inc(count, 1)
            elif br == "cmp" or new:
                copy(pT[n % 2][0:RS, 0, :], ps[4 + n % 2][0:RS, 0:P]).then_inc(count, 1)
            else:
                copy(pT[n % 2][:, :, :], ps[4 + n % 2].rearrange("p (a n) -> p a n", a=4)).then_inc(count, 1)

        @block.scalar
        def _(act):
            def copy(o, x):
                return act.activation(o, x, ACT.Copy)

            for g in range(SG):
                def exp(j, rows):
                    act.wait_ge(exp_ready, 3 * g + j + 1)
                    act.activation(rows, rows, ACT.Exp, bias=stat[:, j, 0:1], scale=SCALE, accum_out=stat[:, j, 1:2]
                                   ).then_inc(exp_done, 1)
                exp(0, cmp_[:, :])
                for w in (1, 3):
                    copy_k(act, copy, k_copied_a, g, w)
                exp(1, win[:, :])
                for w in range(BT + 1, UN, 2):
                    copy_k(act, copy, k_copied_a, g, w)
                exp(2, sel[:, :])
                for j in range(NT):
                    if j % 2:
                        copy_p(act, copy, p_copied_a, g, j)

        @block.vector
        def _(dve):
            s = Steps(dve, stepped)
            dve.wait_ge(masks_loaded, 64)
            for g in range(SG):
                def take_misc(m, op):
                    dve.wait_ge(misc_summed, g * MISC + m + 1)
                    op().then_inc(misc_taken, 1)
                    dve.wait_ge(misc_taken, g * MISC + m + 1)

                def top(j, rows):
                    s.then(dve.tensor_reduce(stat[:, j, 0:1], rows, AX, ALU.max))
                    dve.tensor_scalar(stat[:, j, 0:1], stat[:, j, 0:1], -SCALE, None, ALU.mult).then_inc(exp_ready, 1)

                def weight(j, gate, rows, dst):
                    s.then(dve.reciprocal(stat[:, j, 2:3], stat[:, j, 1:2]))
                    if j == 0:
                        dve.tensor_scalar(cmp_[:, :], cmp_[:, :], stat[:, j, 2:3], None, ALU.mult).then_inc(cmp_norm, 1)
                        dve.wait_ge(cmp_norm, g + 1)
                        dve.tensor_scalar(dst, rows, gate_rows[:, g, gate:gate + 1], None, ALU.mult).then_inc(probs_scaled, 1)
                    else:
                        s.then(dve.tensor_tensor(stat[:, j, 2:3], stat[:, j, 2:3], gate_rows[:, g, gate:gate + 1], ALU.mult))
                        dve.tensor_scalar(dst, rows, stat[:, j, 2:3], None, ALU.mult).then_inc(probs_scaled, 1)

                def take_chunk(c):
                    at = g * CH + c
                    dve.wait_ge(k_used, g * UN + BT * (c + 1))
                    bank = ps[at % 2]
                    if c == 0:
                        dve.tensor_tensor(win[:, 0:WINDOW], bank, mask_win[:, :], ALU.add).then_inc(chunk_taken, 1)
                    else:
                        lay = "p (t k r) -> p t k r"
                        dve.tensor_tensor(sel[:, (c - 1) * 512:c * 512].rearrange(lay, t=4, r=4), bank.rearrange(lay, t=4, r=4),
                                          bcast(bcast(unselected[:, :], 1, 4), 3, 4), ALU.add).then_inc(chunk_taken, 1)

                if g:
                    dve.wait_ge(p_turned, NT * g)
                take_misc(0, lambda: dve.tensor_copy(cmp_[:, :], ps[7][:, 0:NBS]))
                top(0, cmp_[:, :])
                dve.wait_ge(exp_done, 3 * g + 1)
                weight(0, 0, cmp_[:, :], cmp_g[:, :])
                for w in (0, 2):
                    copy_k(dve, dve.tensor_copy, k_copied_v, g, w)
                take_chunk(0)
                take_misc(1, lambda: dve.tensor_tensor(win[:, WINDOW:NW], ps[7][:, 0:RS], mask_new[:, g, :], ALU.add))
                dve.wait_ge(chunk_taken, g * CH + 1)
                top(1, win[:, :])
                take_misc(2, lambda: dve.tensor_copy(imp[:, :], ps[7][:, 0:NBS]))
                cand = imp[:, 1:1 + NCAND]
                a, b = bcast(cand, 1, NCAND), bcast(cand, 2, NCAND)
                s.done(dve.tensor_tensor(ranks[:, 0, :, :], a, b, ALU.is_gt))
                s.then(dve.tensor_tensor(ranks[:, 1, :, :], a, b, ALU.is_equal))
                s.then(dve.tensor_tensor(ranks[:, 1, :, :], ranks[:, 1, :, :], earlier[:, :, :], ALU.mult))
                s.then(dve.tensor_tensor(ranks[:, 0, :, :], ranks[:, 0, :, :], ranks[:, 1, :, :], ALU.add))
                s.done(dve.memset(unselected[:, :], 0.0))
                s.then(dve.tensor_reduce(rank[:, :], ranks[:, 0, :, :], AX, ALU.add))
                s.then(dve.tensor_scalar(unselected[:, 1:1 + NCAND], rank[:, :], float(NFREE), NEG, ALU.is_ge, ALU.mult))
                if g:
                    dve.wait_ge(kv_used, BT * g)
                for w in range(BT, UN):
                    if w % 2 == 0:
                        copy_k(dve, dve.tensor_copy, k_copied_v, g, w)
                    if w % BT == BT - 1:
                        take_chunk(w // BT)
                take_misc(3, lambda: dve.tensor_tensor(sel[:, PAST_LEN:NS], ps[7][:, 0:RS], mask_new[:, g, :], ALU.add))
                dve.wait_ge(exp_done, 3 * g + 2)
                weight(1, 2, win[:, :], win[:, :])
                dve.wait_ge(chunk_taken, (g + 1) * CH)
                top(2, sel[:, :])
                dve.wait_ge(exp_done, 3 * g + 3)
                weight(2, 1, sel[:, :], sel[:, :])
                for j in range(0, NT, 2):
                    copy_p(dve, dve.tensor_copy, p_copied_v, g, j)
                dve.wait_ge(out_done, g + 1)
                if g:
                    dve.wait_ge(out_stored, 16 * g)
                dve.tensor_copy(out, ps[6][0:QR, :]).then_inc(out_taken, 1)


def turn_attention(k, attn, merged, ident):
    nc, ps = k.nc, k.ps
    turned, copied_v, copied_a = k.sems("s8_turned s8_copied_v s8_copied_a")
    with nc.Block() as block:
        @block.tensor
        def _(pe):
            for t in range(TILES + 1):
                n = min(P, ROWS - t * P)
                if t >= 4:
                    pe.wait_ge(copied_a if t % 2 else copied_v, (t - 4) // 2 + 1)
                for c in range(KA):
                    m = pe.transpose(ps[t % 4][:, c * P:c * P + n], attn[0:n, t, c * P:(c + 1) * P], ident[0:n, 0:n])
                m.then_inc(turned, 1)

        def copy(eng, op, count, odd):
            for t in range(odd, TILES + 1, 2):
                n = min(P, ROWS - t * P)
                eng.wait_ge(turned, t + 1)
                op(merged[:, KR:KR + KA, t * P:t * P + n], ps[t % 4].rearrange("p (c n) -> p c n", c=KA)[:, :, 0:n]
                   ).then_inc(count, 1)

        @block.vector
        def _(dve):
            copy(dve, dve.tensor_copy, copied_v, 0)

        @block.scalar
        def _(act):
            copy(act, lambda o, x: act.activation(o, x, ACT.Copy), copied_a, 1)


def add_gated(xT, gate):
    def take(dve, s, i, p, banks, tmp):
        for g in range(NG):
            (a, b), rest = prompt_split(g)
            o = xT[:, ds(i * 2 + p, 1), a:b].rearrange("p a n -> p (a n)")
            s.done(dve.scalar_tensor_tensor(o, banks[g][:, 0:b - a], gate[:, ds(i * 2 + p, 1), 0:1].rearrange("p a n -> p (a n)"),
                                            o, ALU.mult, ALU.add))
            if rest:
                r0 = rest[0] - g * GR
                s.then(dve.tensor_tensor(tmp.rearrange("p (b s) -> p b s", s=DEC_SEQ),
                                         banks[g][:, r0:GR].rearrange("p (b s) -> p b s", s=DEC_SEQ),
                                         bcast(gate[:, ds(i * 2 + p, 1), 1:COND].rearrange("p a n -> p (a n)"), 2, DEC_SEQ),
                                         ALU.mult))
                o = xT[:, ds(i * 2 + p, 1), rest[0]:rest[1]].rearrange("p a n -> p (a n)")
                r = dve.tensor_tensor(o, o, tmp, ALU.add)
        return r
    take.n_loads, take.per = 1, 2 * (NG + 1)
    return take


def ffn_up(k, hT, hidden, space):
    nc, ps, d = k.nc, k.ps, k.dram
    loaded0, loaded1, used0, used1, gate_summed, summed, silu_done, taken = k.sems(
        "s11_loaded0 s11_loaded1 s11_used0 s11_used1 s11_gate_summed s11_summed s11_silu_done s11_taken")
    loaded, used = [loaded0, loaded1], [used0, used1]
    TRIPS = KF // 2
    BODY = 2 * NG
    views = [d[n][0].rearrange("(k p) n -> p k n", p=P) for n in ("w_gate", "w_up")]
    with ExitStack() as st:
        w = [[sb(nc, st, f"w_ff{j}_{p}", [P, KD, P]) for j in range(2)] for p in range(2)]
        act_g = [space[:, g, 0:GR] for g in range(NG)]
        block = st.enter_context(nc.Block())

        @block.sync
        def _(sp):
            with sp.Fori(0, TRIPS) as i:
                for p in range(2):
                    sp.wait_ge(used[p], i + 1)
                    for j in range(2):
                        sp.dma_start(w[p][j][:, :, :], views[j][:, :, ds(i * (2 * P) + p * P, P)]).then_inc(loaded[p], 16)

        @block.tensor
        def _(pe):
            pe.sem_inc(used[0], 1)
            pe.sem_inc(used[1], 1)
            with pe.Fori(0, TRIPS) as i:
                for p in range(2):
                    pe.wait_ge(loaded[p], i * 32 + 32)
                    for g in range(NG):
                        pe.wait_ge(taken, i * BODY + p * NG + g + 1)
                        for j in range(2):
                            for c in range(KD):
                                m = pe.matmul(ps[2 * g + j][:, 0:GR], lhsT=w[p][j][:, c, :], rhs=hT[:, c, g * GR:(g + 1) * GR],
                                              start=(c == 0), stop=(c == KD - 1))
                            if not j:
                                m.then_inc(gate_summed, 1)
                            elif g < NG - 1:
                                m.then_inc(summed, 1)
                    m.then_inc(used[p], 1)

        @block.scalar
        def _(act):
            with act.Fori(0, TRIPS) as i:
                for p in range(2):
                    for g in range(NG):
                        n = p * NG + g
                        act.wait_ge(gate_summed, i * BODY + n + 1)
                        act.wait_ge(taken, i * BODY + n + 1)
                        act.activation(act_g[g], ps[2 * g][:, 0:GR], ACT.Silu).then_inc(silu_done, 1)

        @block.vector
        def _(dve):
            dve.sem_inc(taken, NG)
            with dve.Fori(0, TRIPS) as i:
                for p in range(2):
                    for g in range(NG):
                        n = p * NG + g
                        dve.wait_ge(silu_done, i * BODY + n + 1)
                        if g < NG - 1:
                            dve.wait_ge(summed, i * (2 * (NG - 1)) + p * (NG - 1) + g + 1)
                        else:
                            dve.wait_ge(used[p], i + 2)
                        dve.tensor_tensor(hidden[:, ds(i * 2 + p, 1), g * GR:(g + 1) * GR], act_g[g].unsqueeze(1),
                                          ps[2 * g + 1][:, 0:GR].unsqueeze(1), ALU.mult).then_inc(taken, 1)
            dve.wait_ge(taken, NG + TRIPS * BODY)


def store_rows(k, yT, ident, win_copied):
    nc, ps, d = k.nc, k.ps, k.dram
    turned, copied_v, copied_a, *rows_stored = k.sems("s14_turned s14_copied_v s14_copied_a s14_stored0 s14_stored1 s14_stored2 s14_stored3")
    with ExitStack() as st:
        y = [sb(nc, st, f"y{j}", [P, D_MODEL]) for j in range(4)]
        block = st.enter_context(nc.Block())

        @block.tensor
        def _(pe):
            for t in range(TILES + 1):
                n = min(P, ROWS - t * P)
                for h in range(2):
                    step = 2 * t + h
                    if step >= 8:
                        pe.wait_ge(copied_a if h else copied_v, (step - 8) // 2 + 1)
                    for c in range(4):
                        m = pe.transpose(ps[step % 8][0:n, c * P:(c + 1) * P], yT[:, 4 * h + c, t * P:t * P + n], ident[:, :])
                    m.then_inc(turned, 1)

        def copy(eng, op, count, h):
            for t in range(TILES + 1):
                n = min(P, ROWS - t * P)
                eng.wait_ge(turned, 2 * t + h + 1)
                if t >= 4:
                    eng.wait_ge(rows_stored[t % 4], 16 * (t // 4))
                op(y[t % 4][0:n, h * 512:(h + 1) * 512], ps[(2 * t + h) % 8][0:n, :]).then_inc(count, 1)

        @block.vector
        def _(dve):
            copy(dve, dve.tensor_copy, copied_v, 0)

        @block.scalar
        def _(act):
            copy(act, lambda o, x: act.activation(o, x, ACT.Copy), copied_a, 1)

        @block.sync
        def _(sp):
            for t in range(TILES + 1):
                n = min(P, ROWS - t * P)
                sp.wait_ge(copied_v, t + 1)
                sp.wait_ge(copied_a, t + 1)
                dst = d["y_prompt"][0, t * P:(t + 1) * P, :] if t < TILES else d["y_sample"].rearrange("b s n -> (b s) n")
                sp.dma_start(dst, y[t % 4][0:n, :]).then_inc(rows_stored[t % 4], 16)
            for j in range(4):
                sp.wait_ge(rows_stored[j], 16 * ((TILES - j) // 4 + 1))
            sp.wait_ge(win_copied, 16)




def split_hi(act, hi, raw):
    return act.activation(hi, raw, ACT.Copy)


def split_lo(dve, lo, raw, hi):
    return dve.tensor_tensor(lo, raw, hi.bitcast(F32), ALU.subtract)


def three_passes(pe, out, w_hi, w_lo, x_hi, x_lo, first, last):
    pe.matmul(out, lhsT=w_hi, rhs=x_hi, start=first, stop=False)
    pe.matmul(out, lhsT=w_hi, rhs=x_lo, start=False, stop=False)
    return pe.matmul(out, lhsT=w_lo, rhs=x_hi, start=False, stop=last)


def project_split(k, tag, KC, H, loads, x_hi, x_lo, source, groups, take, space=None):
    nc, ps = k.nc, k.ps
    KB, NGR = KC // H, len(groups)
    trips, n_dma = sum(n for n, _, _ in loads), loads[0][1]
    names = "loaded0 loaded1 hi_done lo_done used x_hi_done x_lo_done taken0 taken1 stepped"
    loaded0, loaded1, hi_done, lo_done, used, x_hi_done, x_lo_done, taken0, taken1, stepped = k.sems(
        " ".join(f"{tag}_{n}" for n in names.split()))
    loaded, taken = [loaded0, loaded1], [taken0, taken1]
    BODY = 2 * H
    with ExitStack() as st:
        if space is None:
            space = sb(nc, st, f"{tag}_raw", [P, 2 * KB * P])
        raw = [space[:, q * KB * P:(q + 1) * KB * P].rearrange("p (k n) -> p k n", k=KB) for q in range(2)]
        w_hi = [sb(nc, st, f"{tag}_hi{q}", [P, KB, P], F32R) for q in range(2)]
        w_lo = [sb(nc, st, f"{tag}_lo{q}", [P, KB, P], F32R) for q in range(2)]
        tmp = sb(nc, st, f"{tag}_tmp", [P, 2, RS])
        block = st.enter_context(nc.Block())

        @block.sync
        def _(sp):
            start = 0
            for n_trips, _, load in loads:
                with sp.Fori(0, n_trips) as i:
                    for n in range(BODY):
                        sp.wait_ge(lo_done, i * BODY + start * BODY + n + 1)
                        for x in load(sp, i, n // H, n % H, raw[n % 2]):
                            x.then_inc(loaded[n % 2], 16)
                start += n_trips

        @block.tensor
        def _(pe):
            pe.sem_inc(used, 2)
            with pe.Fori(0, trips) as i:
                for n in range(BODY):
                    p, h = n // H, n % H
                    pe.wait_ge(lo_done, i * BODY + n + 3)
                    if h == 0:
                        pe.wait_ge(taken[p], i + 1)
                    for j, (a, b) in enumerate(groups):
                        for c in range(KB):
                            cc = h * KB + c
                            if source is not None and p == 0 and j == 0:
                                pe.wait_ge(x_lo_done, cc + 1)
                            m = three_passes(pe, ps[NGR * p + j][:, 0:b - a], w_hi[n % 2][:, c, :], w_lo[n % 2][:, c, :],
                                             x_hi[:, cc, a:b], x_lo[:, cc, a:b], cc == 0, cc == KC - 1)
                    m.then_inc(used, 1)

        @block.scalar
        def _(act):
            def hi(i, n):
                act.wait_ge(loaded[n % 2], (i * H + n // 2) * (16 * n_dma) + 16 * n_dma)
                act.wait_ge(used, i * BODY + n + 1)
                split_hi(act, w_hi[n % 2][:, :, :], raw[n % 2]).then_inc(hi_done, 1)
            hi(0, 0)
            if source is not None:
                for c in range(KC):
                    split_hi(act, x_hi[:, c, :], source(c)).then_inc(x_hi_done, 1)
            for n in range(1, BODY):
                hi(0, n)
            with act.Fori(0, trips - 1) as i:
                for n in range(BODY):
                    hi(i + 1, n)

        @block.vector
        def _(dve):
            s = Steps(dve, stepped)

            def lo(i, n):
                dve.wait_ge(hi_done, i * BODY + n + 1)
                split_lo(dve, w_lo[n % 2][:, :, :], raw[n % 2], w_hi[n % 2][:, :, :]).then_inc(lo_done, 1)

            def trip(i, last):
                s.enter(i, take.per) if not last else None
                for n in range(BODY):
                    if not (last and n == BODY - 1):
                        lo(i + (n + 1) // BODY, (n + 1) % BODY)
                    if n % H == H - 1:
                        p = n // H
                        dve.wait_ge(used, i * BODY + n + 3)
                        take(dve, s, i, p, [ps[NGR * p + j][:, 0:b - a] for j, (a, b) in enumerate(groups)], tmp[:, p, :]
                             ).then_inc(taken[p], 1)
                s.leave(trips - 1) if not last else None
            dve.sem_inc(lo_done, 2)
            dve.sem_inc(taken[0], 1)
            dve.sem_inc(taken[1], 1)
            lo(0, 0)
            if source is not None:
                for c in range(KC):
                    dve.wait_ge(x_hi_done, c + 1)
                    split_lo(dve, x_lo[:, c, :], source(c), x_hi[:, c, :]).then_inc(x_lo_done, 1)
            with dve.Fori(0, trips - 1) as i:
                trip(i, False)
            trip(trips - 1, True)
            for p in range(2):
                dve.wait_ge(taken[p], trips + 1)


def add_gated_rows(xT, gate, groups):
    def take(dve, s, i, p, banks, tmp):
        at = i * 2 + p
        for bank, (x0, x1) in zip(banks, groups):
            x2 = min(x1, SEQ)
            o = xT[:, ds(at, 1), x0:x2].rearrange("p a n -> p (a n)")
            r = dve.scalar_tensor_tensor(o, bank[:, 0:x2 - x0], gate[:, ds(at, 1), 0:1].rearrange("p a n -> p (a n)"), o,
                                         ALU.mult, ALU.add)
            if x1 > SEQ:
                s.done(r)
                s.then(dve.tensor_tensor(tmp.rearrange("p (b s) -> p b s", s=DEC_SEQ),
                                         bank[:, SEQ - x0:x1 - x0].rearrange("p (b s) -> p b s", s=DEC_SEQ),
                                         bcast(gate[:, ds(at, 1), 1:COND].rearrange("p a n -> p (a n)"), 2, DEC_SEQ), ALU.mult))
                o = xT[:, ds(at, 1), SEQ:x1].rearrange("p a n -> p (a n)")
                r = dve.tensor_tensor(o, o, tmp, ALU.add)
            elif (x0, x1) != groups[-1]:
                s.done(r)
        return r
    take.per = 2 * (len(groups) - 1 + (2 if groups[-1][1] > SEQ else 0))
    return take


def ffn(k, hT, xT, gate):
    nc, ps, d = k.nc, k.ps, k.dram
    (loaded0, loaded1, hi_done, lo_done, used, h_hi_done, h_lo_done, gate_summed, silu_done, mixed, hid_hi_done,
     hid_lo_done, taken, stepped) = k.sems(" ".join("s11_" + n for n in (
         "loaded0 loaded1 hi_done lo_done used h_hi_done h_lo_done gate_summed silu_done mixed hid_hi_done hid_lo_done "
         "taken stepped").split()))
    loaded = [loaded0, loaded1]
    UP, HALVES = KF, 2
    HB = KF // HALVES
    DOWN = KD * HALVES
    BLOCKS = UP + DOWN
    up_views = [d[n][0].rearrange("(k p) n -> p k n", p=P) for n in ("w_gate", "w_up")]
    down_view = d["w_down"][0].rearrange("(k p) n -> p k n", p=P)
    with ExitStack() as st:
        raw = [sb(nc, st, f"ff_raw{p}", [P, 2 * KD, P]) for p in range(2)]
        w_hi = [sb(nc, st, f"ff_hi{p}", [P, 2 * KD, P], F32R) for p in range(2)]
        w_lo = [sb(nc, st, f"ff_lo{p}", [P, 2 * KD, P], F32R) for p in range(2)]
        h_hi = sb(nc, st, "ff_h_hi", [P, KD, GR], F32R)
        h_lo = sb(nc, st, "ff_h_lo", [P, KD, GR], F32R)
        hid_hi = sb(nc, st, "hid_hi", [P, KF, GR], F32R)
        hid_lo = sb(nc, st, "hid_lo", [P, KF, GR], F32R)
        silu = [sb(nc, st, f"silu{p}", [P, GR]) for p in range(2)]
        tmp = sb(nc, st, "ff_tmp", [P, 2, RS])
        block = st.enter_context(nc.Block())

        @block.sync
        def _(sp):
            sp.wait_ge(lo_done, 2)
            for g in range(NG):
                b0 = g * BLOCKS
                with sp.Fori(0, UP // 2) as i:
                    for p in range(2):
                        sp.wait_ge(lo_done, i * 2 + b0 + p + 1)
                        for j in range(2):
                            sp.dma_start(raw[p][:, j * KD:(j + 1) * KD, :], up_views[j][:, :, ds(i * (2 * P) + p * P, P)]
                                         ).then_inc(loaded[p], 16)
                b0 += UP
                with sp.Fori(0, KD // 2) as i:
                    for n in range(2 * HALVES):
                        sp.wait_ge(lo_done, i * (2 * HALVES) + b0 + n + 1)
                        k0, at = n % HALVES * HB, i * (2 * P) + n // HALVES * P
                        for a, b in ((0, HB // 2), (HB // 2, HB)):
                            sp.dma_start(raw[n % 2][:, a:b, :], down_view[:, k0 + a:k0 + b, ds(at, P)]
                                         ).then_inc(loaded[n % 2], 16)

        @block.tensor
        def _(pe):
            pe.sem_inc(used, 2)
            for g in range(NG):
                b0, u0, d0 = g * BLOCKS, g * UP, g * KD
                with pe.Fori(0, UP // 2) as i:
                    for p in range(2):
                        pe.wait_ge(lo_done, i * 2 + b0 + p + 3)
                        pe.wait_ge(mixed, i * 2 + u0 + p + 1)
                        for j in range(2):
                            for c in range(KD):
                                if p == 0 and j == 0:
                                    pe.wait_ge(h_lo_done, g * KD + c + 1)
                                m = three_passes(pe, ps[2 * p + j][:, 0:GR], w_hi[p][:, j * KD + c, :],
                                                 w_lo[p][:, j * KD + c, :], h_hi[:, c, :], h_lo[:, c, :], c == 0, c == KD - 1)
                            m.then_inc(used if j else gate_summed, 1)
                pe.wait_ge(hid_lo_done, (g + 1) * UP + 2)
                b0 += UP
                with pe.Fori(0, KD // 2) as i:
                    for n in range(2 * HALVES):
                        p, h = n // HALVES, n % HALVES
                        pe.wait_ge(lo_done, i * (2 * HALVES) + b0 + n + 3)
                        if h == 0:
                            pe.wait_ge(taken, i * 2 + d0 + p + 1)
                        for c in range(HB):
                            cc = h * HB + c
                            m = three_passes(pe, ps[4 + p][:, 0:GR], w_hi[n % 2][:, c, :], w_lo[n % 2][:, c, :],
                                             hid_hi[:, cc, :], hid_lo[:, cc, :], cc == 0, cc == KF - 1)
                        m.then_inc(used, 1)

        def rows_of(g):
            return slice(g * GR, (g + 1) * GR)

        @block.scalar
        def _(act):
            def hi(i, per, b, n):
                s = b % 2
                act.wait_ge(loaded[s], i * (per // 2 * 32) + b // 2 * 32 + 32)
                act.wait_ge(used, i * per + b + 1)
                split_hi(act, w_hi[s][:, 0:n, :], raw[s][:, 0:n, :]).then_inc(hi_done, 1)

            def split_rows(g):
                for c in range(KD):
                    split_hi(act, h_hi[:, c, :], hT[:, c, rows_of(g)]).then_inc(h_hi_done, 1)

            def up_trip(i, g, last):
                b0, u0 = g * BLOCKS, g * UP
                for p in range(2):
                    hi(i, 2, b0 + p + 1, HB if last and p else 2 * KD)
                    act.wait_ge(gate_summed, i * 2 + u0 + p + 1)
                    act.wait_ge(hid_lo_done, i * 2 + u0 + p + 1)
                    act.activation(silu[p][:, :], ps[2 * p][:, 0:GR], ACT.Silu).then_inc(silu_done, 1)
                    act.wait_ge(mixed, i * 2 + u0 + p + 3)
                    split_hi(act, hid_hi[:, ds(i * 2 + p, 1), :], silu[p][:, :].unsqueeze(1)).then_inc(hid_hi_done, 1)

            def down_trip(i, g, last):
                b0 = g * BLOCKS + UP
                for n in range(2 * HALVES):
                    end = last and n == 2 * HALVES - 1
                    if not (end and g == NG - 1):
                        hi(i, 2 * HALVES, b0 + n + 1, 2 * KD if end else HB)
            hi(0, 2, 0, 2 * KD)
            split_rows(0)
            for g in range(NG):
                if g:
                    act.wait_ge(used, g * BLOCKS + 2)
                with act.Fori(0, UP // 2 - 1) as i:
                    up_trip(i, g, False)
                up_trip(UP // 2 - 1, g, True)
                if g + 1 < NG:
                    act.wait_ge(used, g * BLOCKS + UP + 2)
                    split_rows(g + 1)
                with act.Fori(0, KD // 2 - 1) as i:
                    down_trip(i, g, False)
                down_trip(KD // 2 - 1, g, True)

        @block.vector
        def _(dve):
            s = Steps(dve, stepped)

            def lo(i, per, b, n):
                q = b % 2
                dve.wait_ge(hi_done, i * per + b + 1)
                split_lo(dve, w_lo[q][:, 0:n, :], raw[q][:, 0:n, :], w_hi[q][:, 0:n, :]).then_inc(lo_done, 1)

            def split_rows(g):
                for c in range(KD):
                    dve.wait_ge(h_hi_done, g * KD + c + 1)
                    split_lo(dve, h_lo[:, c, :], hT[:, c, rows_of(g)], h_hi[:, c, :]).then_inc(h_lo_done, 1)

            def up_trip(i, g, last):
                b0, u0 = g * BLOCKS, g * UP
                for p in range(2):
                    lo(i, 2, b0 + p + 1, HB if last and p else 2 * KD)
                    dve.wait_ge(silu_done, i * 2 + u0 + p + 1)
                    dve.wait_ge(used, i * 2 + b0 + p + 3)
                    dve.tensor_tensor(silu[p][:, :], silu[p][:, :], ps[2 * p + 1][:, 0:GR], ALU.mult).then_inc(mixed, 1)
                    dve.wait_ge(hid_hi_done, i * 2 + u0 + p + 1)
                    split_lo(dve, hid_lo[:, ds(i * 2 + p, 1), :], silu[p][:, :].unsqueeze(1), hid_hi[:, ds(i * 2 + p, 1), :]
                             ).then_inc(hid_lo_done, 1)

            def down_trip(i, g, last, take):
                b0 = g * BLOCKS + UP
                for n in range(2 * HALVES):
                    end = last and n == 2 * HALVES - 1
                    if not (end and g == NG - 1):
                        lo(i, 2 * HALVES, b0 + n + 1, 2 * KD if end else HB)
                    if n % HALVES == HALVES - 1:
                        p = n // HALVES
                        dve.wait_ge(used, i * (2 * HALVES) + b0 + n + 3)
                        take(dve, s, i, p, [ps[4 + p][:, 0:GR]], tmp[:, p, :]).then_inc(taken, 1)
            for sem in (lo_done, mixed, hid_lo_done, taken):
                dve.sem_inc(sem, 2)
            lo(0, 2, 0, 2 * KD)
            split_rows(0)
            for g in range(NG):
                take = add_gated_rows(xT, gate, [(g * GR, (g + 1) * GR)])
                with dve.Fori(0, UP // 2 - 1) as i:
                    up_trip(i, g, False)
                up_trip(UP // 2 - 1, g, True)
                if g + 1 < NG:
                    split_rows(g + 1)
                with dve.Fori(0, KD // 2 - 1) as i:
                    s.enter(i, take.per)
                    down_trip(i, g, False, take)
                    s.leave(KD // 2 - 1)
                down_trip(KD // 2 - 1, g, True, take)
            dve.wait_ge(taken, NG * KD + 2)


def hymba_step(nc, dram):
    with ExitStack() as outer:
        k = Ctx(nc, outer, dram)
        ident = sb(nc, outer, "ident_m", [P, P])
        ones = sb(nc, outer, "ones_m", [P, P])
        eps = sb(nc, outer, "eps", [P, 1])
        vec = sb(nc, outer, "vec", [P, N_VEC])
        mods = sb(nc, outer, "mods", [P, 6 * KD, COND])
        state = sb(nc, outer, "state", [P, KR, 4 * DEC_BATCH])
        xT = sb(nc, outer, "xT", [P, KD, ROWS])
        cT = sb(nc, outer, "cT", [P, KD, COND])
        kv_stored, win_copied = k.sems("kv_stored win_copied")
        k.made = []
        dram["gate_scratch"] = nc.dram_tensor("gate_scratch", (N_KV, RS, 3 * GROUP), F32, kind="Internal").ap()
        dram["attn_scratch"] = nc.dram_tensor("attn_scratch", (SG, QR, BT, KV_WIDTH), F32, kind="Internal").ap()
        V = {n: vec[:, a:b] for n, (a, b) in VEC.items()}

        def factor(j):
            return mods[:, j * KD:(j + 1) * KD, :]

        w_in = dram["w_in"][0].rearrange("(k p) n -> p k n", p=P)
        hT = sb(nc, outer, "hT", [P, KD, ROWS])
        mixers = ExitStack()
        streams = sb(nc, mixers, "streams", [P, 2 * KR + KA, ROWS])
        z_in, z_gate, qT = streams[:, 0:KR], streams[:, KR:2 * KR], streams[:, 2 * KR:]
        qR, merged = z_in, streams[:, KR:]
        samp = ExitStack()
        q_plain = sb(nc, samp, "q_plain", [P, DEC_BATCH, P])
        q_rot = sb(nc, samp, "q_rot", [P, DEC_BATCH, P])
        k_new = sb(nc, samp, "k_new", [P, 2, RS])
        v_new = sb(nc, samp, "v_new", [RS, 2, KV_WIDTH])
        gate_rows = sb(nc, samp, "gate_rows", [P, SG, 3])
        page_rows = sb(nc, samp, "page_rows", [P, SG, N_LCH], I32)
        page_parts = sb(nc, samp, "page_parts", [P, DEC_BATCH], I32)
        attn = hT[:, :, :].rearrange("p k r -> p (k r)")[:, 0:(TILES + 1) * ATTN_WIDTH].rearrange(
            "p (t n) -> p t n", t=TILES + 1)
        load_and_condition(k, xT, mods, vec, state, cT, ident, ones, eps, page_rows, page_parts, win_copied,
                           [x[:, :, :].rearrange("p k r -> p (k r)") for x in (hT, streams)])
        norm_rows(k, "n1", [list(range(KD))], lambda c: xT[:, c, :], lambda c: hT[:, c, :],
                  (V["ln1_g"], factor(1), lambda c: factor(0)[:, c, :], ones, eps))
        all_rows = [(g * GR, (g + 1) * GR) for g in range(NG)]
        KB = KD // 2

        def load_z(sp, i, p, h, w):
            at = i * (2 * P) + p * P
            return [sp.dma_start(w[:, q * KB // 2:(q + 1) * KB // 2, :],
                                 w_in[:, h * KB + q * KB // 2:h * KB + (q + 1) * KB // 2, ds(at, P)]) for q in range(2)]

        def load_q(sp, i, p, h, w):
            at = i * (2 * HEAD_DIM) + Q_COL + p * HEAD_DIM
            return [sp.dma_start(w[:, :, q * HEAD_DIM:(q + 1) * HEAD_DIM],
                                 w_in[:, h * KB:(h + 1) * KB, ds(at + q * GROUP * HEAD_DIM, HEAD_DIM)]) for q in range(2)]
        with ExitStack() as inp:
            h_hi = sb(nc, inp, "h_hi", [P, KD, ROWS], F32R)
            h_lo = sb(nc, inp, "h_lo", [P, KD, ROWS], F32R)
            project_split(k, "s2", KD, 2, [(KR, 2, load_z), (KA // 2, 2, load_q)], h_hi, h_lo, lambda c: hT[:, c, :],
                          all_rows, copy_chunk(streams))
        rg_lru(k, z_in, z_gate, vec, state, mods, cT, ident)
        compressed = ExitStack()
        ck_s = sb(nc, compressed, "ck_s", [P, DEC_BATCH * NBS])
        cv_s = sb(nc, compressed, "cv_s", [NBS, DEC_BATCH, KV_WIDTH])
        ck_p = sb(nc, compressed, "ck_p", [P, NBP])
        cv_p = sb(nc, compressed, "cv_p", [NBP, KV_WIDTH])
        with ExitStack() as inp:
            kvn = sb(nc, inp, "kvn", [P, TILES + 1, KV_COLS])
            kT = sb(nc, inp, "kT", [P, 2, ROWS])
            gates = sb(nc, inp, "gates", [P, TILES + 1, 3 * N_HEADS])
            keys_and_values(k, hT, qT, qR, kvn, kT, gates, q_plain, q_rot, k_new, v_new, gate_rows, ident, kv_stored)
            compress(k, ck_s, cv_s, ck_p, cv_p, ident, page_rows, hT[:, :, :].rearrange("p k r -> p (k r)"))
            prompt_attention(k, qT, qR, kvn, kT, gates, ck_p, cv_p, attn, ident,
                             hT[:, :, :].rearrange("p k r -> p (k r)")[:, (TILES + 1) * ATTN_WIDTH:])
        k.recycle()
        sample_attention(k, q_plain, q_rot, k_new, v_new, gate_rows, ck_s, cv_s, page_parts, attn, ident,
                         hT[:, :, :].rearrange("p k r -> p (k r)")[:, (TILES + 1) * ATTN_WIDTH:],
                         qR.rearrange("p k r -> p (k r)"), qT.rearrange("p k r -> p (k r)"))
        compressed.close()
        samp.close()
        with ExitStack() as mo:
            turn_attention(k, attn, merged, ident)
            gains = vec[:, VEC["gn_rnn"][0]:VEC["gn_attn"][1]]
            norm_rows(k, "n2", [list(range(KR)), list(range(KR, KR + KA))],
                      lambda c: merged[:, c, :], lambda c: merged[:, c, :],
                      (gains, None, None, ones, eps))
            w_out = dram["w_out"][0].rearrange("(k p) n -> p k n", p=P)
            m_hi = sb(nc, mo, "merged_hi", [P, KD, ROWS], F32R)
            m_lo = sb(nc, mo, "merged_lo", [P, KD, ROWS], F32R)
            project_split(k, "s9", KD, 1,
                          [(KD // 2, 1, lambda sp, i, p, h, w: [sp.dma_start(w, w_out[:, :, ds(i * (2 * P) + p * P, P)])])],
                          m_hi, m_lo, lambda c: merged[:, c, :], all_rows, add_gated_rows(xT, factor(2), all_rows),
                          hT[:, :, :].rearrange("p k r -> p (k r)"))
        mixers.close()
        norm_rows(k, "n3", [list(range(KD))], lambda c: xT[:, c, :], lambda c: hT[:, c, :],
                  (V["ln2_g"], factor(4), lambda c: factor(3)[:, c, :], ones, eps))
        ffn(k, hT, xT, factor(5))
        norm_rows(k, "n4", [list(range(KD))], lambda c: xT[:, c, :], lambda c: xT[:, c, :],
                  (V["final_g"], None, None, ones, eps))
        store_rows(k, xT, ident, win_copied)


_INS = ['x_prompt', 'x_sample', 'cache_cmp_kv', 'cache_sel_kv', 'state_win_kv', 'state_conv', 'state_lru_h',
        'page_table', 'c_prompt', 'c_sample', 'ln1_g', 'ln2_g', 'w_ada', 'b_ada', 'w_in', 'conv_w', 'conv_b',
        'lru_wa', 'lru_ba', 'lru_wx', 'lru_bx', 'lru_lambda', 'cmp_pe', 'cmp_w1', 'cmp_w2', 'gn_rnn', 'gn_attn',
        'w_out', 'w_gate', 'w_up', 'w_down', 'final_g']
_OUTS = [("y_prompt", (1, SEQ, D_MODEL)), ("y_sample", (DEC_BATCH, DEC_SEQ, D_MODEL)),
         ("new_cmp_prompt", (1, 1, SEQ, 2, N_KV, HEAD_DIM)), ("new_cmp_sample", (1, DEC_BATCH, DEC_SEQ, 2, N_KV, HEAD_DIM)),
         ("new_sel_prompt", (1, 1, SEQ, 2, N_KV, HEAD_DIM)), ("new_sel_sample", (1, DEC_BATCH, DEC_SEQ, 2, N_KV, HEAD_DIM)),
         ("new_win_prompt", (1, 1, WINDOW, 2, N_KV, HEAD_DIM)), ("new_win_sample", (1, DEC_BATCH, WINDOW, 2, N_KV, HEAD_DIM)),
         ("new_conv_prompt", (1, 1, CONV_W - 1, RNN_WIDTH)), ("new_conv_sample", (1, DEC_BATCH, CONV_W - 1, RNN_WIDTH)),
         ("new_lru_h_prompt", (1, 1, RNN_WIDTH)), ("new_lru_h_sample", (1, DEC_BATCH, RNN_WIDTH))]


def kernel(**inputs):
    import concourse.bacc as _bacc
    from concourse.bass_utils import run_bass_kernel_spmd as _run

    nc = _bacc.Bacc("TRN2", target_bir_lowering=False, num_devices=1)
    arrays, dram = {}, {}
    laid = {name: np.ascontiguousarray(inputs[name]) for name in _INS}
    laid.update(constants())
    for name, a in laid.items():
        arrays[f"in_{name}"] = a
        dram[name] = nc.dram_tensor(f"in_{name}", a.shape, mybir.dt.from_np(a.dtype), kind="ExternalInput").ap()
    for name, shape in _OUTS:
        dram[name] = nc.dram_tensor(f"out_{name}", shape, F32, kind="ExternalOutput").ap()
    hymba_step(nc, dram)
    r = _run(nc, [arrays], core_ids=[0])
    return tuple(r.results[0][f"out_{name}"] for name, _ in _OUTS)
```
